# Optimizing a Trainium2 kernel written in Bass

```python
import jax, jax.numpy as jnp
from jax import lax
import numpy as np
import math

D_MODEL = 1024
BATCH = 1
SEQ = 1024
DEPTH = 1

CTX_LEN = 256
GRID_W = 64

GLA_HEADS = 4
GLA_DK = 128
GLA_DV = 256
GLA_KW = GLA_HEADS * GLA_DK
GLA_VW = GLA_HEADS * GLA_DV
GATE_RANK = 16
GATE_NORM = 16.0
CHUNK = 64
ROPE_BASE = 10000.0

POOL_WINDOWS = (2, 4, 8, 16)
POOL_GROUPS = 4
POOL_W = D_MODEL
POOL_GW = POOL_W // POOL_GROUPS

EPS = 1e-6

IN_SPLITS = (GLA_KW, GLA_KW, GLA_VW, GLA_VW, GATE_RANK, GATE_RANK, POOL_W, POOL_W, D_MODEL, D_MODEL)
D_IN = 2 * GLA_KW + 2 * GLA_VW + 2 * GATE_RANK + 2 * POOL_W + 2 * D_MODEL


def rmsnorm(x, g):
    xf = x.astype(jnp.float32)
    y = xf * lax.rsqrt(jnp.mean(xf * xf, axis=-1, keepdims=True) + EPS)
    return (y * g.astype(jnp.float32)).astype(x.dtype)

def rope_2d(t, row, col):
    half = GLA_DK // 2
    nf = half // 2
    freqs = ROPE_BASE ** (-jnp.arange(nf, dtype=jnp.float32) / nf)

    def rot(xp, pos):
        ang = pos[:, None] * freqs
        cos = jnp.cos(ang)[None, :, None, :]
        sin = jnp.sin(ang)[None, :, None, :]
        xa, xb = xp[..., :nf], xp[..., nf:]
        return jnp.concatenate([xa * cos - xb * sin, xa * sin + xb * cos], axis=-1)

    return jnp.concatenate([rot(t[..., :half], row), rot(t[..., half:], col)], axis=-1)

def gla_chunked(q, k, v, log_a, s0, with_output):
    B, L, H, DK = q.shape
    n = L // CHUNK

    def to_chunks(t):
        return t.astype(jnp.float32).reshape(B, n, CHUNK, H, t.shape[-1]).transpose(1, 0, 3, 2, 4)

    tri = jnp.tril(jnp.ones((CHUNK, CHUNK), dtype=bool))

    def step(S, inp):
        qc, kc, vc, ac = inp
        b = jnp.cumsum(ac, axis=2)
        bC = b[:, :, -1:, :]
        S_new = jnp.exp(bC[:, :, 0, :, None]) * S + jnp.einsum(
            'bhjd,bhjv->bhdv', kc * jnp.exp(bC - b), vc)
        if not with_output:
            return S_new, None
        diff = b[:, :, :, None, :] - b[:, :, None, :, :]
        decay = jnp.exp(jnp.where(tri[:, :, None], diff, -jnp.inf))
        scores = jnp.einsum('bhid,bhjd,bhijd->bhij', qc, kc, decay)
        o = jnp.einsum('bhij,bhjv->bhiv', scores, vc) + jnp.einsum(
            'bhid,bhdv->bhiv', qc * jnp.exp(b), S)
        return S_new, o

    S, o = lax.scan(step, s0, (to_chunks(q), to_chunks(k), to_chunks(v), to_chunks(log_a)))
    if not with_output:
        return None, S
    o = o.transpose(1, 0, 3, 2, 4).reshape(B, L, H, v.shape[-1])
    return o, S

def gla_bidir(q, k, v, la_f, la_b, s0_f, s0_b, with_output):
    flip = lambda t: t[:, ::-1]
    o_f, s_f = gla_chunked(q, k, v, la_f, s0_f, with_output)
    o_b, s_b = gla_chunked(flip(q), flip(k), flip(v), flip(la_b), s0_b, with_output)
    o = o_f + flip(o_b) if with_output else None
    return o, s_f, s_b

def gla_log_decay(lowrank, w_up, b):
    B, L, _ = lowrank.shape
    gk = (lowrank @ w_up + b).astype(jnp.float32)
    return (jax.nn.log_sigmoid(gk) / GATE_NORM).reshape(B, L, GLA_HEADS, GLA_DK)

def mixer_inputs(h, w_in, w_up_f, b_f, w_up_b, b_b, row, col):
    B, L, _ = h.shape
    p = h @ w_in
    idx = np.cumsum(IN_SPLITS)[:-1].tolist()
    pq, pk, pv, zA, lr_f, lr_b, uB, zB, gA, gB = jnp.split(p, idx, axis=-1)
    q = pq.reshape(B, L, GLA_HEADS, GLA_DK) * (GLA_DK ** -0.5)
    k = pk.reshape(B, L, GLA_HEADS, GLA_DK)
    if row is not None:
        q = rope_2d(q, row, col)
        k = rope_2d(k, row, col)
    v = pv.reshape(B, L, GLA_HEADS, GLA_DV)
    la_f = gla_log_decay(lr_f, w_up_f, b_f)
    la_b = gla_log_decay(lr_b, w_up_b, b_b)
    return q, k, v, la_f, la_b, zA, uB, zB, gA, gB

def multiscale_pool(u, w_pool, pool_scale):
    B, L, _ = u.shape
    uf = u.astype(jnp.float32)
    cs = jnp.concatenate([jnp.zeros_like(uf[:, :1]), jnp.cumsum(uf, axis=1)], axis=1)
    t = jnp.arange(L)
    parts = []
    for g, w in enumerate(POOL_WINDOWS):
        lo = jnp.clip(t - w // 2, 0, L - 1)
        hi = jnp.clip(t + (w - 1 - w // 2), 0, L - 1)
        sl = slice(g * POOL_GW, (g + 1) * POOL_GW)
        csg = cs[..., sl]
        cnt = (hi - lo + 1).astype(jnp.float32)[:, None]
        parts.append((csg[:, hi + 1] - csg[:, lo]) / cnt - uf[..., sl])
    d = jnp.stack(parts, axis=2)
    y = jnp.einsum('blgc,gcd->blgd', d, w_pool.astype(jnp.float32)).reshape(B, L, POOL_W)
    return (y * pool_scale.astype(jnp.float32)).astype(u.dtype)

def branch_out(o, zA, uB, zB, gA, gB, gla_norm_g, w_pool, pool_scale, w_branch_a, w_branch_b, w_out):
    B, L, _ = zA.shape
    o_n = rmsnorm(o, gla_norm_g).astype(zA.dtype).reshape(B, L, GLA_VW)
    yA = (o_n * jax.nn.silu(zA)) @ w_branch_a
    yB = (multiscale_pool(uB, w_pool, pool_scale) * jax.nn.silu(zB)) @ w_branch_b
    merged = jax.nn.sigmoid(gA) * yA + jax.nn.sigmoid(gB) * yB
    return merged @ w_out

def first_inputs(seed: int = 0) -> dict:
    key = jax.random.key(seed)
    ks = jax.random.split(key, 24)
    f32 = jnp.float32
    nrm = lambda k, s, sc: jax.random.normal(k, s, f32) * sc
    return {
        "x": nrm(ks[0], (BATCH, SEQ, D_MODEL), 1.0),
        "c": nrm(ks[1], (BATCH, D_MODEL), 1.0),
        "ctx": nrm(ks[2], (BATCH, CTX_LEN, D_MODEL), 1.0),
        "c_ctx": nrm(ks[3], (D_MODEL,), 1.0),
        "w_mod": nrm(ks[4], (DEPTH, D_MODEL, 3 * D_MODEL), D_MODEL ** -0.5),
        "b_mod": nrm(ks[5], (DEPTH, 3 * D_MODEL), 0.01),
        "norm_g": 1.0 + nrm(ks[6], (DEPTH, D_MODEL), 0.1),
        "w_in": nrm(ks[7], (DEPTH, D_MODEL, D_IN), D_MODEL ** -0.5),
        "w_gate_up_f": nrm(ks[8], (DEPTH, GATE_RANK, GLA_KW), GATE_RANK ** -0.5),
        "b_gate_f": jax.random.uniform(ks[9], (DEPTH, GLA_KW), f32, 1.0, 5.0),
        "w_gate_up_b": nrm(ks[10], (DEPTH, GATE_RANK, GLA_KW), GATE_RANK ** -0.5),
        "b_gate_b": jax.random.uniform(ks[11], (DEPTH, GLA_KW), f32, 1.0, 5.0),
        "gla_norm_g": 1.0 + nrm(ks[12], (DEPTH, GLA_DV), 0.1),
        "w_pool": nrm(ks[13], (DEPTH, POOL_GROUPS, POOL_GW, POOL_GW), POOL_GW ** -0.5),
        "pool_scale": 1.0 + nrm(ks[14], (DEPTH, POOL_W), 0.1),
        "w_branch_a": nrm(ks[15], (DEPTH, GLA_VW, D_MODEL), GLA_VW ** -0.5),
        "w_branch_b": nrm(ks[16], (DEPTH, POOL_W, D_MODEL), POOL_W ** -0.5),
        "w_out": nrm(ks[17], (DEPTH, D_MODEL, D_MODEL), D_MODEL ** -0.5),
        "final_norm_g": 1.0 + nrm(ks[18], (D_MODEL,), 0.1),
    }

def first_block(x, c, ctx, c_ctx, w_mod, b_mod, norm_g, w_in, w_gate_up_f, b_gate_f,
              w_gate_up_b, b_gate_b, gla_norm_g, w_pool, pool_scale, w_branch_a,
              w_branch_b, w_out, final_norm_g):
    B, L, _ = x.shape
    ROWS = L // GRID_W
    t = jnp.arange(ROWS * GRID_W)
    row = (t // GRID_W).astype(jnp.float32)
    col = (t % GRID_W).astype(jnp.float32)

    for l in range(DEPTH):
        last = l == DEPTH - 1
        shift_x, scale_x, gate_x = jnp.split(jax.nn.silu(c) @ w_mod[l] + b_mod[l], 3, axis=-1)
        shift_x, scale_x, gate_x = shift_x[:, None], scale_x[:, None], gate_x[:, None]
        shift_c, scale_c, gate_c = jnp.split(jax.nn.silu(c_ctx) @ w_mod[l] + b_mod[l], 3, axis=-1)

        hc = rmsnorm(ctx, norm_g[l]) * (1.0 + scale_c) + shift_c
        qc, kc, vc, laf_c, lab_c, zAc, uBc, zBc, gAc, gBc = mixer_inputs(
            hc, w_in[l], w_gate_up_f[l], b_gate_f[l], w_gate_up_b[l], b_gate_b[l], None, None)
        s_zero = jnp.zeros((B, GLA_HEADS, GLA_DK, GLA_DV), jnp.float32)
        oc, s_f, s_b = gla_bidir(qc, kc, vc, laf_c, lab_c, s_zero, s_zero, not last)

        hx = rmsnorm(x, norm_g[l]) * (1.0 + scale_x) + shift_x
        q, k, v, la_f, la_b, zA, uB, zB, gA, gB = mixer_inputs(
            hx, w_in[l], w_gate_up_f[l], b_gate_f[l], w_gate_up_b[l], b_gate_b[l], row, col)
        ox, _, _ = gla_bidir(q, k, v, la_f, la_b, s_f, s_b, True)
        y = branch_out(ox.astype(x.dtype), zA, uB, zB, gA, gB, gla_norm_g[l], w_pool[l],
                       pool_scale[l], w_branch_a[l], w_branch_b[l], w_out[l])
        x_new = x + gate_x * y

        if not last:
            yc = branch_out(oc.astype(ctx.dtype), zAc, uBc, zBc, gAc, gBc, gla_norm_g[l], w_pool[l],
                            pool_scale[l], w_branch_a[l], w_branch_b[l], w_out[l])
            ctx = ctx + gate_c * yc
        x = x_new

    return rmsnorm(x, final_norm_g)


HEAD_DIM = 64
ATT_W = D_MODEL // 2
NA_HEADS = ATT_W // HEAD_DIM
NA_ROWS_MAX = 8
NA_COLS = 16
NA_QCOLS = 16
SG_W = D_MODEL // 4
SG_GROUPS = 4
SG_CHUNK = 128
CV_W = D_MODEL // 4
CV_GROUPS = 4
CV_KERNEL = 31
MIX_W = ATT_W + SG_W + CV_W
N_IN = 3 * ATT_W + 2 * SG_W + 2 * CV_W
D_FF = 256 * ((8 * D_MODEL // 3 + 255) // 256)
FFN_KERNEL = 3
NEG_INF = -1e30


def _rmsnorm(x, g):
    x32 = x.astype(jnp.float32)
    y = x32 * lax.rsqrt(jnp.mean(x32 * x32, axis=-1, keepdims=True) + EPS)
    return y.astype(x.dtype) * g

def _layernorm(x, g, b):
    x32 = x.astype(jnp.float32)
    mu = jnp.mean(x32, axis=-1, keepdims=True)
    var = jnp.mean(jnp.square(x32 - mu), axis=-1, keepdims=True)
    return ((x32 - mu) * lax.rsqrt(var + EPS)).astype(x.dtype) * g + b

def _group_layernorm(x, g, b, groups):
    shp = x.shape
    x32 = x.astype(jnp.float32).reshape(shp[:-1] + (groups, shp[-1] // groups))
    mu = jnp.mean(x32, axis=-1, keepdims=True)
    var = jnp.mean(jnp.square(x32 - mu), axis=-1, keepdims=True)
    y = ((x32 - mu) * lax.rsqrt(var + EPS)).reshape(shp).astype(x.dtype)
    return y * g + b

def _modulate(h, shift, scale):
    return h * (1 + scale) + shift

def _dwconv(x, w, b):
    k = w.shape[0]
    ch = x.shape[-1]
    y = lax.conv_general_dilated(
        x, w[:, None, :].astype(x.dtype), window_strides=(1,),
        padding=[((k - 1) // 2, k // 2)],
        dimension_numbers=("NWC", "WIO", "NWC"), feature_group_count=ch)
    return y + b

def _heads(t):
    bn, ln, _ = t.shape
    return t.reshape(bn, ln, NA_HEADS, HEAD_DIM).transpose(0, 2, 1, 3)

def _axis_span(length, win, qblk):
    span = min(qblk + win, length)
    start = np.clip(np.arange(length) - win // 2, 0, length - win)
    a = np.clip(np.arange(0, length, qblk) - win // 2, 0, length - span)
    qpos = np.arange(length).reshape(-1, qblk)
    kpos = a[:, None] + np.arange(span)[None, :]
    s_q = start[qpos][:, :, None]
    inwin = (kpos[:, None, :] >= s_q) & (kpos[:, None, :] < s_q + win)
    off = kpos[:, None, :] - qpos[:, :, None]
    return kpos, inwin, off

def _na_index(rows):
    win_r = min(NA_ROWS_MAX, rows)
    qr = next(q for q in (8, 4, 2, 1) if rows % q == 0)
    kr, mr, dr = _axis_span(rows, win_r, qr)
    kc, mc, dc = _axis_span(GRID_W, NA_COLS, NA_QCOLS)
    nbr, nbc = kr.shape[0], kc.shape[0]
    nq = qr * NA_QCOLS
    key_idx = (kr[:, None, :, None] * GRID_W + kc[None, :, None, :]).reshape(nbr * nbc, -1)
    mask = (mr[:, None, :, None, :, None] & mc[None, :, None, :, None, :]).reshape(nbr * nbc, nq, -1)
    ridx = np.clip(dr + NA_ROWS_MAX - 1, 0, 2 * NA_ROWS_MAX - 2)
    cidx = np.clip(dc + NA_COLS - 1, 0, 2 * NA_COLS - 2)
    bias_idx = (ridx[:, None, :, None, :, None] * (2 * NA_COLS - 1)
                + cidx[None, :, None, :, None, :]).reshape(nbr * nbc, nq, -1)
    return qr, key_idx.astype(np.int32), mask, bias_idx.astype(np.int32)

def _neighbourhood_attention(q, k, v, k_ctx, v_ctx, rpb, rows):
    bn, nh, sl, dh = q.shape
    qr, key_idx, mask, bias_idx = _na_index(rows)
    nbr, nbc = rows // qr, GRID_W // NA_QCOLS
    span = key_idx.shape[-1]
    qb = q.reshape(bn, nh, nbr, qr, nbc, NA_QCOLS, dh).transpose(2, 4, 0, 1, 3, 5, 6)
    qb = qb.reshape(nbr * nbc, bn, nh, qr * NA_QCOLS, dh)
    rpb_flat = rpb.reshape(nh, -1)
    scale = dh ** -0.5

    def block(args):
        qblk, kidx, m, bidx = args
        kb = jnp.take(k, kidx, axis=2)
        vb = jnp.take(v, kidx, axis=2)
        s_loc = jnp.einsum("bhqd,bhkd->bhqk", qblk, kb).astype(jnp.float32) * scale
        s_loc = s_loc + jnp.take(rpb_flat, bidx, axis=1).astype(jnp.float32)[None]
        s_loc = jnp.where(m[None, None], s_loc, NEG_INF)
        s_ctx = jnp.einsum("bhqd,bhkd->bhqk", qblk, k_ctx).astype(jnp.float32) * scale
        p = jax.nn.softmax(jnp.concatenate([s_loc, s_ctx], axis=-1), axis=-1).astype(v.dtype)
        return (jnp.einsum("bhqk,bhkd->bhqd", p[..., :span], vb)
                + jnp.einsum("bhqk,bhkd->bhqd", p[..., span:], v_ctx))

    out = lax.map(block, (qb, jnp.asarray(key_idx), jnp.asarray(mask), jnp.asarray(bias_idx)))
    out = out.reshape(nbr, nbc, bn, nh, qr, NA_QCOLS, dh).transpose(2, 0, 4, 1, 5, 3, 6)
    return out.reshape(bn, sl, nh * dh)

def _context_attention(q, k, v):
    s = jnp.einsum("bhqd,bhkd->bhqk", q, k).astype(jnp.float32) * (q.shape[-1] ** -0.5)
    p = jax.nn.softmax(s, axis=-1).astype(v.dtype)
    o = jnp.einsum("bhqk,bhkd->bhqd", p, v)
    bn, nh, ln, dh = o.shape
    return o.transpose(0, 2, 1, 3).reshape(bn, ln, nh * dh)

def _spatial_gating(u, v, ln_g, ln_b, w_s, b_s):
    u = jax.nn.gelu(u)
    v = _layernorm(jax.nn.gelu(v), ln_g, ln_b)
    bn, ln, ch = v.shape
    vr = v.reshape(bn, ln // SG_CHUNK, SG_CHUNK, SG_GROUPS, ch // SG_GROUPS)
    mixed = jnp.einsum("gpq,bnqgc->bnpgc", w_s, vr) + b_s.T[None, None, :, :, None]
    return u * mixed.reshape(bn, ln, ch)

def _conformer_conv(a, gate, w, b, ng, nb):
    h = a * jax.nn.sigmoid(gate)
    h = _dwconv(h, w, b)
    h = _group_layernorm(h, ng, nb, CV_GROUPS)
    return jax.nn.silu(h)

def _mix_out(att, z, sg_ng, sg_nb, sg_w, sg_b, cv_w, cv_b, cv_ng, cv_nb, w_out):
    o1 = 3 * ATT_W
    o2 = o1 + 2 * SG_W
    sg = _spatial_gating(z[..., o1:o1 + SG_W], z[..., o1 + SG_W:o2], sg_ng, sg_nb, sg_w, sg_b)
    cv = _conformer_conv(z[..., o2:o2 + CV_W], z[..., o2 + CV_W:o2 + 2 * CV_W],
                         cv_w, cv_b, cv_ng, cv_nb)
    return jnp.concatenate([att, sg, cv], axis=-1) @ w_out

def _conv_ffn(h, w_up, conv_w, conv_b, w_down):
    gate, up = jnp.split(h @ w_up, 2, axis=-1)
    gate = _dwconv(gate, conv_w, conv_b)
    return (jax.nn.silu(gate) * up) @ w_down

def second_inputs(seed: int = 0) -> dict:
    key = jax.random.key(seed)
    ks = jax.random.split(key, 24)
    D = D_MODEL

    def n(k, shape, s):
        return jax.random.normal(k, shape, jnp.float32) * s

    return {
        "x": n(ks[0], (BATCH, SEQ, D), 1.0),
        "c": n(ks[1], (BATCH, D), 1.0),
        "ctx": n(ks[2], (BATCH, CTX_LEN, D), 1.0),
        "c_ctx": n(ks[3], (D,), 1.0),
        "ada_w": n(ks[4], (DEPTH, D, 6 * D), 0.5 * D ** -0.5),
        "ada_b": n(ks[5], (DEPTH, 6 * D), 0.02),
        "norm1_g": 1.0 + n(ks[6], (DEPTH, D), 0.05),
        "w_in": n(ks[7], (DEPTH, D, N_IN), D ** -0.5),
        "na_rpb": n(ks[8], (DEPTH, NA_HEADS, 2 * NA_ROWS_MAX - 1, 2 * NA_COLS - 1), 0.5),
        "sg_norm_g": 1.0 + n(ks[9], (DEPTH, SG_W), 0.05),
        "sg_norm_b": n(ks[10], (DEPTH, SG_W), 0.02),
        "sg_w": n(ks[11], (DEPTH, SG_GROUPS, SG_CHUNK, SG_CHUNK), SG_CHUNK ** -0.5),
        "sg_b": 1.0 + n(ks[12], (DEPTH, SG_GROUPS, SG_CHUNK), 0.1),
        "cv_w": n(ks[13], (DEPTH, CV_KERNEL, CV_W), CV_KERNEL ** -0.5),
        "cv_b": n(ks[14], (DEPTH, CV_W), 0.02),
        "cv_norm_g": 1.0 + n(ks[15], (DEPTH, CV_W), 0.05),
        "cv_norm_b": n(ks[16], (DEPTH, CV_W), 0.02),
        "w_out": n(ks[17], (DEPTH, MIX_W, D), MIX_W ** -0.5),
        "norm2_g": 1.0 + n(ks[18], (DEPTH, D), 0.05),
        "ffn_w_up": n(ks[19], (DEPTH, D, 2 * D_FF), D ** -0.5),
        "ffn_conv_w": n(ks[20], (DEPTH, FFN_KERNEL, D_FF), FFN_KERNEL ** -0.5),
        "ffn_conv_b": n(ks[21], (DEPTH, D_FF), 0.02),
        "ffn_w_down": n(ks[22], (DEPTH, D_FF, D), D_FF ** -0.5),
        "final_norm_g": 1.0 + n(ks[23], (D,), 0.05),
    }

def second_block(x, c, ctx, c_ctx, ada_w, ada_b, norm1_g, w_in, na_rpb, sg_norm_g, sg_norm_b,
              sg_w, sg_b, cv_w, cv_b, cv_norm_g, cv_norm_b, w_out, norm2_g, ffn_w_up,
              ffn_conv_w, ffn_conv_b, ffn_w_down, final_norm_g):
    rows = x.shape[1] // GRID_W
    xc = ctx
    for l in range(DEPTH):
        last = l == DEPTH - 1
        mod_l = jnp.split((jax.nn.silu(c) @ ada_w[l] + ada_b[l])[:, None, :], 6, axis=-1)
        mod_c = jnp.split((jax.nn.silu(c_ctx) @ ada_w[l] + ada_b[l])[None, None, :], 6, axis=-1)

        h = _modulate(_rmsnorm(x, norm1_g[l]), mod_l[0], mod_l[1])
        hc = _modulate(_rmsnorm(xc, norm1_g[l]), mod_c[0], mod_c[1])
        z = h @ w_in[l]
        q = _heads(z[..., :ATT_W])
        k = _heads(z[..., ATT_W:2 * ATT_W])
        v = _heads(z[..., 2 * ATT_W:3 * ATT_W])
        if last:
            kvc = hc @ w_in[l][:, ATT_W:3 * ATT_W]
            kc = _heads(kvc[..., :ATT_W])
            vc = _heads(kvc[..., ATT_W:])
        else:
            zc = hc @ w_in[l]
            kc = _heads(zc[..., ATT_W:2 * ATT_W])
            vc = _heads(zc[..., 2 * ATT_W:3 * ATT_W])
        att = _neighbourhood_attention(q, k, v, kc, vc, na_rpb[l], rows)
        y = _mix_out(att, z, sg_norm_g[l], sg_norm_b[l], sg_w[l], sg_b[l], cv_w[l], cv_b[l],
                     cv_norm_g[l], cv_norm_b[l], w_out[l])
        x = x + mod_l[2] * y
        if not last:
            att_c = _context_attention(_heads(zc[..., :ATT_W]), kc, vc)
            yc = _mix_out(att_c, zc, sg_norm_g[l], sg_norm_b[l], sg_w[l], sg_b[l], cv_w[l],
                          cv_b[l], cv_norm_g[l], cv_norm_b[l], w_out[l])
            xc = xc + mod_c[2] * yc

        h2 = _modulate(_rmsnorm(x, norm2_g[l]), mod_l[3], mod_l[4])
        x = x + mod_l[5] * _conv_ffn(h2, ffn_w_up[l], ffn_conv_w[l], ffn_conv_b[l], ffn_w_down[l])
        if not last:
            h2c = _modulate(_rmsnorm(xc, norm2_g[l]), mod_c[3], mod_c[4])
            xc = xc + mod_c[5] * _conv_ffn(h2c, ffn_w_up[l], ffn_conv_w[l], ffn_conv_b[l],
                                           ffn_w_down[l])
    return _rmsnorm(x, final_norm_g)


def setup_inputs(seed=0):
    out = dict(first_inputs(seed))
    for name, value in second_inputs(seed + 1).items():
        if name != "x":
            out[name + "_2"] = value
    return out


def reference(
    x, c, ctx, c_ctx, w_mod, b_mod, norm_g, w_in, w_gate_up_f, b_gate_f, w_gate_up_b, b_gate_b,
    gla_norm_g, w_pool, pool_scale, w_branch_a, w_branch_b, w_out, final_norm_g, c_2, ctx_2,
    c_ctx_2, ada_w_2, ada_b_2, norm1_g_2, w_in_2, na_rpb_2, sg_norm_g_2, sg_norm_b_2, sg_w_2,
    sg_b_2, cv_w_2, cv_b_2, cv_norm_g_2, cv_norm_b_2, w_out_2, norm2_g_2, ffn_w_up_2,
    ffn_conv_w_2, ffn_conv_b_2, ffn_w_down_2, final_norm_g_2,
):
    x = first_block(
        x, c, ctx, c_ctx, w_mod, b_mod, norm_g, w_in, w_gate_up_f, b_gate_f, w_gate_up_b,
        b_gate_b, gla_norm_g, w_pool, pool_scale, w_branch_a, w_branch_b, w_out, final_norm_g,
    )
    return second_block(
        x, c_2, ctx_2, c_ctx_2, ada_w_2, ada_b_2, norm1_g_2, w_in_2, na_rpb_2, sg_norm_g_2,
        sg_norm_b_2, sg_w_2, sg_b_2, cv_w_2, cv_b_2, cv_norm_g_2, cv_norm_b_2, w_out_2,
        norm2_g_2, ffn_w_up_2, ffn_conv_w_2, ffn_conv_b_2, ffn_w_down_2, final_norm_g_2,
    )


_drawn_inputs = setup_inputs


def setup_inputs(seed=0):
    import zlib

    import numpy as np

    out = dict(_drawn_inputs(seed))
    spreads = {}
    factors = {'b_mod': 4.782,
     'ctx_2': 3.207,
     'norm1_g_2': 5.269,
     'na_rpb_2': 7.679,
     'sg_norm_g_2': 8.0,
     'sg_norm_b_2': 23.446,
     'sg_b_2': 4.878,
     'cv_b_2': 64.0,
     'cv_norm_g_2': 57.01,
     'cv_norm_b_2': 177.796,
     'norm2_g_2': 3.541,
     'ffn_conv_b_2': 23.086}
    for name, (base, spread) in spreads.items():
        noise = np.random.default_rng([zlib.crc32(name.encode()), seed]).standard_normal(out[name].shape)
        drawn = base * np.exp(spread * noise) if base else spread * noise
        out[name] = __import__('jax').numpy.asarray(drawn.astype(out[name].dtype))
    for name, factor in factors.items():
        out[name] = (out[name] * factor).astype(out[name].dtype)
    return out
```

```python
from contextlib import ExitStack

import concourse.bass as bass
from concourse import mybir

F32 = mybir.dt.float32
F32R = mybir.dt.float32r
I32 = mybir.dt.int32
ACT = mybir.ActivationFunctionType
ALU = mybir.AluOpType

P = 128
D = 1024
KT = D // P
T = 1024
C = 256
TA = T + C
H = 512
EPS = 1e-6
HEADS, DK, DV = 4, 128, 256
CH = 128
NC = TA // CH
NCX = T // CH
LEVELS = 7
GATE_NORM = 16.0
WINDOWS = (2, 4, 8, 16)
PAD = 8
FF = 2816
FT = FF // P
GROUPS = FT // 2
TAPS = 31
GRID_W, ROWS = 64, 16
AH = 8
KSPAN = (0, 8, 24, 32)

T_K, T_V, T_LR, T_Q = 0, 4, 12, 13
T_ZA, T_UB, T_ZB, T_GA, T_GB = 17, 25, 33, 41, 49
T_POOL, T_B, T_A, T_OUT = 57, 59, 67, 75
T_CV, T_SG, T_K2, T_V2, T_Q2, T_W2 = 83, 87, 91, 95, 99, 103
T_FF = 111
NT = T_FF + 6 * GROUPS


def _first_units():
    count, first = 0, []
    for t in range(NT):
        first.append(count)
        if t < T_Q or T_K2 <= t < T_Q2:
            count += 3
        elif T_POOL <= t < T_B:
            count += 8
        elif t >= T_FF + 4 and (t - T_FF - 4) % 6 >= 4 or t >= NT - 2:
            count += 8
        else:
            count += 2
    return first + [count]


UNIT = _first_units()

_COLS = [("norm_g", 8), ("b_mod", 24), ("gla_g", 2), ("pool_scale", 8), ("final_g", 8),
         ("ada_b", 48), ("norm1_g", 8), ("norm2_g", 8), ("sg_g", 2), ("sg_b", 2), ("cv_w", 2 * TAPS),
         ("cv_b", 2), ("cv_g", 2), ("cv_nb", 2), ("ff_w", 3 * FT), ("ff_b", FT), ("final_g2", 8)]
COL = {}
_at = 0
for _name, _n in _COLS:
    COL[_name] = _at
    _at += _n
NCOL = _at


def build(nc, modw, crow, cols, mats, tabs, tabq, lev, hmask, inv, sgb, xT, ctxT, ctx2T, wall, wup, sgw, bias,
          out):
    ctx = ExitStack()
    with ctx:
        def sem(name):
            return ctx.enter_context(nc.semaphore(name))

        def dram(name, shape, dt=F32):
            return nc.dram_tensor(name, shape, dt, kind="Internal").ap()

        place = {"next": (nc.sbuf_base + 63) // 64 * 64}

        def at(name, shape, offset, dt=F32):
            n = 4
            for s in shape[1:]:
                n *= s
            n = (n + 31) // 32 * 32
            assert offset % 32 == 0 and offset + n <= nc.sbuf_usable_end, (name, offset + n)
            return nc.alloc_sbuf_tensor_at(name, shape, dt, offset=offset), offset + n

        def keep(name, shape, dt=F32):
            t, place["next"] = at(name, shape, place["next"], dt)
            return t

        w_raw = keep("w_raw", [P, 2, 1024])
        w_hi = keep("w_hi", [P, 2, 1024], F32R)
        w_lo = keep("w_lo", [P, 2, 1024], F32R)
        col = keep("col", [P, NCOL])
        modx = keep("modx", [P, 72])
        modc = keep("modc", [P, 72])
        gain = keep("gain", [P, 2, KT])
        mat = keep("mat", [P, 7, P])
        mod_sum = keep("mod_sum", [P, 2, 4])
        one = keep("one", [P, 1])
        tick = keep("tick", [P, 1])
        epsc = keep("epsc", [P, 1])
        dec = keep("dec", [P, NC, 8])
        ident, mean_d, mean_v, mean_g = (mat[:, n, :] for n in range(4))
        arena = place["next"]

        pb = [ctx.enter_context(nc.psum_tensor(f"pb{i}", [P, H], F32)) for i in range(2)]
        g = ctx.enter_context(nc.psum_tensor("g", [P, 6, H], F32))

        proj_d = dram("proj_d", [T_POOL, P, TA])

        w_in = [sem("w_in0"), sem("w_in1")]
        one_ready = sem("one_ready")
        w_high = sem("w_high")
        w_split = sem("w_split")
        w_begun = sem("w_begun")
        unit_done = sem("unit_done")
        bank_free = [sem("bank_free0"), sem("bank_free1")]
        sq_ready = sem("sq_ready")
        sq_used = sem("sq_used")
        std_ready = sem("std_ready")
        rstd_ready = sem("rstd_ready")
        t_ready = sem("t_ready")
        h_ready = sem("h_ready")
        xh_ready = sem("xh_ready")
        xl_ready = sem("xl_ready")
        const_in = sem("const_in")
        cond_in = sem("cond_in")
        cond_ready = sem("cond_ready")
        x_in = sem("x_in")
        mod_in = [sem(f"mod_in{i}") for i in range(4)]
        mod_ctx = sem("mod_ctx")
        mod_free = sem("mod_free")
        mod_kept = sem("mod_kept")
        gain_ready = sem("gain_ready")
        store_done = [sem("store_done0"), sem("store_done1")]
        phase = sem("phase")

        xh, a = at("xh", [P, KT, TA], arena, F32R)
        xl, a = at("xl", [P, KT, TA], a, F32R)
        after_operand = a
        xin, a = at("xin", [P, KT, TA], after_operand)
        rstd, a = at("rstd", [P, TA], a)
        squares, a = at("squares", [P, 2, TA], a)
        crow_sb, a = at("crow_sb", [P, 4, 1024], a)
        mod_raw, a = at("mod_raw", [P, 4, 1024], a)
        prod, a = at("prod", [P, 1024], a)
        stage, _ = at("stage", [P, 2, TA], after_operand)

        kr_d = dram("kr_d", [NC, P, H])
        la_d = dram("la_d", [NC, 2, P, 1024])
        kt_d = dram("kt_d", [NC, P, 1024])
        vt_d = dram("vt_d", [NC, P, 1024])
        sb_d = dram("sb_d", [NC, P, 1024])
        tab, a = at("tab", [P, 2, TA], arena)
        levr, a = at("levr", [P, 2, 1024], a, F32R)
        matr, a = at("matr", [P, 3, P], a, F32R)
        mask, a = at("mask", [P, LEVELS, P], a)
        wup_sb, a = at("wup_sb", [64, H], a)
        stf, a = at("stf", [P, 2, HEADS, DV], a)
        gla_arena = a
        levf, _ = at("levf", [P, 2, 1024], gla_arena)
        kc, a = at("kc", [P, 2, HEADS, CH], gla_arena)
        ks, a = at("ks", [P, 2, HEADS, CH], a)
        vc, a = at("vc", [P, 2, 8, CH], a)
        lrc, a = at("lrc", [64, 2, CH], a)
        kr, a = at("kr", [P, 2, HEADS, CH], a)
        rot, a = at("rot", [P, HEADS, CH], a)
        soft, a = at("soft", [P, 2, H], a)
        la, a = at("la", [P, 2, H], a)
        lah, a = at("lah", [P, 2, 2, H], a, F32R)
        lal, a = at("lal", [P, 2, 2, H], a, F32R)
        ef, a = at("ef", [P, 2, H], a)
        kt, a = at("kt", [P, 2, 2, H], a)
        vt, a = at("vt", [P, 2, 1024], a)
        skb, a = at("skb", [P, 2, H], gla_arena)
        svt, a = at("svt", [P, 2, 1024], a)
        stb, a = at("stb", [P, 2, HEADS, DV], a)
        oall, a = at("oall", [P, 8, T], gla_arena)
        fk, a = at("fk", [P, 2, HEADS, CH], a)
        fq, a = at("fq", [P, 2, HEADS, CH], a)
        fs, a = at("fs", [P, 2, HEADS, CH], a)
        fla, a = at("fla", [P, 2, 2, 2, H], a, F32R)
        fkt, a = at("fkt", [P, 2, H], a)
        fvt, a = at("fvt", [P, 2, 1024], a)
        fsb, a = at("fsb", [P, 2, HEADS, DV], a)
        ex, a = at("ex", [P, 2, HEADS, H], a)
        lk, a = at("lk", [P, LEVELS, HEADS, CH], a)
        lq, a = at("lq", [P, LEVELS, HEADS, CH], a)
        qi, a = at("qi", [P, 2, HEADS, CH], a)
        pt, a = at("pt", [P, HEADS, CH], a)
        frot, a = at("frot", [P, HEADS, CH], a)
        tab_in = sem("tab_in")
        tab_ready = sem("tab_ready")
        p_in = [sem("p_in0"), sem("p_in1")]
        p_out = [sem("p_out0"), sem("p_out1")]
        p_dve = sem("p_dve")
        p_kr = sem("p_kr")
        p_gk = sem("p_gk")
        p_act = sem("p_act")
        p_ln = sem("p_ln")
        p_la = sem("p_la")
        p_lah = sem("p_lah")
        p_lal = sem("p_lal")
        p_vtr = sem("p_vtr")
        p_vt = sem("p_vt")
        p_ktr = sem("p_ktr")
        p_arg = sem("p_arg")
        p_exp = sem("p_exp")
        p_kt = sem("p_kt")
        s_in = [sem("s_in0"), sem("s_in1")]
        s_out = [sem("s_out0"), sem("s_out1")]
        s_mm = sem("s_mm")
        s_upd = sem("s_upd")
        f_in = [sem("f_in0"), sem("f_in1")]
        f_rot = sem("f_rot")
        f_qr = sem("f_qr")
        f_arg = sem("f_arg")
        f_exp = sem("f_exp")
        f_mul = sem("f_mul")
        f_lev = sem("f_lev")
        f_diag = sem("f_diag")
        f_pred = sem("f_pred")
        f_omm = sem("f_omm")
        f_oev = sem("f_oev")
        f_smm = sem("f_smm")
        f_upd = sem("f_upd")

        ah, a = at("ah", [P, 8, T], arena, F32R)
        up, a = at("up", [P, 2, T + 2 * PAD], arena)
        sums, a = at("sums", [P, 2, T + 2 * PAD], a)
        inv_sb, a = at("inv_sb", [P, T], a)
        zb, a = at("zb", [P, 2, T], a)
        yb, a = at("yb", [P, 2, H], a)
        assert a <= gla_arena
        _, a = at("oall_end", [P, 8, T], gla_arena)
        al, _ = at("al", [P, 8, T], gla_arena, F32R)
        bh, a = at("bh", [P, 8, T], a, F32R)
        bl, a = at("bl", [P, 8, T], a, F32R)
        mix, _ = at("mix", [P, 8, T], a)
        dh, a = at("dh", [P, 2, 2, T], a, F32R)
        dl, a = at("dl", [P, 2, 2, T], a, F32R)
        osq_at = a
        osq, a = at("osq", [P, 2, T], a)
        orstd, a = at("orstd", [P, T], a)
        za, _ = at("za", [P, T], a)
        ga, _ = at("ga", [P, 2, T], osq_at)
        sq1, _ = at("sq1", [P, 2, T], osq_at)
        xp_d = dram("xp_d", [KT, P, T])
        q_in = [sem("q_in0"), sem("q_in1")]
        q_inv = sem("q_inv")
        q_z = [sem("q_z0"), sem("q_z1")]
        q_pad = sem("q_pad")
        q_s = sem("q_s")
        q_d = sem("q_d")
        q_dh = sem("q_dh")
        q_dl = sem("q_dl")
        q_sil = sem("q_sil")
        q_y = sem("q_y")
        q_yh = sem("q_yh")
        q_yl = sem("q_yl")
        b_in = sem("b_in")
        b_sg = sem("b_sg")
        o_in = sem("o_in")
        o_sq = sem("o_sq")
        o_st = sem("o_st")
        o_std = sem("o_std")
        o_rec = sem("o_rec")
        o_t = sem("o_t")
        o_sil = sem("o_sil")
        o_n = sem("o_n")
        o_h = sem("o_h")
        o_l = sem("o_l")
        a_in = [sem("a_in0"), sem("a_in1")]
        a_sg = sem("a_sg")
        a_m = sem("a_m")
        a_mh = sem("a_mh")
        a_ml = sem("a_ml")
        r_in = sem("r_in")
        n1_x = sem("n1_x")
        xp_out = sem("xp_out")
        ctx2_in = sem("ctx2_in")

        KB = 1024
        mh, a = at("mh", [P, 8, T], arena, F32R)
        ml, a = at("ml", [P, 8, T], a, F32R)
        vsq, a = at("vsq", [P, 2, T], a)
        vtok, _ = at("vtok", [P, NCX, 256], arena + 64 * KB)
        vroot, a = at("vroot", [P, T], a)
        sgw_sb, a = at("sgw_sb", [P, 4, P], a)
        sgb_sb, a = at("sgb_sb", [P, 2, P], a)
        assert a <= after_operand
        zcs, a = at("zcs", [P, 8, T], after_operand)
        hpad, a = at("hpad", [P, 2, T + TAPS - 1], a)
        zkv, a = at("zkv", [P, 8, TA], a)
        zq, a = at("zq", [P, 4, T], a)
        kq_end = a
        at_bias, a = at("at_bias", [P, 4, H], arena + 64 * KB)
        sl, a = at("sl", [P, 2, H], a)
        pr, a = at("pr", [P, 2, H + C], a)
        ptr, a = at("ptr", [P, 2, H + C], a)
        ks2, a = at("ks2", [P, TA], a)
        vs2, a = at("vs2", [P, 4 * H + C], a)
        qs2, a = at("qs2", [P, T], a)
        vtk, a = at("vtk", [P, 2, H], a)
        vcx, a = at("vcx", [P, C], a)
        osb, a = at("osb", [P, 2, P], a)
        tiny, a = at("tiny", [P, 2, 8], a)
        assert a <= after_operand + 40 * KB
        x2, a = at("x2", [P, KT, T], arena + 64 * KB)
        sq2, a = at("sq2", [P, 2, T], a)
        root2, a = at("root2", [P, T], a)
        xw, a = at("xw", [P, KT, T], a)
        hh, a = at("hh", [P, 2, 2, T], a, F32R)
        hl, a = at("hl", [P, 2, 2, T], a, F32R)
        gp, a = at("gp", [P, 2, T + 2], arena + 96 * KB)
        cb, a = at("cb", [P, 2, T], a)
        sgm, a = at("sgm", [P, 2, T], a)
        z_h = sem("z_h")
        z_cv = sem("z_cv")
        z_pe = sem("z_pe")
        z_act = sem("z_act")
        z_dve = sem("z_dve")
        y_pe = sem("y_pe")
        y_act = sem("y_act")
        y_dve = sem("y_dve")
        sg_in = sem("sg_in")
        bias_in = [sem(f"bias_in{i}") for i in range(4)]
        at_stq = sem("at_stq")
        at_stv = sem("at_stv")
        at_vt = sem("at_vt")
        at_vtk = sem("at_vtk")
        at_s = sem("at_s")
        at_sc = sem("at_sc")
        at_m = sem("at_m")
        at_nm = sem("at_nm")
        at_ex = sem("at_ex")
        at_sum = sem("at_sum")
        at_r = sem("at_r")
        at_tr = sem("at_tr")
        at_ptc = sem("at_ptc")
        at_pv = sem("at_pv")
        at_o = sem("at_o")
        at_ot = sem("at_ot")
        at_hi = sem("at_hi")
        at_lo = sem("at_lo")
        x2_in = sem("x2_in")
        f_pad = sem("f_pad")
        f_cv = sem("f_cv")
        f_sil = sem("f_sil")
        f_hid = sem("f_hid")
        f_hh = sem("f_hh")
        f_hl = sem("f_hl")
        f_fin = sem("f_fin")
        out_done = sem("out_done")

        block = ctx.enter_context(nc.Block())

        def end_phase(eng, n):
            eng.drain().then_inc(phase, 1)
            eng.wait_ge(phase, 3 * n)

        def step(base, i, by):
            return base if i is None else i * by + base


        def pe_unit(pe, b, xhi, xlo, tokens, kts, wcols, bank, ready=None):
            n = tokens.stop - tokens.start
            total, count = 3 * len(kts), 0
            first = None
            for k, wc in zip(kts, wcols):
                if ready is not None:
                    pe.wait_ge(xh_ready, ready + k)
                    pe.wait_ge(xl_ready, ready + k)
                for w, x in ((w_hi, xhi), (w_lo, xhi), (w_hi, xlo)):
                    mm = pe.matmul(pb[bank][:, 0:n], w[:, b, wc:wc + P], x[:, k, tokens],
                                   start=(count == 0), stop=(count == total - 1))
                    first = first or mm
                    count += 1
            return first, mm

        def pe_tile(pe, t0, i=None, tiles=0, units=0, xhi=None, xlo=None, ready=None):
            b, u0 = t0 % 2, UNIT[t0]
            xhi, xlo = xhi or xh, xlo or xl
            pe.wait_ge(w_split, step(t0 + 1, i, tiles))
            for n in range(UNIT[t0 + 1] - u0):
                bank = (u0 + n) % 2
                pe.wait_ge(bank_free[bank], step((u0 + n) // 2 + 1, i, units // 2))
                tokens = slice(n * H, min(n * H + H, TA))
                first, last = pe_unit(pe, b, xhi, xlo, tokens, range(KT), range(0, 1024, P), bank,
                                      ready if n == 0 else None)
                if n == 0:
                    first.then_inc(w_begun, 1)
                last.then_inc(unit_done, 1)

        def act_squares(act, n, tokens, src, sq, wait=None):
            with act.Fori(0, KT // 2) as i:
                for b in range(2):
                    if wait is not None:
                        wait(i, b)
                    act.wait_ge(sq_used, i * 2 + (KT * n + b + 1))
                    act.activation(sq[:, b, 0:tokens], src[:, i * 2 + b, 0:tokens],
                                   ACT.Square).then_inc(sq_ready, 1)

        def pe_squares(pe, n, tokens, sq):
            for k in range(KT):
                pe.wait_ge(sq_ready, KT * n + k + 1)
                for u in range(0, tokens, H):
                    w = min(H, tokens - u)
                    mm = pe.matmul(g[:, u // H, 0:w], mean_d, sq[:, k % 2, u:u + w],
                                   start=(k == 0), stop=(k == KT - 1))
                mm.then_inc(sq_used, 1)

        def act_roots(act, n, tokens, root):
            act.wait_ge(sq_used, 2 + KT * (n + 1))
            for u in range(0, tokens, H):
                w = min(H, tokens - u)
                r = act.activation(root[:, u:u + w], g[:, u // H, 0:w], ACT.Sqrt, bias=epsc[:, 0:1])
            r.then_inc(std_ready, 1)

        UP = [T_FF if n == 0 else T_FF + 4 + 6 * (n - 1) for n in range(GROUPS)]
        DOWN = [T_FF + 8 + 6 * n if n < GROUPS - 1 else NT - 2 for n in range(GROUPS)]
        DOWN_END = [UNIT[t + 2] for t in DOWN]
        DOWN_LAST = UNIT[DOWN[-1]]
        F_UNITS = UNIT[UP[3]] - UNIT[UP[2]]
        gp_root = sq2[:, 0, :]
        out_tiles = out.rearrange("p t n -> t p n")

        def at_tokens(br, bc):
            return lambda x: x.rearrange("p (r c) -> p r c", c=GRID_W)[:, 8 * br:8 * br + 8,
                                                                      16 * bc:16 * bc + 16]

        def step_of(k):
            return k // 4, k // 2 % 2, k % 2

        @block.sync
        def _(sp):
            sp.dma_start(crow_sb[:, :, :], crow).then_inc(cond_in, 16)
            for j in range(4):
                sp.dma_start(mod_raw[:, j, :], modw[j]).then_inc(mod_in[j], 16)
            sp.dma_start(xin[:, :, 0:T], xT).then_inc(x_in, 16)
            sp.dma_start(xin[:, :, T:TA], ctxT).then_inc(x_in, 16)
            sp.dma_start(mat[:, :, :], mats).then_inc(const_in, 16)
            sp.dma_start(col[:, :], cols).then_inc(const_in, 16)
            for b in range(2):
                sp.dma_start(w_raw[:, b, :], wall[b]).then_inc(w_in[b], 16)
            modw4 = modw.rearrange("(i j) p n -> i j p n", j=4)
            modw2 = modw.rearrange("(i j) p n -> i j p n", j=2)
            wall2 = wall[0:NT - 1].rearrange("(i j) p n -> i j p n", j=2)
            with sp.Fori(1, 4) as i:
                for j in range(4):
                    sp.wait_ge(mod_free, i * 4 + (j - 2))
                    sp.dma_start(mod_raw[:, j, :], modw4[i, j]).then_inc(mod_in[j], 16)
            with sp.Fori(1, T_POOL // 2 + 1) as i:
                for b in range(2):
                    sp.wait_ge(w_split, i * 2 + (b - 1))
                    sp.dma_start(w_raw[:, b, :], wall2[i, b]).then_inc(w_in[b], 16)
                for b in range(2):
                    sp.wait_ge(mod_free, i * 2 + (14 + b))
                    sp.dma_start(mod_raw[:, b, :], modw2[i + 7, b]).then_inc(mod_in[b], 16)
            with sp.Fori((T_POOL + 1) // 2, T_W2 // 2 + 1) as i:
                for b in range(2):
                    sp.wait_ge(w_split, i * 2 + (b - 1))
                    sp.dma_start(w_raw[:, b, :], wall2[i, b]).then_inc(w_in[b], 16)
            sp.wait_ge(phase, 18)
            bias6 = bias.rearrange("r c (i j) q k -> r c i j q k", j=2)
            with sp.Fori(0, AH // 2) as i:
                for k in range(16):
                    bc, br, j = step_of(k)
                    sp.wait_ge(at_sc, i * 16 + (k + 1))
                    sp.dma_start(at_bias[:, k % 4, :], bias6[br, bc, i, j]).then_inc(bias_in[k % 4], 16)
            with sp.Fori(T_W2 // 2 + 1, NT // 2) as i:
                for b in range(2):
                    sp.wait_ge(w_split, i * 2 + (b - 1))
                    sp.dma_start(w_raw[:, b, :], wall2[i, b]).then_inc(w_in[b], 16)
            sp.wait_ge(w_split, NT - 2)
            sp.dma_start(w_raw[:, 0, :], wall[NT - 1]).then_inc(w_in[0], 16)

        @block.gpsimd
        def _(pool):
            def split(b, high, raw):
                pool.wait_ge(w_in[b], raw)
                nc.gpsimd.tensor_tensor(w_hi[:, b, :], w_raw[:, b, :], one[:, 0:1].to_broadcast([P, 1024]),
                                        ALU.mult).then_inc(w_high, 1)
                pool.wait_ge(w_high, high)
                nc.gpsimd.tensor_tensor(w_lo[:, b, :], w_raw[:, b, :], w_hi[:, b, :],
                                        ALU.subtract).then_inc(w_split, 1)

            nc.gpsimd.memset(one[:, :], 1.0).then_inc(one_ready, 1)
            pool.wait_ge(one_ready, 1)
            for b in range(2):
                split(b, b + 1, 16)
            with pool.Fori(1, NT // 2) as i:
                for b in range(2):
                    pool.wait_ge(w_begun, i * 2 + b)
                    split(b, i * 2 + (b + 1), i * 16 + 16)
            pool.wait_ge(w_begun, NT - 1)
            split(0, NT, 16 * (NT // 2 + 1))

        @block.scalar
        def _(act):
            act.sem_inc(sq_used, 2)
            for b in range(2):
                act.sem_inc(store_done[b], 16)

            def operand_tiles(n, tokens, m0, work, high):
                with act.Fori(0, KT) as k:
                    act.wait_ge(t_ready, k + (KT * n + 1))
                    m = act.activation(work[:, k, 0:T], work[:, k, 0:T], ACT.Identity,
                                       scale=gain[:, 0, bass.ds(k, 1)],
                                       bias=modx[:, bass.ds(k + m0, 1)])
                    if tokens > T:
                        m = act.activation(work[:, k, T:TA], work[:, k, T:TA], ACT.Identity,
                                           scale=gain[:, 1, bass.ds(k, 1)],
                                           bias=modc[:, bass.ds(k + m0, 1)])
                    m.then_inc(h_ready, 1)
                    act.wait_ge(h_ready, k + (KT * n + 1))
                    act.activation(high[:, k, 0:tokens], work[:, k, 0:tokens], ACT.Copy)\
                       .then_inc(xh_ready, 1)

            act.wait_ge(cond_in, 16)
            act.activation(crow_sb[:, :, :], crow_sb[:, :, :], ACT.Silu).then_inc(cond_ready, 1)
            act.wait_ge(x_in, 32)
            act_squares(act, 0, TA, xin, squares)
            act.wait_ge(gain_ready, 1)
            act_roots(act, 0, TA, rstd)
            act.wait_ge(gain_ready, 5)
            operand_tiles(0, TA, 0, xin, xh)

            def store_tile(t0, dst, i=None, tiles=0, units=0):
                b, u0, nu = t0 % 2, UNIT[t0], UNIT[t0 + 1] - UNIT[t0]
                act.wait_ge(store_done[b], step(16 * (t0 // 2 + 1), i, 8 * tiles))
                for n in range(nu):
                    u, w = u0 + n, min(H, TA - n * H)
                    act.wait_ge(unit_done, step(u + 1, i, units))
                    act.activation(stage[:, b, n * H:n * H + w], pb[u % 2][:, 0:w], ACT.Copy)\
                       .then_inc(bank_free[u % 2], 1)
                for u in (u0 + nu - 2, u0 + nu - 1):
                    act.wait_ge(bank_free[u % 2], step(u // 2 + 2, i, units // 2))
                act.dma_start(dst[:, 0:min(nu * H, TA)], stage[:, b, 0:min(nu * H, TA)])\
                   .then_inc(store_done[b], 16)

            kv_d = proj_d[0:T_LR].rearrange("(i j) p n -> i j p n", j=2)
            rest_d = proj_d[T_Q:T_POOL].rearrange("(i j) p n -> i j p n", j=2)
            act.wait_ge(xl_ready, KT)
            with act.Fori(0, T_LR // 2) as i:
                for b in range(2):
                    store_tile(b, kv_d[i, b], i, 2, 6)
            store_tile(T_LR, proj_d[T_LR])
            with act.Fori(0, (T_POOL - T_Q) // 2) as i:
                for b in range(2):
                    store_tile(T_Q + b, rest_d[i, b], i, 2, 4)

            for b in range(2):
                act.wait_ge(store_done[b], 16 * ((T_POOL - b + 1) // 2 + 1))
            end_phase(act, 1)
            for src, dst in ((tabs, tab), (lev, levf), (hmask, mask)):
                act.dma_start(dst[:, :, :], src).then_inc(tab_in, 16)
            act.dma_start(wup_sb[:, :], wup).then_inc(tab_in, 16)
            for q in p_out:
                act.sem_inc(q, 80)
            for q, n in ((p_vt, 1), (p_exp, 1), (p_kt, 1), (s_upd, 1), (s_mm, 1), (s_out[0], 16), (s_out[1], 16),
                         (f_exp, 4), (f_mul, 2), (f_pred, 7), (f_omm, 1), (f_oev, 1), (f_smm, 1),
                         (f_upd, 1)):
                act.sem_inc(q, n)
            act.wait_ge(tab_ready, 4)

            def rows_of(t0, n):
                return proj_d[t0:t0 + n].rearrange("t p (c n) -> p t c n", n=CH)

            def load_swapped(dst, src, sem):
                for quad in range(4):
                    act.dma_start(dst[32 * quad:32 * quad + 32], src[32 * (quad ^ 1):32 * (quad ^ 1) + 32])\
                       .then_inc(sem, 16)

            def p_load(c, b):
                act.dma_start(kc[:, b], rows_of(T_K, 4)[:, :, c, :]).then_inc(p_in[b], 16)
                load_swapped(ks[:, b], rows_of(T_K, 4)[:, :, c, :], p_in[b])
                act.dma_start(vc[:, b], rows_of(T_V, 8)[:, :, c, :]).then_inc(p_in[b], 16)
                for r in (0, 32):
                    act.dma_start(lrc[r:r + 16, b], rows_of(T_LR, 1)[r:r + 16, 0, c, :])\
                       .then_inc(p_in[b], 16)

            def p_chunk(i, b, more):
                c = i * 2 + b
                if more:
                    act.wait_ge(p_kt, c + 1)
                    p_load(i * 2 + (b + 1), 1 - b)
                act.wait_ge(p_gk, c + 1)
                act.activation(soft[:, :, :], g[:, 0:2, :], ACT.Abs).then_inc(p_act, 1)
                act.wait_ge(p_act, i * 4 + (2 * b + 1))
                act.activation(soft[:, :, :], soft[:, :, :], ACT.Exp, scale=-1.0).then_inc(p_act, 1)
                act.wait_ge(p_act, i * 4 + (2 * b + 2))
                act.activation(soft[:, :, :], soft[:, :, :], ACT.Ln, bias=1.0).then_inc(p_ln, 1)
                act.wait_ge(p_out[b], i * 80 + 80)
                act.wait_ge(p_vtr, c + 1)
                act.activation(vt[:, b, :].rearrange("p (a n) -> p a n", a=2), g[:, 3:5, :], ACT.Copy)\
                   .then_inc(p_vt, 1)
                act.wait_ge(p_la, c + 1)
                act.activation(lah[:, b], la[:, :, :], ACT.Copy).then_inc(p_lah, 1)
                act.wait_ge(p_arg, c + 1)
                act.wait_ge(p_kt, c + 1)
                act.activation(ef[:, :, :], g[:, 0:2, :], ACT.Exp)
                act.activation(dec[:, c, :], g[:, 5, 0:16].rearrange("p (a n) -> p a n", n=2)[:, :, 0],
                               ACT.Exp).then_inc(p_exp, 1)
                act.wait_ge(p_kr, c + 1)
                act.dma_start(kr_d[c], kr[:, b].rearrange("p h n -> p (h n)")).then_inc(p_out[b], 16)
                act.wait_ge(p_lal, c + 1)
                act.wait_ge(p_lah, c + 1)
                act.dma_start(la_d[c, 0], lah[:, b].bitcast(F32).rearrange("p h n -> p (h n)")).then_inc(p_out[b], 16)
                act.dma_start(la_d[c, 1], lal[:, b].bitcast(F32).rearrange("p h n -> p (h n)")).then_inc(p_out[b], 16)
                act.wait_ge(p_vt, c + 2)
                act.dma_start(vt_d[c], vt[:, b, :]).then_inc(p_out[b], 16)
                act.wait_ge(p_kt, c + 2)
                act.dma_start(kt_d[c], kt[:, b].rearrange("p h n -> p (h n)")).then_inc(p_out[b], 16)

            p_load(0, 0)
            with act.Fori(0, NC // 2 - 1) as i:
                for b in range(2):
                    p_chunk(i, b, True)
            p_chunk(NC // 2 - 1, 0, True)
            p_chunk(NC // 2 - 1, 1, False)
            for b in range(2):
                act.wait_ge(p_out[b], 80 * (NC // 2 + 1))
            end_phase(act, 2)

            def s_load(c, b, half):
                act.dma_start(skb[:, b, :], kt_d[c][:, half * H:half * H + H]).then_inc(s_in[b], 16)
                act.dma_start(svt[:, b, :], vt_d[c]).then_inc(s_in[b], 16)

            def s_step(n, b, c, then):
                act.wait_ge(s_mm, n + 1)
                if then is not None:
                    s_load(then[0], 1 - b, then[1])
                if c is not None:
                    act.wait_ge(s_upd, n + 2)
                    act.dma_start(sb_d[c], stb[:, b].rearrange("p h n -> p (h n)")).then_inc(s_out[b], 16)

            s_load(NC - 1, 0, 1)
            with act.Fori(0, NC // 2 - 1) as i:
                for b in range(2):
                    s_step(i * 2 + b, b, i * -2 + (NC - 1 - b), (i * -2 + (NC - 2 - b), 1))
            s_step(NC - 2, 0, 1, (0, 1))
            s_step(NC - 1, 1, 0, (NCX, 0))
            s_step(NC, 0, None, (NCX + 1, 0))
            for b in range(2):
                act.wait_ge(s_out[b], 16 * (NC // 2 + 1))
            end_phase(act, 3)

            def f_load(c, b):
                act.dma_start(fk[:, b].rearrange("p h n -> p (h n)"), kr_d[c]).then_inc(f_in[b], 16)
                act.dma_start(fq[:, b], rows_of(T_Q, 4)[:, :, c, :]).then_inc(f_in[b], 16)
                load_swapped(fs[:, b], rows_of(T_Q, 4)[:, :, c, :], f_in[b])
                act.dma_start(fla[:, b].bitcast(F32).rearrange("p a d n -> p a (d n)"),
                              la_d[c].rearrange("a p n -> p a n")).then_inc(f_in[b], 16)
                act.dma_start(fkt[:, b, :], kt_d[c][:, 0:H]).then_inc(f_in[b], 16)
                act.dma_start(fvt[:, b, :], vt_d[c]).then_inc(f_in[b], 16)
                act.dma_start(fsb[:, b].rearrange("p h n -> p (h n)"), sb_d[c]).then_inc(f_in[b], 16)

            def f_chunk(i, b, more):
                c = i * 2 + b
                if more:
                    act.wait_ge(f_smm, c + 1)
                    act.wait_ge(f_mul, i * 8 + (4 * b + 2))
                    f_load(i * 2 + (b + 1), 1 - b)
                act.wait_ge(f_lev, i * 16 + (8 * b + 1))
                act.wait_ge(f_omm, c + 1)
                act.activation(pt[:, :, :].rearrange("p h n -> p (h n)"), g[:, 4, :], ACT.Copy, scale=2.0)                   .then_inc(f_diag, 1)
                for n in range(4):
                    act.wait_ge(f_mul, i * 8 + (4 * b + n + 1))
                    for h in range(HEADS):
                        act.wait_ge(f_arg, i * 32 + (16 * b + 4 * n + h + 1))
                        act.activation(ex[:, n % 2, h, :], g[:, h, :], ACT.Exp).then_inc(f_exp, 1)
                act.wait_ge(f_omm, c + 2)
                act.activation(oall[:, :, :].rearrange("p t (c n) -> p c t n", n=CH)[:, c, :, :],
                               g[:, 2:4, :].rearrange("p a (t n) -> p (a t) n", n=CH), ACT.Copy)                   .then_inc(f_oev, 1)

            act.dma_start(tab[:, :, :], tabq).then_inc(tab_in, 16)
            f_load(0, 0)
            with act.Fori(0, NCX // 2 - 1) as i:
                for b in range(2):
                    f_chunk(i, b, True)
            f_chunk(NCX // 2 - 1, 0, True)
            f_chunk(NCX // 2 - 1, 1, False)
            end_phase(act, 4)

            for q, n in ((o_std, 1), (o_n, 1), (a_m, 2)):
                act.sem_inc(q, n)

            def q_load(n):
                act.dma_start(up[:, n % 2, PAD:PAD + T], proj_d[T_UB + n][:, 0:T]).then_inc(q_in[n % 2], 16)

            def q_high(grp):
                if grp:
                    act.wait_ge(q_dl, 2 * grp)
                act.dma_start(inv_sb[:, :], inv[:, grp, :]).then_inc(q_inv, 16)
                for n in (2 * grp, 2 * grp + 1):
                    if grp >= 2 and n % 2 == 0:
                        act.wait_ge(unit_done, UNIT[T_POOL] + 4 * grp - 4)
                    act.wait_ge(q_d, n + 1)
                    act.activation(dh[:, grp % 2, n % 2, :], sums[:, 1, 0:T], ACT.Copy).then_inc(q_dh, 1)
                    if n + 2 < 8:
                        q_load(n + 2)

            def q_gate(grp):
                for n in (2 * grp, 2 * grp + 1):
                    if n >= 2:
                        act.wait_ge(q_y, 2 * n - 2)
                    act.dma_start(zb[:, n % 2, :], proj_d[T_ZB + n][:, 0:T]).then_inc(q_z[n % 2], 16)
                for n in (2 * grp, 2 * grp + 1):
                    act.wait_ge(q_z[n % 2], 16 * (n // 2 + 1))
                    act.activation(zb[:, n % 2, :], zb[:, n % 2, :], ACT.Silu).then_inc(q_sil, 1)
                for n in (2 * grp, 2 * grp + 1):
                    for half in range(2):
                        u = 2 * n + half
                        act.wait_ge(q_y, u + 1)
                        act.activation(bh[:, n, H * half:H * half + H], yb[:, u % 2, :], ACT.Copy)\
                           .then_inc(q_yh, 1)

            act.wait_ge(q_pad, 1)
            q_load(0)
            q_load(1)
            q_high(0)
            for grp in range(1, 4):
                q_high(grp)
                q_gate(grp - 1)
            q_gate(3)

            act.wait_ge(unit_done, UNIT[T_B])
            act.dma_start(mix[:, :, :], proj_d[T_GB:T_GB + 8, :, 0:T].rearrange("t p n -> p t n"))\
               .then_inc(b_in, 16)
            act.wait_ge(b_in, 16)
            with act.Fori(0, 8) as t:
                act.activation(mix[:, t, :], mix[:, t, :], ACT.Sigmoid).then_inc(b_sg, 1)
            za_d = proj_d[T_ZA:T_ZA + 8].rearrange("(h v) p n -> h v p n", v=2)
            with act.Fori(0, HEADS) as h:
                act.wait_ge(o_st, h) if False else None
                act.wait_ge(o_std, h + 1)
                for v in range(2):
                    q = act.activation(osq[:, v, :], oall[:, h * 2 + v, :], ACT.Square)
                q.then_inc(o_sq, 1)
                act.wait_ge(o_st, h + 1)
                act.wait_ge(o_n, h * 2 + 1)
                for u in range(2):
                    r = act.activation(orstd[:, H * u:H * u + H], g[:, u, :], ACT.Sqrt, bias=epsc[:, 0:1])
                r.then_inc(o_std, 1)
                for v in range(2):
                    act.wait_ge(o_n, h * 2 + (v + 1))
                    act.dma_start(za[:, :], za_d[h, v][:, 0:T]).then_inc(o_in, 16)
                    act.wait_ge(o_in, h * 32 + (16 * v + 16))
                    act.activation(za[:, :], za[:, :], ACT.Silu).then_inc(o_sil, 1)
                    act.wait_ge(o_n, h * 2 + (v + 2))
                    act.activation(ah[:, h * 2 + v, :], oall[:, h * 2 + v, :], ACT.Copy).then_inc(o_h, 1)

            ga_d = proj_d[T_GA:T_GA + 8].rearrange("(i j) p n -> i j p n", j=2)
            act.wait_ge(o_l, 8)
            for b in range(2):
                act.dma_start(ga[:, b, :], ga_d[0, b][:, 0:T]).then_inc(a_in[b], 16)

            def a_high(i, b, load):
                act.wait_ge(a_m, i * 2 + (b + 3))
                act.activation(bh[:, i * 2 + b, :], mix[:, i * 2 + b, :], ACT.Copy).then_inc(a_mh, 1)
                if load:
                    act.dma_start(ga[:, b, :], ga_d[i + 1, b][:, 0:T]).then_inc(a_in[b], 16)

            def a_sigmoid(i, b):
                act.wait_ge(a_in[b], i * 16 + 16)
                act.activation(ga[:, b, :], ga[:, b, :], ACT.Sigmoid).then_inc(a_sg, 1)

            with act.Fori(0, 3) as i:
                for b in range(2):
                    a_sigmoid(i, b)
                for b in range(2):
                    a_high(i, b, True)
            for b in range(2):
                a_sigmoid(3, b)
            for b in range(2):
                a_high(3, b, False)

            act.wait_ge(a_ml, 8)
            act.dma_start(mix[:, :, :], xT).then_inc(r_in, 16)

            def tile_out(i, b):
                for n in range(2):
                    u = UNIT[T_OUT] + 2 * b + n
                    act.wait_ge(bank_free[u % 2], i * 2 + (u // 2 + 2))

            act_squares(act, 1, T, mix, sq1, tile_out)
            act_roots(act, 1, T, orstd)
            act.dma_start(xin[:, :, T:TA], ctx2T).then_inc(ctx2_in, 16)
            act.wait_ge(n1_x, 8)
            act.dma_start(xp_d.rearrange("t p n -> p t n"), xin[:, :, 0:T]).then_inc(xp_out, 16)
            act.wait_ge(ctx2_in, 16)
            act_squares(act, 2, TA, xin, squares)
            act_roots(act, 2, TA, rstd)
            act.wait_ge(xp_out, 16)
            operand_tiles(1, TA, 24, xin, xh)

            def read_out(t0, dst, func, i=None, tiles=0, units=0, scale=1.0):
                u0, nu = UNIT[t0], UNIT[t0 + 1] - UNIT[t0]
                for n in range(nu):
                    u, w = u0 + n, min(H, TA - n * H)
                    act.wait_ge(unit_done, step(u + 1, i, units))
                    act.activation(dst[:, n * H:n * H + w], pb[u % 2][:, 0:w], func, scale=scale)\
                       .then_inc(bank_free[u % 2], 1)

            act.wait_ge(xl_ready, 2 * KT)
            for t in range(4):
                read_out(T_CV + t, zcs[:, t, :], ACT.Copy if t < 2 else ACT.Sigmoid)
            with act.Fori(0, 2) as i:
                for b in range(2):
                    read_out(T_SG + b, zcs[:, i * 2 + (b + 4), :], ACT.Gelu_apprx_tanh, i, 2, 4)
            with act.Fori(0, 4) as i:
                for b in range(2):
                    read_out(T_K2 + b, zkv[:, i * 2 + b, :], ACT.Copy, i, 2, 6)
            with act.Fori(0, 2) as i:
                for b in range(2):
                    read_out(T_Q2 + b, zq[:, i * 2 + b, :], ACT.Copy, i, 2, 4, scale=0.125)
            for q, n in ((at_vtk, 1), (at_sc, 4), (at_ex, 2), (at_tr, 2), (at_ptc, 1), (at_pv, 2),
                         (at_o, 2), (at_ot, 2), (at_lo, 1)):
                act.sem_inc(q, n)
            end_phase(act, 5)

            act.dma_start(sgw_sb[:, :, :], sgw).then_inc(sg_in, 16)
            act.dma_start(sgb_sb[:, :, :], sgb).then_inc(sg_in, 16)
            act.wait_ge(z_dve, 1)
            act.activation(zcs[:, 2:4, :], zcs[:, 0:2, :], ACT.Square).then_inc(z_act, 1)
            act.wait_ge(y_dve, 1)
            act.activation(vsq[:, :, :], zcs[:, 6:8, :], ACT.Square).then_inc(y_act, 1)
            act.wait_ge(z_pe, 2)
            act.activation(zcs[:, 2:4, :].rearrange("p t (u n) -> p (t u) n", u=2), g[:, 0:4, :],
                           ACT.Sqrt, bias=epsc[:, 0:1]).then_inc(z_act, 1)
            act.wait_ge(y_pe, 2)
            act.activation(vroot[:, :].rearrange("p (u n) -> p u n", u=2), g[:, 4:6, :], ACT.Sqrt,
                           bias=epsc[:, 0:1]).then_inc(y_act, 1)
            act.wait_ge(y_dve, 3)
            for t in range(2):
                n, m = COL["sg_g"] + t, COL["sg_b"] + t
                v = act.activation(zcs[:, 6 + t, :], zcs[:, 6 + t, :], ACT.Identity,
                                   scale=col[:, n:n + 1], bias=col[:, m:m + 1])
            v.then_inc(y_act, 1)
            act.wait_ge(z_dve, 3)
            for t in range(2):
                n, m = COL["cv_g"] + t, COL["cv_nb"] + t
                v = act.activation(zcs[:, t, :], zcs[:, t, :], ACT.Silu, scale=col[:, n:n + 1],
                                   bias=col[:, m:m + 1])
            v.then_inc(z_act, 1)
            act.wait_ge(y_pe, 3)
            act.activation(vtok[:, :, :].rearrange("p (a n) c -> p a (n c)", a=4), g[:, 0:4, :],
                           ACT.Copy).then_inc(y_act, 1)
            act.wait_ge(z_act, 3)
            act.activation(mh[:, 6:8, :], zcs[:, 0:2, :], ACT.Copy).then_inc(z_act, 1)
            act.wait_ge(y_dve, 5)
            act.activation(mh[:, 4:6, :], zcs[:, 6:8, :], ACT.Copy).then_inc(y_act, 1)
            end_phase(act, 6)

            def at_exp(i, k):
                b = k % 2
                act.wait_ge(at_nm, i * 16 + (k + 1))
                act.wait_ge(at_tr, i * 16 + (k + 1))
                act.activation(pr[:, b, 0:H], sl[:, b, :], ACT.Exp, bias=tiny[:, b, 2:3],
                               accum_out=tiny[:, b, 3:4])
                act.activation(pr[:, b, H:H + C], pb[b][:, 0:C], ACT.Exp,
                               bias=tiny[:, b, 2:3], accum_out=tiny[:, b, 4:5]).then_inc(at_ex, 1)

            def at_high(i, k):
                bc, br, _ = step_of(k)
                act.wait_ge(at_ot, i * 8 + (k // 2 + 3))
                act.activation(at_tokens(br, bc)(mh[:, i, :]),
                               g[:, 4, P:2 * P].rearrange("p (r c) -> p r c", c=16), ACT.Copy)\
                   .then_inc(at_hi, 1)

            with act.Fori(0, AH // 2) as i:
                act.wait_ge(at_pv, i * 16 + 2)
                act.activation(ks2[:, :], zkv[:, i, :], ACT.Copy)
                act.activation(qs2[:, :].rearrange("p (b r c) -> p b r c", r=ROWS, c=16),
                               zq[:, i, :].rearrange("p (r b c) -> p b r c", b=4, c=16), ACT.Copy)\
                   .then_inc(at_stq, 1)
                for k in range(2):
                    at_exp(i, k)
                for k in range(16):
                    act.wait_ge(at_tr, i * 16 + (k + 3))
                    act.wait_ge(at_pv, i * 16 + (k + 1))
                    act.activation(ptr[:, k % 2, :],
                                   g[:, 2:4, :].rearrange("p a n -> p (a n)")[:, 0:H + C], ACT.Copy)\
                       .then_inc(at_ptc, 1)
                    if k and k % 2 == 0:
                        at_high(i, k - 1)
                    if k + 2 < 16:
                        at_exp(i, k + 2)
                at_high(i, 15)
            end_phase(act, 7)

            act.dma_start(x2[:, :, :], xp_d.rearrange("t p n -> p t n")).then_inc(x2_in, 16)

            def tile_added(u0):
                def wait(i, b):
                    for n in range(2):
                        u = u0 + 2 * b + n
                        act.wait_ge(bank_free[u % 2], i * 2 + (u // 2 + 2))
                return wait

            act_squares(act, 3, T, x2, sq2, tile_added(UNIT[T_W2]))
            act_roots(act, 3, T, root2)
            operand_tiles(2, T, 48, xw, mh)

            act.wait_ge(xl_ready, 3 * KT)
            act.wait_ge(f_pad, 1)

            def f_copy(t0, kt, tile, i=None):
                for n in range(2):
                    u = UNIT[t0] + n
                    act.wait_ge(unit_done, step(u + 1, i, 2 * F_UNITS))
                    if n == 0 and tile >= 2:
                        act.wait_ge(f_cv, step(3 * (tile - 1), i, 12))
                    act.activation(gp[:, kt, 1 + H * n:1 + H * n + H], pb[u % 2][:, :], ACT.Copy)\
                       .then_inc(bank_free[u % 2], 1)

            def f_silu(kt, tile, i=None):
                fb = COL["ff_b"] + tile
                act.wait_ge(f_cv, step(3 * (tile + 1), i, 12))
                if tile >= 2:
                    act.wait_ge(f_hid, step(2 * (tile - 1), i, 8))
                bias_of = col[:, fb:fb + 1] if i is None else col[:, bass.ds(i * 4 + fb, 1)]
                act.activation(sgm[:, kt, :], cb[:, kt, :], ACT.Silu, bias=bias_of).then_inc(f_sil, 1)

            def f_high(par, kt, tile, i=None):
                act.wait_ge(f_hid, step(2 * (tile + 1), i, 8))
                if tile >= 4:
                    act.wait_ge(unit_done, step(DOWN_END[tile // 2 - 2], i, 2 * F_UNITS))
                act.activation(hh[:, par, kt, :], cb[:, kt, :], ACT.Copy).then_inc(f_hh, 1)

            def f_up(group, i=None):
                for kt in range(2):
                    tile = 2 * group + kt
                    f_copy(UP[group] + 2 * kt, kt, tile, i)
                    f_silu(kt, tile, i)
                    f_high(group % 2, kt, tile, i)

            f_up(0)
            f_up(1)
            f_up(2)
            with act.Fori(0, (GROUPS - 3) // 2) as i:
                f_up(3, i)
                f_up(4, i)
            act_squares(act, 4, T, x2, cb, tile_added(DOWN_LAST))
            act_roots(act, 4, T, gp_root)
            with act.Fori(0, KT) as k:
                act.wait_ge(f_fin, k + 1)
                act.dma_start(out_tiles[k], x2[:, k, :]).then_inc(out_done, 16)
            act.wait_ge(out_done, 16 * KT)

        @block.vector
        def _(dve):
            def mod_tile(slot, buf, landed, tile, cond, ctx_done=None):
                dve.wait_ge(mod_in[buf], landed)
                dve.wait_ge(mod_free, tile + 1)
                if ctx_done is not None:
                    nc.vector.tensor_tensor_reduce(
                        out=prod[:, :], in0=mod_raw[:, buf, :], in1=crow_sb[:, cond + 1, :], scale=1.0,
                        scalar=0.0, op0=ALU.mult, op1=ALU.add,
                        accum_out=mod_sum[:, 1, slot:slot + 1]).then_inc(mod_ctx, 1)
                    dve.wait_ge(mod_ctx, ctx_done)
                nc.vector.tensor_tensor_reduce(
                    out=prod[:, :], in0=mod_raw[:, buf, :], in1=crow_sb[:, cond, :], scale=1.0,
                    scalar=0.0, op0=ALU.mult, op1=ALU.add,
                    accum_out=mod_sum[:, 0, slot:slot + 1]).then_inc(mod_free, 1)

            def mod_pairs(m0, n, landed, cond, ctx_done):
                vx = modx[:, m0:m0 + 2 * n].rearrange("p (i j) -> p i j", j=2)
                vc = modc[:, m0:m0 + 2 * n].rearrange("p (i j) -> p i j", j=2)
                with dve.Fori(0, n) as i:
                    dve.wait_ge(mod_kept, i + (5 + (m0 - 16) // 2))
                    for b in range(2):
                        mod_tile(b, b, i * 16 + landed, i * 2 + (m0 + b), cond,
                                 None if ctx_done is None else i * 2 + (ctx_done + b))
                    dve.wait_ge(mod_free, i * 2 + (m0 + 3))
                    if ctx_done is not None:
                        nc.vector.tensor_copy(vc[:, i, :], mod_sum[:, 1, 0:2])
                    nc.vector.tensor_copy(vx[:, i, :], mod_sum[:, 0, 0:2]).then_inc(mod_kept, 1)

            nc.vector.memset(epsc[:, :], EPS).then_inc(gain_ready, 1)
            nc.vector.memset(prod[:, :], 0.0).then_inc(mod_free, 1)
            dve.sem_inc(mod_kept, 1)
            dve.wait_ge(cond_ready, 1)
            with dve.Fori(0, 4) as i:
                dve.wait_ge(mod_kept, i + 1)
                for j in range(4):
                    mod_tile(j, j, i * 16 + 16, i * 4 + j, 0, i * 4 + (j + 1))
                dve.wait_ge(mod_free, i * 4 + 5)
                nc.vector.tensor_copy(modc[:, 0:16].rearrange("p (i j) -> p i j", j=4)[:, i, :],
                                      mod_sum[:, 1, :])
                nc.vector.tensor_copy(modx[:, 0:16].rearrange("p (i j) -> p i j", j=4)[:, i, :],
                                      mod_sum[:, 0, :]).then_inc(mod_kept, 1)

            def gains(n, m0, bias, norm, seen):
                for j, m in enumerate((modx, modc)):
                    nc.vector.tensor_tensor(m[:, m0:m0 + 16], m[:, m0:m0 + 16], bias, ALU.add)\
                      .then_inc(gain_ready, 1)
                dve.wait_ge(gain_ready, seen + 2)
                for j, m in enumerate((modx, modc)):
                    nc.vector.scalar_tensor_tensor(gain[:, j, :], m[:, m0 + 8:m0 + 16], 1.0, norm,
                                                   ALU.add, ALU.mult).then_inc(gain_ready, 1)

            dve.wait_ge(const_in, 32)
            dve.wait_ge(mod_kept, 5)
            gains(0, 0, col[:, COL["b_mod"]:COL["b_mod"] + 16], col[:, COL["norm_g"]:COL["norm_g"] + 8], 1)

            def reciprocals(n, tokens, root):
                dve.wait_ge(std_ready, n + 1)
                nc.vector.reciprocal(root[:, 0:tokens], root[:, 0:tokens]).then_inc(rstd_ready, 1)
                dve.wait_ge(rstd_ready, n + 1)

            def normalise(n, tokens, root, src, work, high, low):
                def low_part(k, count):
                    dve.wait_ge(xh_ready, count)
                    nc.vector.tensor_tensor(low[:, k, 0:tokens], work[:, k, 0:tokens],
                                            high[:, k, 0:tokens], ALU.subtract).then_inc(xl_ready, 1)

                def scaled(k):
                    nc.vector.tensor_tensor(work[:, k, 0:tokens], src[:, k, 0:tokens],
                                            root[:, 0:tokens], ALU.mult).then_inc(t_ready, 1)

                scaled(0)
                with dve.Fori(1, KT) as k:
                    scaled(k)
                    low_part(k - 1, k + KT * n)
                low_part(KT - 1, KT * n + KT)

            reciprocals(0, TA, rstd)
            normalise(0, TA, rstd, xin, xin, xh, xl)
            mod_pairs(16, 4, 80, 0, None)
            mod_pairs(24, 8, 144, 2, 17)
            mod_pairs(40, 16, 272, 2, None)

            end_phase(dve, 1)
            nc.vector.memset(lrc[:, :, :], 1.0).then_inc(tab_ready, 1)
            nc.vector.memset(stf[:, 0], 0.0).then_inc(tab_ready, 1)
            dve.wait_ge(tab_in, 64)
            nc.vector.tensor_copy(levr[:, :, :], levf[:, :, :]).then_inc(tab_ready, 1)
            nc.vector.tensor_copy(matr[:, :, :], mat[:, 4:7, :]).then_inc(tab_ready, 1)

            def p_chunk(i, b):
                c = i * 2 + b
                dve.wait_ge(p_in[b], i * 128 + 128)
                dve.wait_ge(p_out[b], i * 80 + 80)
                at_c = (bass.ds(c * CH, CH))
                cos = tab[:, 0, at_c].unsqueeze(1).to_broadcast([P, HEADS, CH])
                sin = tab[:, 1, at_c].unsqueeze(1).to_broadcast([P, HEADS, CH])
                nc.vector.tensor_tensor(kr[:, b], kc[:, b], cos, ALU.mult).then_inc(p_dve, 1)
                nc.vector.tensor_tensor(rot[:, :, :], ks[:, b], sin, ALU.mult).then_inc(p_dve, 1)
                dve.wait_ge(p_dve, i * 4 + (2 * b + 2))
                nc.vector.tensor_tensor(kr[:, b], kr[:, b], rot[:, :, :], ALU.add).then_inc(p_kr, 1)
                dve.wait_ge(p_gk, c + 1)
                dve.wait_ge(p_ln, c + 1)
                nc.vector.scalar_tensor_tensor(la[:, :, :], g[:, 0:2, :], 0.0, soft[:, :, :], ALU.min,
                                               ALU.subtract).then_inc(p_la, 1)
                dve.wait_ge(p_lah, c + 1)
                nc.vector.tensor_tensor(lal[:, b], la[:, :, :], lah[:, b], ALU.subtract).then_inc(p_lal, 1)
                dve.wait_ge(p_exp, c + 2)
                dve.wait_ge(p_ktr, c + 1)
                nc.vector.tensor_tensor(kt[:, b, 0, :], ef[:, 0, :], g[:, 2, :], ALU.mult)
                nc.vector.tensor_tensor(kt[:, b, 1, :], ef[:, 1, :], g[:, 2, :], ALU.mult).then_inc(p_kt, 1)

            with dve.Fori(0, NC // 2) as i:
                for b in range(2):
                    p_chunk(i, b)
            end_phase(dve, 2)

            def s_update(n, b, c, d, st, saved):
                dve.wait_ge(s_mm, n + 2)
                dve.wait_ge(s_upd, n + 2)
                if saved is not None:
                    dve.wait_ge(s_out[1 - b], saved)
                for h in range(HEADS):
                    u = nc.vector.scalar_tensor_tensor(
                        st[:, 1 - b, h, :], st[:, b, h, :], dec[:, c, 4 * d + h:4 * d + h + 1],
                        g[:, 2 * b + h // 2, DV * (h % 2):DV * (h % 2) + DV], ALU.mult, ALU.add)
                u.then_inc(s_upd, 1)

            nc.vector.memset(stb[:, 0], 0.0).then_inc(s_upd, 1)
            with dve.Fori(0, NC // 2) as i:
                for b in range(2):
                    s_update(i * 2 + b, b, i * -2 + (NC - 1 - b), 1, stb, i * 16 + (16 + 16 * b))
            for b in range(2):
                s_update(NC + b, b, NCX + b, 0, stf, None)
            end_phase(dve, 3)

            dve.wait_ge(tab_in, 80)

            def f_chunk(i, b):
                c = i * 2 + b
                dve.wait_ge(f_in[b], i * 160 + 160)
                at_c = (bass.ds(c * CH, CH))
                cos = tab[:, 0, at_c].unsqueeze(1).to_broadcast([P, HEADS, CH])
                sin = tab[:, 1, at_c].unsqueeze(1).to_broadcast([P, HEADS, CH])
                nc.vector.tensor_tensor(fq[:, b], fq[:, b], cos, ALU.mult).then_inc(f_rot, 1)
                nc.vector.tensor_tensor(frot[:, :, :], fs[:, b], sin, ALU.mult).then_inc(f_rot, 1)
                dve.wait_ge(f_rot, i * 4 + (2 * b + 2))
                nc.vector.tensor_tensor(fq[:, b], fq[:, b], frot[:, :, :], ALU.add).then_inc(f_qr, 1)
                dve.wait_ge(f_qr, c + 1)
                dve.wait_ge(f_smm, c + 1)
                for n in range(4):
                    half, d = n // 2, n % 2
                    dve.wait_ge(f_exp, i * 32 + (16 * b + 4 * n + 8))
                    part = half if d == 0 else 1 - half
                    src, dst = (fk, lk) if half == 0 else (fq, lq)
                    for l in range(LEVELS):
                        m = 1 << l
                        def blocks(x):
                            return x.rearrange("p h (k s m) -> p h k s m", s=2, m=m)[:, :, :, part, :]
                        nc.vector.tensor_tensor(
                            blocks(dst[:, l]), blocks(src[:, b]),
                            ex[:, n % 2, :, 64 * l:64 * l + 64].rearrange("p h (k m) -> p h k m", m=m),
                            ALU.mult)
                    nc.vector.tensor_tensor(
                        qi[:, d, :, 64 * half:64 * half + 64], fq[:, b, :, 64 * half:64 * half + 64],
                        ex[:, n % 2, :, 448:512], ALU.mult).then_inc(f_mul, 1)
                for l in range(LEVELS):
                    if l == 0:
                        dve.wait_ge(f_diag, c + 1)
                    dve.wait_ge(f_lev, i * 16 + (8 * b + l + 2))
                    dve.wait_ge(f_pred, i * 14 + (7 * b + l + 7))
                    nc.vector.memset(tick[:, :], 0.0)
                    nc.vector.copy_predicated(
                        pt[:, :, :], mask[:, l, :].bitcast(I32).unsqueeze(1).to_broadcast([P, HEADS, CH]),
                        g[:, 4 + (l + 1) % 2, :].rearrange("p (h n) -> p h n", n=CH)).then_inc(f_pred, 1)
                dve.wait_ge(f_smm, c + 2)
                dve.wait_ge(f_upd, c + 1)
                dve.wait_ge(f_omm, c + 2)
                for h in range(HEADS):
                    u = nc.vector.scalar_tensor_tensor(
                        stf[:, 1 - b, h, :], stf[:, b, h, :], dec[:, c, h:h + 1],
                        g[:, h // 2, DV * (h % 2):DV * (h % 2) + DV], ALU.mult, ALU.add)
                u.then_inc(f_upd, 1)

            with dve.Fori(0, NCX // 2) as i:
                for b in range(2):
                    f_chunk(i, b)
            end_phase(dve, 4)

            for b in range(2):
                nc.vector.memset(up[:, b, 0:PAD], 0.0)
                m = nc.vector.memset(up[:, b, PAD + T:PAD + T + PAD], 0.0)
            m.then_inc(q_pad, 1)
            steps = [0]

            def q_step(instruction):
                steps[0] += 1
                instruction.then_inc(q_s, 1)
                dve.wait_ge(q_s, steps[0])

            def q_pool(grp):
                for n in (2 * grp, 2 * grp + 1):
                    dve.wait_ge(q_in[n % 2], 16 * (n // 2 + 1))
                    if n:
                        dve.wait_ge(q_dl, n)
                    u = up[:, n % 2, :]
                    src, lo, hi = u, 1, T + 2 * PAD
                    q_step(nc.vector.tensor_tensor(sums[:, 0, lo:hi], src[:, lo - 1:hi - 1], src[:, lo:hi],
                                                   ALU.add))
                    cur = 0
                    for w in WINDOWS[:grp]:
                        k = w // 2
                        lo, hi = lo + k, hi - k
                        q_step(nc.vector.tensor_tensor(sums[:, 1 - cur, lo:hi], sums[:, cur, lo - k:hi - k],
                                                       sums[:, cur, lo + k:hi + k], ALU.add))
                        cur = 1 - cur
                    dve.wait_ge(q_inv, 16 * (grp + 1))
                    q_step(nc.vector.tensor_tensor(sums[:, 0, PAD:PAD + T], sums[:, cur, PAD:PAD + T],
                                                   inv_sb[:, :], ALU.mult))
                    nc.vector.tensor_tensor(sums[:, 1, 0:T], sums[:, 0, PAD:PAD + T], u[:, PAD:PAD + T],
                                            ALU.subtract).then_inc(q_d, 1)
                    dve.wait_ge(q_dh, n + 1)
                    nc.vector.tensor_tensor(dl[:, grp % 2, n % 2, :], sums[:, 1, 0:T],
                                            dh[:, grp % 2, n % 2, :], ALU.subtract).then_inc(q_dl, 1)

            def q_gate(grp):
                scale = COL["pool_scale"]

                def low_part(u):
                    dve.wait_ge(q_yh, u + 1)
                    half = slice(H * (u % 2), H * (u % 2) + H)
                    nc.vector.tensor_tensor(bl[:, u // 2, half], yb[:, u % 2, :], bh[:, u // 2, half],
                                            ALU.subtract).then_inc(q_yl, 1)

                for u in range(4 * grp, 4 * grp + 4):
                    n, half = u // 2, slice(H * (u % 2), H * (u % 2) + H)
                    unit = UNIT[T_POOL] + u
                    dve.wait_ge(unit_done, unit + 1)
                    dve.wait_ge(q_sil, n + 1)
                    if u >= 2:
                        dve.wait_ge(q_yl, u - 1)
                    nc.vector.scalar_tensor_tensor(
                        yb[:, u % 2, :], pb[unit % 2][:, :], col[:, scale + n:scale + n + 1],
                        zb[:, n % 2, half], ALU.mult, ALU.mult).then_inc(q_y, 1)
                    dve.wait_ge(q_y, u + 1)
                    nc.vector.tensor_copy(tick[:, :], yb[:, u % 2, 0:1]).then_inc(bank_free[unit % 2], 1)
                    if u % 4:
                        low_part(u - 1)
                low_part(4 * grp + 3)

            q_pool(0)
            for grp in range(1, 4):
                q_pool(grp)
                q_gate(grp - 1)
            q_gate(3)

            with dve.Fori(0, HEADS) as h:
                dve.wait_ge(o_std, h + 2)
                nc.vector.reciprocal(orstd[:, :], orstd[:, :]).then_inc(o_rec, 1)
                dve.wait_ge(o_rec, h + 1)
                for v in range(2):
                    t = h * 2 + v
                    nc.vector.tensor_tensor(oall[:, t, :], oall[:, t, :], orstd[:, :], ALU.mult)\
                      .then_inc(o_t, 1)
                    dve.wait_ge(o_t, t + 1)
                    dve.wait_ge(o_sil, t + 1)
                    gg = COL["gla_g"] + v
                    nc.vector.scalar_tensor_tensor(oall[:, t, :], oall[:, t, :], col[:, gg:gg + 1], za[:, :],
                                                   ALU.mult, ALU.mult).then_inc(o_n, 1)
                    dve.wait_ge(o_h, t + 1)
                    dve.wait_ge(o_n, t + 2)
                    nc.vector.tensor_tensor(al[:, t, :], oall[:, t, :], ah[:, t, :], ALU.subtract)\
                      .then_inc(o_l, 1)
                for v in range(2):
                    t = h * 2 + v
                    dve.wait_ge(b_sg, t + 1)
                    for n in range(2):
                        u = UNIT[T_B] + 2 * v + n
                        dve.wait_ge(unit_done, h * 4 + (u + 1))
                        half = slice(H * n, H * n + H)
                        nc.vector.tensor_tensor(mix[:, t, half], mix[:, t, half], pb[u % 2][:, :], ALU.mult)\
                          .then_inc(bank_free[u % 2], 1)

            with dve.Fori(0, 4) as i:
                for b in range(2):
                    t = i * 2 + b
                    dve.wait_ge(a_sg, t + 1)
                    for n in range(2):
                        u = UNIT[T_A] + 2 * b + n
                        dve.wait_ge(unit_done, i * 4 + (u + 1))
                        half = slice(H * n, H * n + H)
                        nc.vector.tensor_tensor(ga[:, b, half], ga[:, b, half], pb[u % 2][:, :], ALU.mult)\
                          .then_inc(bank_free[u % 2], 1)
                    for u in (UNIT[T_A] + 2 * b, UNIT[T_A] + 2 * b + 1):
                        dve.wait_ge(bank_free[u % 2], i * 2 + (u // 2 + 2))
                    nc.vector.tensor_tensor(mix[:, t, :], mix[:, t, :], ga[:, b, :], ALU.add)\
                      .then_inc(a_m, 1)
                    dve.wait_ge(a_m, t + 3)
                    dve.wait_ge(a_mh, t + 1)
                    nc.vector.tensor_tensor(bl[:, t, :], mix[:, t, :], bh[:, t, :], ALU.subtract)\
                      .then_inc(a_ml, 1)

            gb = COL["b_mod"] + 16
            nc.vector.tensor_tensor(modx[:, 16:24], modx[:, 16:24], col[:, gb:gb + 8], ALU.add)\
              .then_inc(gain_ready, 1)
            dve.wait_ge(gain_ready, 6)
            dve.wait_ge(r_in, 16)
            with dve.Fori(0, 4) as i:
                for b in range(2):
                    t = i * 2 + b
                    for n in range(2):
                        u = UNIT[T_OUT] + 2 * b + n
                        dve.wait_ge(unit_done, i * 4 + (u + 1))
                        half = slice(H * n, H * n + H)
                        nc.vector.scalar_tensor_tensor(
                            mix[:, t, half], pb[u % 2][:, :], modx[:, bass.ds(i * 2 + (16 + b), 1)],
                            mix[:, t, half], ALU.mult, ALU.add).then_inc(bank_free[u % 2], 1)

            dve.wait_ge(mod_kept, 29)
            ab = COL["ada_b"]
            gains(1, 24, col[:, ab:ab + 16], col[:, COL["norm1_g"]:COL["norm1_g"] + 8], 6)
            nc.vector.tensor_tensor(modx[:, 40:72], modx[:, 40:72], col[:, ab + 16:ab + 48], ALU.add)\
              .then_inc(gain_ready, 1)
            reciprocals(1, T, orstd)
            for u in (UNIT[T_OUT] + 14, UNIT[T_OUT] + 15):
                dve.wait_ge(bank_free[u % 2], u // 2 + 2)
            with dve.Fori(0, KT) as k:
                nc.vector.scalar_tensor_tensor(
                    xin[:, k, 0:T], mix[:, k, :], col[:, bass.ds(k + COL["final_g"], 1)], orstd[:, :],
                    ALU.mult, ALU.mult).then_inc(n1_x, 1)
            reciprocals(2, TA, rstd)
            dve.wait_ge(xp_out, 16)
            normalise(1, TA, rstd, xin, xin, xh, xl)

            dve.wait_ge(xl_ready, 2 * KT)
            half = TAPS // 2
            nc.vector.memset(hpad[:, :, 0:half], 0.0)
            nc.vector.memset(hpad[:, :, half + T:half + T + half], 0.0).then_inc(z_h, 1)
            for t in range(2):
                for u in range(UNIT[T_CV + 3], UNIT[T_CV + 4]) if t == 0 else ():
                    dve.wait_ge(bank_free[u % 2], u // 2 + 2)
                nc.vector.tensor_tensor(hpad[:, t, half:half + T], zcs[:, t, :], zcs[:, 2 + t, :],
                                        ALU.mult).then_inc(z_h, 1)
            dve.wait_ge(z_h, 3)
            cw, cbias = COL["cv_w"], COL["cv_b"]
            for t in range(2):
                nc.vector.tensor_scalar(zcs[:, t, :], hpad[:, t, 0:T], col[:, cw + TAPS * t:cw + TAPS * t + 1],
                                        col[:, cbias + t:cbias + t + 1], ALU.mult, ALU.add).then_inc(z_cv, 1)
            with dve.Fori(1, TAPS) as tap:
                for t in range(2):
                    dve.wait_ge(z_cv, tap * 2 + (t - 1))
                    nc.vector.scalar_tensor_tensor(
                        zcs[:, t, :], hpad[:, t, bass.ds(tap, T)], col[:, bass.ds(tap + (cw + TAPS * t), 1)],
                        zcs[:, t, :], ALU.mult, ALU.add).then_inc(z_cv, 1)
            end_phase(dve, 5)

            dve.wait_ge(z_pe, 1)
            nc.vector.tensor_tensor(zcs[:, 0:2, :].rearrange("p t (u n) -> p (t u) n", u=2),
                                    zcs[:, 0:2, :].rearrange("p t (u n) -> p (t u) n", u=2), g[:, 0:4, :],
                                    ALU.subtract).then_inc(z_dve, 1)
            dve.wait_ge(y_pe, 1)
            for t in range(2):
                v = nc.vector.tensor_tensor(zcs[:, 6 + t, :].rearrange("p (u n) -> p u n", u=2),
                                            zcs[:, 6 + t, :].rearrange("p (u n) -> p u n", u=2),
                                            g[:, 4:6, :], ALU.subtract)
            v.then_inc(y_dve, 1)
            dve.wait_ge(y_act, 2)
            nc.vector.reciprocal(vroot[:, :], vroot[:, :]).then_inc(y_dve, 1)
            dve.wait_ge(y_dve, 2)
            nc.vector.tensor_tensor(zcs[:, 6:8, :], zcs[:, 6:8, :],
                                    vroot[:, :].unsqueeze(1).to_broadcast([P, 2, T]), ALU.mult)\
              .then_inc(y_dve, 1)
            dve.wait_ge(z_act, 2)
            nc.vector.reciprocal(zcs[:, 2:4, :], zcs[:, 2:4, :]).then_inc(z_dve, 1)
            dve.wait_ge(z_dve, 2)
            nc.vector.tensor_tensor(zcs[:, 0:2, :], zcs[:, 0:2, :], zcs[:, 2:4, :], ALU.mult)\
              .then_inc(z_dve, 1)
            dve.wait_ge(z_act, 4)
            nc.vector.tensor_tensor(ml[:, 6:8, :], zcs[:, 0:2, :], mh[:, 6:8, :], ALU.subtract)\
              .then_inc(z_dve, 1)
            dve.wait_ge(y_pe, 4)
            dve.wait_ge(sg_in, 32)
            for t in range(2):
                v = nc.vector.tensor_tensor(
                    zcs[:, 6 + t, :].rearrange("p (n q) -> p n q", q=CH),
                    g[:, 2 * t:2 * t + 2, :].rearrange("p a (n q) -> p (a n) q", q=CH),
                    sgb_sb[:, t, :].unsqueeze(1).to_broadcast([P, NCX, CH]), ALU.add)
            v.then_inc(y_dve, 1)
            dve.wait_ge(y_dve, 4)
            nc.vector.tensor_tensor(zcs[:, 6:8, :], zcs[:, 6:8, :], zcs[:, 4:6, :], ALU.mult)\
              .then_inc(y_dve, 1)
            dve.wait_ge(y_act, 5)
            nc.vector.tensor_tensor(ml[:, 4:6, :], zcs[:, 6:8, :], mh[:, 4:6, :], ALU.subtract)\
              .then_inc(y_dve, 1)
            end_phase(dve, 6)

            def at_values(i, n, dst):
                dve.wait_ge(at_vt, i * 5 + (n + 1))
                w = C if n == 0 else H
                if n >= 3:
                    dve.wait_ge(at_pv, i * 16 + (4 * (n - 2) + 2))
                nc.vector.tensor_copy(dst, g[:, 5, 0:w]).then_inc(at_vtk, 1)

            def at_scores(i, k):
                b, bc = k % 2, k // 4
                if k % 4 == 0:
                    at_values(i, bc + 1, vtk[:, bc % 2, :])
                dve.wait_ge(bias_in[k % 4], i * 64 + (16 * (k // 4) + 16))
                dve.wait_ge(at_s, i * 16 + (k + 1))
                dve.wait_ge(at_ex, i * 16 + (k + 1))
                nc.vector.memset(tick[:, :], 0.0)
                nc.vector.tensor_tensor_reduce(
                    out=sl[:, b, :], in0=g[:, b, :], in1=at_bias[:, k % 4, :], scale=1.0, scalar=-3e38,
                    op0=ALU.add, op1=ALU.max, accum_out=tiny[:, b, 0:1]).then_inc(at_sc, 1)
                nc.vector.tensor_reduce(tiny[:, b, 1:2], pb[b][:, 0:C], mybir.AxisListType.X,
                                        ALU.max).then_inc(at_m, 1)
                dve.wait_ge(at_sc, i * 16 + (k + 5))
                dve.wait_ge(at_m, i * 16 + (k + 1))
                nc.vector.tensor_scalar(tiny[:, b, 2:3], tiny[:, b, 0:1], tiny[:, b, 1:2], -1.0, ALU.max,
                                        ALU.mult).then_inc(at_nm, 1)

            def at_low(i, k):
                bc, br, _ = step_of(k)
                dve.wait_ge(at_hi, i * 8 + (k // 2 + 1))
                nc.vector.tensor_tensor(at_tokens(br, bc)(ml[:, i, :]),
                                        g[:, 4, P:2 * P].rearrange("p (r c) -> p r c", c=16),
                                        at_tokens(br, bc)(mh[:, i, :]), ALU.subtract).then_inc(at_lo, 1)

            with dve.Fori(0, AH // 2) as i:
                dve.wait_ge(at_pv, i * 16 + 2)
                v_rows = zkv[:, i + 4, 0:T].rearrange("p (r c) -> p r c", c=GRID_W)
                for w, first in enumerate(KSPAN):
                    nc.vector.tensor_copy(vs2[:, H * w:H * w + H].rearrange("p (r c) -> p r c", c=32),
                                          v_rows[:, :, first:first + 32])
                nc.vector.tensor_copy(vs2[:, 4 * H:4 * H + C], zkv[:, i + 4, T:TA]).then_inc(at_stv, 1)
                at_values(i, 0, vcx[:, :])
                for k in range(2):
                    at_scores(i, k)
                for k in range(16):
                    b = k % 2
                    dve.wait_ge(at_ex, i * 16 + (k + 3))
                    nc.vector.tensor_tensor(tiny[:, b, 5:6], tiny[:, b, 3:4], tiny[:, b, 4:5], ALU.add)\
                      .then_inc(at_sum, 1)
                    dve.wait_ge(at_sum, i * 16 + (k + 1))
                    nc.vector.reciprocal(tiny[:, b, 6:7], tiny[:, b, 5:6]).then_inc(at_r, 1)
                    if k and k % 2 == 0:
                        at_low(i, k - 1)
                    if k + 2 < 16:
                        at_scores(i, k + 2)
                    dve.wait_ge(at_pv, i * 16 + (k + 3))
                    dve.wait_ge(at_r, i * 16 + (k + 1))
                    dve.wait_ge(at_ot, i * 8 + (k // 2 + 1))
                    nc.vector.tensor_scalar(osb[:, k // 2 % 2, 64 * b:64 * b + 64],
                                            g[:, 4, 64 * b:64 * b + 64], tiny[:, b, 6:7], None,
                                            ALU.mult).then_inc(at_o, 1)
                at_low(i, 15)
            end_phase(dve, 7)

            gains_x = COL["norm2_g"]
            nc.vector.scalar_tensor_tensor(gain[:, 0, :], modx[:, 56:64], 1.0,
                                           col[:, gains_x:gains_x + 8], ALU.add, ALU.mult)\
              .then_inc(gain_ready, 1)
            dve.wait_ge(x2_in, 16)
            with dve.Fori(0, 4) as i:
                for b in range(2):
                    for n in range(2):
                        u = UNIT[T_W2] + 2 * b + n
                        dve.wait_ge(unit_done, i * 4 + (u + 1))
                        half = slice(H * n, H * n + H)
                        nc.vector.scalar_tensor_tensor(
                            x2[:, i * 2 + b, half], pb[u % 2][:, :], modx[:, bass.ds(i * 2 + (40 + b), 1)],
                            x2[:, i * 2 + b, half], ALU.mult, ALU.add).then_inc(bank_free[u % 2], 1)
            reciprocals(3, T, root2)
            for u in (UNIT[T_FF] - 2, UNIT[T_FF] - 1):
                dve.wait_ge(bank_free[u % 2], u // 2 + 2)
            normalise(2, T, root2, x2, xw, mh, ml)

            dve.wait_ge(xl_ready, 3 * KT)
            nc.vector.memset(gp[:, :, 0:1], 0.0)
            nc.vector.memset(gp[:, :, T + 1:T + 2], 0.0).then_inc(f_pad, 1)
            dve.wait_ge(f_pad, 1)

            def f_taps(t0, kt, tile, i=None):
                fw = COL["ff_w"] + 3 * tile
                for u in (UNIT[t0], UNIT[t0] + 1):
                    dve.wait_ge(bank_free[u % 2], step(u // 2 + 2, i, F_UNITS))
                if tile >= 2:
                    dve.wait_ge(f_hl, step(tile - 1, i, 4))
                for tap in range(3):
                    w = col[:, fw + tap:fw + tap + 1] if i is None else col[:, bass.ds(i * 12 + (fw + tap), 1)]
                    if tap == 0:
                        v = nc.vector.tensor_scalar(cb[:, kt, :], gp[:, kt, 0:T], w, None, ALU.mult)
                    else:
                        v = nc.vector.scalar_tensor_tensor(cb[:, kt, :], gp[:, kt, tap:tap + T], w,
                                                           cb[:, kt, :], ALU.mult, ALU.add)
                    v.then_inc(f_cv, 1)
                    if tap < 2:
                        dve.wait_ge(f_cv, step(3 * tile + tap + 1, i, 12))

            def f_hidden(t0, kt, tile, i=None):
                dve.wait_ge(f_sil, step(tile + 1, i, 4))
                for n in range(2):
                    u = UNIT[t0] + n
                    dve.wait_ge(unit_done, step(u + 1, i, 2 * F_UNITS))
                    half = slice(H * n, H * n + H)
                    nc.vector.tensor_tensor(cb[:, kt, half], sgm[:, kt, half], pb[u % 2][:, :], ALU.mult)\
                      .then_inc(f_hid, 1)
                    dve.wait_ge(f_hid, step(2 * tile + n + 1, i, 8))
                    nc.vector.tensor_copy(tick[:, :], cb[:, kt, H * n:H * n + 1])\
                      .then_inc(bank_free[u % 2], 1)

            def f_low(par, kt, tile, i=None):
                dve.wait_ge(f_hh, step(tile + 1, i, 4))
                nc.vector.tensor_tensor(hl[:, par, kt, :], cb[:, kt, :], hh[:, par, kt, :], ALU.subtract)\
                  .then_inc(f_hl, 1)

            def f_up(group, i=None):
                for kt in range(2):
                    tile, t = 2 * group + kt, UP[group] + 2 * kt
                    f_taps(t, kt, tile, i)
                    f_hidden(t + 1, kt, tile, i)
                    f_low(group % 2, kt, tile, i)

            def f_down(group, i=None):
                u0 = UNIT[DOWN[group]]
                if group:
                    for u in (DOWN_END[group - 1] - 2, DOWN_END[group - 1] - 1):
                        dve.wait_ge(bank_free[u % 2], step(u // 2 + 2, i, F_UNITS))
                for m in range(KT):
                    for n in range(2):
                        u = u0 + 2 * m + n
                        dve.wait_ge(unit_done, step(u + 1, i, 2 * F_UNITS))
                        half = slice(H * n, H * n + H)
                        nc.vector.scalar_tensor_tensor(
                            x2[:, m, half], pb[u % 2][:, :], modx[:, 64 + m:65 + m], x2[:, m, half],
                            ALU.mult, ALU.add).then_inc(bank_free[u % 2], 1)

            f_up(0)
            f_up(1)
            f_down(0)
            f_up(2)
            f_down(1)
            with dve.Fori(0, (GROUPS - 3) // 2) as i:
                f_up(3, i)
                f_down(2, i)
                f_up(4, i)
                f_down(3, i)
            f_down(GROUPS - 1)
            reciprocals(4, T, gp_root)
            for u in (UNIT[NT] - 2, UNIT[NT] - 1):
                dve.wait_ge(bank_free[u % 2], u // 2 + 2)
            with dve.Fori(0, KT) as k:
                nc.vector.scalar_tensor_tensor(
                    x2[:, k, :], x2[:, k, :], col[:, bass.ds(k + COL["final_g2"], 1)], gp_root,
                    ALU.mult, ALU.mult).then_inc(f_fin, 1)

        @block.tensor
        def _(pe):
            for b in range(2):
                pe.sem_inc(bank_free[b], 1)
            pe.wait_ge(const_in, 32)
            pe_squares(pe, 0, TA, squares)
            pe_tile(pe, 0, ready=1)
            pe_tile(pe, 1)
            with pe.Fori(1, T_LR // 2) as i:
                for b in range(2):
                    pe_tile(pe, b, i, 2, 6)
            pe_tile(pe, T_LR)
            with pe.Fori(0, (T_POOL - T_Q) // 2) as i:
                for b in range(2):
                    pe_tile(pe, T_Q + b, i, 2, 4)

            end_phase(pe, 1)
            pe.wait_ge(tab_ready, 4)

            def p_chunk(i, b):
                c = i * 2 + b
                pe.wait_ge(p_in[b], i * 128 + 128)
                pe.wait_ge(p_exp, c + 1)
                for d in range(2):
                    r = slice(32 * d, 32 * d + 17)
                    mm = pe.matmul(g[:, d, :], lrc[r, b, :], wup_sb[r, :], start=True, stop=True)
                mm.then_inc(p_gk, 1)
                pe.wait_ge(p_vt, c + 1)
                for n in range(8):
                    mm = pe.transpose(g[:, 3 + n // 4, CH * (n % 4):CH * (n % 4) + CH], vc[:, b, n, :], ident)
                mm.then_inc(p_vtr, 1)
                pe.wait_ge(p_kr, c + 1)
                pe.wait_ge(p_kt, c + 1)
                for h in range(HEADS):
                    mm = pe.transpose(g[:, 2, CH * h:CH * h + CH], kr[:, b, h, :], ident)
                mm.then_inc(p_ktr, 1)
                pe.wait_ge(p_lal, c + 1)
                for d in range(2):
                    for n, x in enumerate((lah, lal)):
                        pe.matmul(g[:, d, :], matr[:, d, :], x[:, b, d, :], start=(n == 0), stop=(n == 1))
                for d in range(2):
                    for h in range(HEADS):
                        o = 2 * (HEADS * d + h)
                        for n, x in enumerate((lah, lal)):
                            mm = pe.matmul(g[:, 5, o:o + 2], x[:, b, d, DK * h:DK * h + DK],
                                           matr[:, 2, 0:2], start=(n == 0), stop=(n == 1))
                mm.then_inc(p_arg, 1)

            with pe.Fori(0, NC // 2) as i:
                for b in range(2):
                    p_chunk(i, b)
            end_phase(pe, 2)

            def s_products(n, b, loads):
                pe.wait_ge(s_in[b], loads)
                pe.wait_ge(s_upd, n + 1)
                for h in range(HEADS):
                    mm = pe.matmul(g[:, 2 * b + h // 2, DV * (h % 2):DV * (h % 2) + DV],
                                   skb[:, b, DK * h:DK * h + DK], svt[:, b, DV * h:DV * h + DV],
                                   start=True, stop=True)
                mm.then_inc(s_mm, 1)

            with pe.Fori(0, NC // 2) as i:
                for b in range(2):
                    s_products(i * 2 + b, b, i * 32 + 32)
            for b in range(2):
                s_products(NC + b, b, 32 * (NC // 2 + 1))
            end_phase(pe, 3)

            def f_chunk(i, b):
                c = i * 2 + b

                def scores(m, keys, queries):
                    for h in range(HEADS):
                        mm = pe.matmul(g[:, 4 + m % 2, CH * h:CH * h + CH], keys[:, h, :],
                                       queries[:, h, :], start=True, stop=True)
                    mm.then_inc(f_lev, 1)

                pe.wait_ge(f_in[b], i * 160 + 160)
                pe.wait_ge(f_qr, c + 1)
                pe.wait_ge(f_pred, i * 14 + (7 * b + 6))
                scores(0, fk[:, b], fq[:, b])
                pe.wait_ge(f_upd, c + 1)
                pe.wait_ge(f_oev, c + 1)
                for n in range(4):
                    half, d = n // 2, n % 2
                    for h in range(HEADS):
                        pe.wait_ge(f_exp, i * 32 + (16 * b + 4 * n + h + 1))
                        for x in range(2):
                            mm = pe.matmul(g[:, h, :], fla[:, b, x, d, DK * h:DK * h + DK],
                                           levr[:, d, H * half:H * half + H], start=(x == 0), stop=(x == 1))
                        mm.then_inc(f_arg, 1)
                pe.wait_ge(f_mul, i * 8 + (4 * b + 6))
                for l in range(LEVELS):
                    if l == 1:
                        pe.wait_ge(f_diag, c + 1)
                    pe.wait_ge(f_pred, i * 14 + (7 * b + (7 if l == 0 else l + 6)))
                    scores(l + 1, lk[:, l], lq[:, l])
                pe.wait_ge(f_pred, i * 14 + (7 * b + 14))
                for h in range(HEADS):
                    for v in range(2):
                        o = g[:, 2 + h // 2, DV * (h % 2) + CH * v:DV * (h % 2) + CH * v + CH]
                        f = slice(DV * h + CH * v, DV * h + CH * v + CH)
                        pe.matmul(o, fvt[:, b, f], pt[:, h, :], start=True, stop=False)
                        pe.matmul(o, stf[:, b, h, CH * v:CH * v + CH], qi[:, 0, h, :], start=False, stop=False)
                        mm = pe.matmul(o, fsb[:, b, h, CH * v:CH * v + CH], qi[:, 1, h, :], start=False,
                                       stop=True)
                mm.then_inc(f_omm, 1)
                for h in range(HEADS):
                    mm = pe.matmul(g[:, h // 2, DV * (h % 2):DV * (h % 2) + DV], fkt[:, b, DK * h:DK * h + DK],
                                   fvt[:, b, DV * h:DV * h + DV], start=True, stop=True)
                mm.then_inc(f_smm, 1)

            with pe.Fori(0, NCX // 2) as i:
                for b in range(2):
                    f_chunk(i, b)
            end_phase(pe, 4)

            for grp in range(4):
                t = T_POOL + grp // 2
                if grp % 2 == 0:
                    pe.wait_ge(w_split, t + 1)
                pe.wait_ge(q_dl, 2 * grp + 2)
                for m in range(2):
                    for half in range(2):
                        u = UNIT[T_POOL] + 4 * grp + 2 * m + half
                        pe.wait_ge(bank_free[u % 2], u // 2 + 1)
                        first, last = pe_unit(pe, t % 2, dh[:, grp % 2], dl[:, grp % 2],
                                              slice(H * half, H * half + H), range(2),
                                              [512 * (grp % 2) + 256 * k + P * m for k in range(2)], u % 2)
                        if grp % 2 == 0 and m == 0 and half == 0:
                            first.then_inc(w_begun, 1)
                        last.then_inc(unit_done, 1)

            pe.wait_ge(q_yl, 16)
            with pe.Fori(0, HEADS) as h:
                pe.wait_ge(o_sq, h + 1)
                for u in range(2):
                    for v in range(2):
                        mm = pe.matmul(g[:, u, :], mean_v, osq[:, v, H * u:H * u + H], start=(v == 0),
                                       stop=(v == 1))
                mm.then_inc(o_st, 1)
                for b in range(2):
                    pe_tile(pe, T_B + b, h, 2, 4, bh, bl)

            pe.wait_ge(o_l, 8)
            with pe.Fori(0, 4) as i:
                for b in range(2):
                    pe_tile(pe, T_A + b, i, 2, 4, ah, al)
            pe.wait_ge(a_ml, 8)
            with pe.Fori(0, 4) as i:
                for b in range(2):
                    pe_tile(pe, T_OUT + b, i, 2, 4, bh, bl)
            pe_squares(pe, 1, T, sq1)
            pe_squares(pe, 2, TA, squares)

            pe_tile(pe, T_CV, ready=KT + 1)
            for t in range(T_CV + 1, T_SG):
                pe_tile(pe, t)
            with pe.Fori(0, 2) as i:
                for b in range(2):
                    pe_tile(pe, T_SG + b, i, 2, 4)
            with pe.Fori(0, 4) as i:
                for b in range(2):
                    pe_tile(pe, T_K2 + b, i, 2, 6)
            with pe.Fori(0, 2) as i:
                for b in range(2):
                    pe_tile(pe, T_Q2 + b, i, 2, 4)
            end_phase(pe, 5)

            def conv_means(src):
                for t in range(2):
                    for n in range(2):
                        mm = pe.matmul(g[:, 2 * t + n, :], mean_g, src[:, t, H * n:H * n + H], start=True,
                                       stop=True)
                mm.then_inc(z_pe, 1)

            def gating_means(src):
                for n in range(2):
                    for t in range(2):
                        mm = pe.matmul(g[:, 4 + n, :], mean_v, src[:, t, H * n:H * n + H], start=(t == 0),
                                       stop=(t == 1))
                mm.then_inc(y_pe, 1)

            conv_means(zcs[:, 0:2, :])
            gating_means(zcs[:, 6:8, :])
            pe.wait_ge(z_act, 1)
            pe.wait_ge(z_dve, 1)
            conv_means(zcs[:, 2:4, :])
            pe.wait_ge(y_act, 1)
            gating_means(vsq[:, :, :])
            pe.wait_ge(z_act, 2)
            pe.wait_ge(y_act, 3)
            for n in range(NCX):
                for t in range(2):
                    o = (2 * n + t) * P
                    mm = pe.transpose(g[:, o // H, o % H:o % H + P], zcs[:, 6 + t, CH * n:CH * n + CH], ident)
            mm.then_inc(y_pe, 1)
            pe.wait_ge(y_act, 4)
            pe.wait_ge(sg_in, 32)
            for n in range(NCX):
                for q in range(4):
                    t, r = q // 2, 64 * (q % 2)
                    mm = pe.matmul(g[r:r + 64, 2 * t + n // 4, CH * (n % 4):CH * (n % 4) + CH],
                                   vtok[:, n, 64 * q:64 * q + 64], sgw_sb[:, q, :], start=True, stop=True)
            mm.then_inc(y_pe, 1)
            end_phase(pe, 6)

            def at_scores(i, k):
                bc, br, j = step_of(k)
                head = slice(64 * j, 64 * j + 64)

                def transposed(n, first, chunks):
                    pe.wait_ge(at_vtk, i * 5 + (n + 1))
                    for c in range(chunks):
                        mm = pe.transpose(g[:, 5, P * c:P * c + P], vs2[:, first + P * c:first + P * c + P],
                                          ident)
                    mm.then_inc(at_vt, 1)

                window = slice(KSPAN[bc], KSPAN[bc] + 32)
                if k == 0:
                    transposed(0, 4 * H, 2)
                if k % 4 == 0:
                    transposed(bc + 1, H * bc, 4)
                pe.wait_ge(at_ex, i * 16 + (k + 1))
                block = 2 * bc + br
                q = qs2[head, P * block:P * block + P]
                pe.matmul(g[:, k % 2, :], q, ks2[head, 0:T].rearrange("p (r c) -> p r c", c=GRID_W)[:, :, window],
                          start=True, stop=True)
                pe.matmul(pb[k % 2][:, 0:C], q, ks2[head, T:TA], start=True, stop=True)\
                  .then_inc(at_s, 1)

            def at_output(i, k):
                pe.wait_ge(at_o, i * 16 + (k + 3))
                pe.wait_ge(at_lo, i * 8 + (k // 2 + 1))
                pe.transpose(g[:, 4, P:2 * P], osb[:, k // 2 % 2, :], ident).then_inc(at_ot, 1)

            with pe.Fori(0, AH // 2) as i:
                pe.wait_ge(at_stv, i + 1)
                pe.wait_ge(at_stq, i + 1)
                for k in range(2):
                    at_scores(i, k)
                for k in range(16):
                    bc, br, j = step_of(k)
                    pe.wait_ge(at_ex, i * 16 + (k + 3))
                    pe.wait_ge(at_ptc, i * 16 + (k + 1))
                    for c in range(6):
                        mm = pe.transpose(g[:, 2 + c // 4, P * (c % 4):P * (c % 4) + P],
                                          pr[:, k % 2, P * c:P * c + P], ident)
                    mm.then_inc(at_tr, 1)
                    if k and k % 2 == 0:
                        at_output(i, k - 1)
                    if k + 2 < 16:
                        at_scores(i, k + 2)
                    pe.wait_ge(at_ptc, i * 16 + (k + 2))
                    pe.wait_ge(at_vtk, i * 5 + (bc + 3))
                    pe.wait_ge(at_o, i * 16 + (k + 2))
                    pe.wait_ge(at_lo, i * 8 + (k // 2 + 1))
                    for c in range(6):
                        v = vtk[:, bc % 2, P * c + 64 * j:P * c + 64 * j + 64] if c < 4 else \
                            vcx[:, P * (c - 4) + 64 * j:P * (c - 4) + 64 * j + 64]
                        mm = pe.matmul(g[:, 4, 64 * j:64 * j + 64], ptr[:, k % 2, P * c:P * c + P], v,
                                       start=(c == 0), stop=(c == 5))
                    mm.then_inc(at_pv, 1)
                at_output(i, 15)
            end_phase(pe, 7)

            with pe.Fori(0, 4) as i:
                for b in range(2):
                    pe_tile(pe, T_W2 + b, i, 2, 4, mh, ml)
            pe_squares(pe, 3, T, sq2)

            def f_up(group, i=None, ready=None):
                for n in range(4):
                    pe_tile(pe, UP[group] + n, i, 12, 2 * F_UNITS, mh, ml, ready if n == 0 else None)

            def f_down(group, i=None):
                pe.wait_ge(f_hl, step(2 * group + 2, i, 4))
                for h in range(2):
                    t0 = DOWN[group] + h
                    pe.wait_ge(w_split, step(t0 + 1, i, 12))
                    for m in range(4):
                        for n in range(2):
                            u = UNIT[t0] + 2 * m + n
                            pe.wait_ge(bank_free[u % 2], step(u // 2 + 1, i, F_UNITS))
                            first, last = pe_unit(pe, t0 % 2, hh[:, group % 2], hl[:, group % 2],
                                                  slice(H * n, H * n + H), range(2),
                                                  [256 * m + P * kt for kt in range(2)], u % 2)
                            if m == 0 and n == 0:
                                first.then_inc(w_begun, 1)
                            last.then_inc(unit_done, 1)

            f_up(0, ready=2 * KT + 1)
            f_up(1)
            f_down(0)
            f_up(2)
            f_down(1)
            with pe.Fori(0, (GROUPS - 3) // 2) as i:
                f_up(3, i)
                f_down(2, i)
                f_up(4, i)
                f_down(3, i)
            f_down(GROUPS - 1)
            pe_squares(pe, 4, T, cb)


def arrays_of(inputs):
    import numpy as np
    f = {k: np.asarray(v) for k, v in inputs.items()}

    def tiles(w):
        k, n = w.shape
        return w.reshape(k // P, P, n // P, P).transpose(2, 1, 0, 3).reshape(n // P, P, k)

    def columns(v):
        return v.reshape(-1, P).T

    def feature_major(x):
        return np.ascontiguousarray(x[0].T.reshape(KT, P, -1).transpose(1, 0, 2))

    w = f["w_in"][0]
    cut = np.cumsum([512, 512, 1024, 1024, 16, 16, 1024, 1024, 1024, 1024])
    q, k, v, za, lrf, lrb, ub, zb, ga, gb = np.split(w, cut[:-1], axis=1)
    lr = np.zeros((D, P), np.float32)
    lr[:, 0:16], lr[:, 32:48] = lrf, lrb
    wp = f["w_pool"][0].reshape(2, 2, 2, P, 256).transpose(0, 3, 1, 2, 4).reshape(2, P, 1024)
    w2 = f["w_in_2"][0]
    q2, k2, v2, sg, cv = np.split(w2, [512, 1024, 1536, 2048], axis=1)
    up, down = tiles(f["ffn_w_up_2"][0]), f["ffn_w_down_2"][0]
    dn = down.reshape(GROUPS, 2, P, 2, 4, P).transpose(0, 3, 2, 4, 1, 5).reshape(GROUPS, 2, P, 1024)
    ff = [up[0:1], up[FT:FT + 1], up[1:2], up[FT + 1:FT + 2]]
    for n in range(GROUPS):
        if n + 1 < GROUPS:
            a = 2 * (n + 1)
            ff += [up[a:a + 1], up[FT + a:FT + a + 1], up[a + 1:a + 2], up[FT + a + 1:FT + a + 2]]
        ff.append(dn[n])
    wall = np.concatenate([tiles(x) for x in (k, v, lr, q, za, ub, zb, ga, gb)] + [wp]
                          + [tiles(f[n][0]) for n in ("w_branch_b", "w_branch_a", "w_out")]
                          + [tiles(x) for x in (cv, sg, k2, v2, q2)] + [tiles(f["w_out_2"][0])] + ff)
    assert wall.shape == (NT, P, 1024), wall.shape

    def rows(m):
        return np.ascontiguousarray(m.T).reshape(-1, P, D)

    cw = f["cv_w_2"][0].reshape(TAPS, 2, P).transpose(2, 1, 0).reshape(P, 2 * TAPS)
    fw = f["ffn_conv_w_2"][0].reshape(3, FT, P).transpose(2, 1, 0).reshape(P, 3 * FT)
    vecs = {"norm_g": f["norm_g"], "b_mod": f["b_mod"], "gla_g": f["gla_norm_g"],
            "pool_scale": f["pool_scale"], "final_g": f["final_norm_g"], "ada_b": f["ada_b_2"],
            "norm1_g": f["norm1_g_2"], "norm2_g": f["norm2_g_2"], "sg_g": f["sg_norm_g_2"],
            "sg_b": f["sg_norm_b_2"], "cv_b": f["cv_b_2"], "cv_g": f["cv_norm_g_2"],
            "cv_nb": f["cv_norm_b_2"], "ff_b": f["ffn_conv_b_2"], "final_g2": f["final_norm_g_2"]}
    cols = np.concatenate([{"cv_w": cw, "ff_w": fw}[n] if n in ("cv_w", "ff_w") else columns(vecs[n])
                           for n, _ in _COLS], axis=1)
    crow = np.stack([f["c"][0], f["c_ctx"], f["c_2"][0], f["c_ctx_2"]])

    mats = np.zeros((P, 7, P), np.float32)
    i = np.arange(P)
    mats[:, 0] = np.eye(P)
    mats[:, 1] = 1 / D
    mats[:, 2] = 1 / DV
    mats[:, 3] = (i[:, None] // 64 == i[None] // 64) / 64.0
    mats[:, 4] = (i[:, None] > i[None]) / GATE_NORM
    mats[:, 5] = (i[:, None] < i[None]) / GATE_NORM
    mats[:, 6] = 1 / GATE_NORM
    nf = DK // 4
    freqs = (np.float32(10000.0) ** (-np.arange(nf, dtype=np.float32) / np.float32(nf))).astype(np.float32)
    t = np.arange(T)
    pos = np.stack([t // GRID_W, t % GRID_W]).astype(np.float32)
    ang = pos[:, None, :] * freqs[None, :, None]
    tabs = np.zeros((P, 2, TA), np.float32)
    tabs[:, 0, T:] = 1
    for half in range(2):
        for part in range(2):
            r = slice(half * 64 + part * 32, half * 64 + part * 32 + 32)
            tabs[r, 0, :T] = np.cos(ang[half])
            tabs[r, 1, :T] = np.sin(ang[half]) * (1 if part else -1)
    tabq = (tabs * np.float32(DK ** -0.5)).astype(np.float32)
    lev = np.zeros((2, 2, 8, P, 64), np.float32)
    hmask = np.zeros((P, LEVELS, P), np.float32)
    for l in range(LEVELS):
        m = 1 << l
        first = i[(i // m) % 2 == 0]
        second = first + m
        r = (first // (2 * m)) * 2 * m + m
        j = i[:, None]
        lev[0, 0, l] = (j > first) & (j < r)
        lev[0, 1, l] = (j >= r) & (j <= second)
        lev[1, 0, l] = (j >= r) & (j < second)
        lev[1, 1, l] = (j >= first) & (j < r)
        same = (i[:, None] // (2 * m)) == (i[None] // (2 * m))
        hmask[:, l] = same & ((i[:, None] // m) != (i[None] // m))
    for half in range(2):
        tok = np.arange(64) + 64 * half
        lev[0, half, 7] = i[:, None] <= tok
        lev[1, half, 7] = i[:, None] >= tok
    lev = (lev / GATE_NORM).transpose(3, 0, 1, 2, 4).reshape(P, 2, 1024).astype(np.float32)
    inv = np.zeros((P, 4, T), np.float32)
    for n, wdw in enumerate(WINDOWS):
        lo, hi = np.clip(t - wdw // 2, 0, T - 1), np.clip(t + (wdw - 1 - wdw // 2), 0, T - 1)
        inv[:, n] = 1.0 / (hi - lo + 1)
    wup = np.zeros((64, 512), np.float32)
    wup[0:16], wup[16] = f["w_gate_up_f"][0], f["b_gate_f"][0]
    wup[32:48], wup[48] = f["w_gate_up_b"][0], f["b_gate_b"][0]
    sgw = f["sg_w_2"][0].transpose(2, 0, 1)
    sgb = np.repeat(f["sg_b_2"][0].reshape(2, 2, 1, P), 64, axis=2).reshape(2, P, P).transpose(1, 0, 2)

    rpb = f["na_rpb_2"][0]
    bias = np.full((2, 4, AH, P, 4 * P), -1e30, np.float32)
    qr, qc = np.arange(8), np.arange(16)
    kr = np.arange(ROWS)
    for br in range(2):
        for bc in range(4):
            qrow, qcol, kcol = br * 8 + qr, bc * 16 + qc, KSPAN[bc] + np.arange(32)
            sr, sc = np.clip(qrow - 4, 0, ROWS - 8), np.clip(qcol - 8, 0, GRID_W - 16)
            inr = (kr[None] >= sr[:, None]) & (kr[None] < sr[:, None] + 8)
            inc = (kcol[None] >= sc[:, None]) & (kcol[None] < sc[:, None] + 16)
            ri = np.clip(kr[None] - qrow[:, None] + 7, 0, 14)
            ci = np.clip(kcol[None] - qcol[:, None] + 15, 0, 30)
            m = inr[:, None, :, None] & inc[None, :, None, :]
            b = rpb[:, ri[:, None, :, None], ci[None, :, None, :]]
            bias[br, bc] = np.where(m, b, np.float32(-1e30)).reshape(AH, P, 4 * P)
    arrays = {
        "modw": np.concatenate([rows(f["w_mod"][0]), rows(f["ada_w_2"][0])]),
        "crow": np.broadcast_to(crow, (P, 4, D)), "cols": cols, "mats": mats, "tabs": tabs, "tabq": tabq,
        "lev": lev, "hmask": hmask, "inv": inv, "sgb": sgb, "xT": feature_major(f["x"]),
        "ctxT": feature_major(f["ctx"]), "ctx2T": feature_major(f["ctx_2"]), "wall": wall, "wup": wup,
        "sgw": sgw, "bias": bias,
    }
    return {k: np.ascontiguousarray(v, dtype=np.float32) for k, v in arrays.items()}


def kernel(**inputs):
    import numpy as np
    import concourse.bacc as bacc
    from concourse.bass_utils import run_bass_kernel_spmd

    nc = bacc.Bacc("TRN2", target_bir_lowering=False, num_devices=1)
    arrays = arrays_of(inputs)
    args = [nc.dram_tensor(f"in_{n}", a.shape, F32, kind="ExternalInput").ap() for n, a in arrays.items()]
    args.append(nc.dram_tensor("out_T", (P, KT, T), F32, kind="ExternalOutput").ap())
    build(nc, *args)
    r = run_bass_kernel_spmd(nc, [{f"in_{n}": a for n, a in arrays.items()}], core_ids=[0])
    y = r.results[0]["out_T"]
    return np.ascontiguousarray(y.transpose(2, 1, 0)).reshape(1, T, D)
```

```python
from contextlib import ExitStack

import concourse.bass as bass
from concourse import mybir

F32 = mybir.dt.float32
F32R = mybir.dt.float32r
I32 = mybir.dt.int32
ACT = mybir.ActivationFunctionType
ALU = mybir.AluOpType

P = 128
D = 1024
KT = D // P
T = 1024
C = 256
TA = T + C
H = 512
EPS = 1e-6
HEADS, DK, DV = 4, 128, 256
CH = 128
NC = TA // CH
NCX = T // CH
LEVELS = 7
GATE_NORM = 16.0
WINDOWS = (2, 4, 8, 16)
PAD = 8
FF = 2816
FT = FF // P
GROUPS = FT // 2
TAPS = 31
GRID_W, ROWS = 64, 16
AH = 8
KSPAN = (0, 8, 24, 32)

T_K, T_V, T_LR, T_Q = 0, 4, 12, 13
T_ZA, T_UB, T_ZB, T_GA, T_GB = 17, 25, 33, 41, 49
T_POOL, T_B, T_A, T_OUT = 57, 59, 67, 75
T_CV, T_SG, T_K2, T_V2, T_Q2, T_W2 = 83, 87, 91, 95, 99, 103
T_FF = 111
NT = T_FF + 6 * GROUPS


def _first_units():
    count, first = 0, []
    for t in range(NT):
        first.append(count)
        if t < T_Q or T_K2 <= t < T_Q2:
            count += 3
        elif T_POOL <= t < T_B:
            count += 8
        elif t >= T_FF + 4 and (t - T_FF - 4) % 6 >= 4 or t >= NT - 2:
            count += 8
        else:
            count += 2
    return first + [count]


UNIT = _first_units()

_COLS = [("norm_g", 8), ("b_mod", 24), ("gla_g", 2), ("pool_scale", 8), ("final_g", 8),
         ("ada_b", 48), ("norm1_g", 8), ("norm2_g", 8), ("sg_g", 2), ("sg_b", 2), ("cv_w", 2 * TAPS),
         ("cv_b", 2), ("cv_g", 2), ("cv_nb", 2), ("ff_w", 3 * FT), ("ff_b", FT), ("final_g2", 8)]
COL = {}
_at = 0
for _name, _n in _COLS:
    COL[_name] = _at
    _at += _n
NCOL = _at


def build(nc, modw, crow, cols, mats, tabs, tabq, lev, hmask, inv, sgb, xT, ctxT, ctx2T, wall, wup, sgw, bias,
          out):
    ctx = ExitStack()
    with ctx:
        def sem(name):
            return ctx.enter_context(nc.semaphore(name))

        def dram(name, shape, dt=F32):
            return nc.dram_tensor(name, shape, dt, kind="Internal").ap()

        place = {"next": (nc.sbuf_base + 63) // 64 * 64}

        def at(name, shape, offset, dt=F32):
            n = 4
            for s in shape[1:]:
                n *= s
            n = (n + 31) // 32 * 32
            assert offset % 32 == 0 and offset + n <= nc.sbuf_usable_end, (name, offset + n)
            return nc.alloc_sbuf_tensor_at(name, shape, dt, offset=offset), offset + n

        def keep(name, shape, dt=F32):
            t, place["next"] = at(name, shape, place["next"], dt)
            return t

        w_raw = keep("w_raw", [P, 2, 1024])
        w_hi = keep("w_hi", [P, 2, 1024], F32R)
        w_lo = keep("w_lo", [P, 2, 1024], F32R)
        col = keep("col", [P, NCOL])
        modx = keep("modx", [P, 72])
        modc = keep("modc", [P, 72])
        gain = keep("gain", [P, 2, KT])
        mat = keep("mat", [P, 7, P])
        mod_sum = keep("mod_sum", [P, 2, 4])
        one = keep("one", [P, 1])
        tick = keep("tick", [P, 1])
        epsc = keep("epsc", [P, 1])
        dec = keep("dec", [P, NC, 8])
        ident, mean_d, mean_v, mean_g = (mat[:, n, :] for n in range(4))
        arena = place["next"]

        pb = [ctx.enter_context(nc.psum_tensor(f"pb{i}", [P, H], F32)) for i in range(2)]
        g = ctx.enter_context(nc.psum_tensor("g", [P, 6, H], F32))

        proj_d = dram("proj_d", [T_POOL, P, TA])

        w_in = [sem("w_in0"), sem("w_in1")]
        one_ready = sem("one_ready")
        w_high = sem("w_high")
        w_split = sem("w_split")
        w_begun = sem("w_begun")
        unit_done = sem("unit_done")
        bank_free = [sem("bank_free0"), sem("bank_free1")]
        sq_ready = sem("sq_ready")
        sq_used = sem("sq_used")
        std_ready = sem("std_ready")
        rstd_ready = sem("rstd_ready")
        t_ready = sem("t_ready")
        h_ready = sem("h_ready")
        xh_ready = sem("xh_ready")
        xl_ready = sem("xl_ready")
        const_in = sem("const_in")
        cond_in = sem("cond_in")
        cond2_in = sem("cond2_in")
        cond_ready = sem("cond_ready")
        x_in = sem("x_in")
        mod_in = [sem(f"mod_in{i}") for i in range(4)]
        mod_ctx = sem("mod_ctx")
        mod_free = sem("mod_free")
        mod_kept = sem("mod_kept")
        gain_ready = sem("gain_ready")
        store_done = [sem("store_done0"), sem("store_done1")]
        phase = sem("phase")

        xh, a = at("xh", [P, KT, TA], arena, F32R)
        xl, a = at("xl", [P, KT, TA], a, F32R)
        after_operand = a
        xin, a = at("xin", [P, KT, TA], after_operand)
        rstd, a = at("rstd", [P, TA], a)
        squares, a = at("squares", [P, 2, TA], a)
        crow_sb, a = at("crow_sb", [P, 4, 1024], a)
        mod_raw, a = at("mod_raw", [P, 4, 1024], a)
        prod, a = at("prod", [P, 1024], a)
        stage, _ = at("stage", [P, 2, TA], after_operand)

        kr_d = dram("kr_d", [NC, P, H])
        la_d = dram("la_d", [NC, 2, P, 1024])
        kt_d = dram("kt_d", [NC, P, 1024])
        vt_d = dram("vt_d", [NC, P, 1024])
        sb_d = dram("sb_d", [NC, P, 1024])
        tab, a = at("tab", [P, 2, TA], after_operand + 8 * TA)
        matr, a = at("matr", [P, 3, P], a, F32R)
        wup_sb, a = at("wup_sb", [64, H], a)
        gla_buffers = a
        kc, a = at("kc", [P, 2, HEADS, CH], gla_buffers)
        ks, a = at("ks", [P, 2, HEADS, CH], a)
        vc, a = at("vc", [P, 2, 8, CH], a)
        lrc, a = at("lrc", [64, 2, CH], a)
        kr, a = at("kr", [P, 2, HEADS, CH], a)
        rot, a = at("rot", [P, HEADS, CH], a)
        soft, a = at("soft", [P, 2, H], a)
        la, a = at("la", [P, 2, H], a)
        lah, a = at("lah", [P, 2, 2, H], a, F32R)
        lal, a = at("lal", [P, 2, 2, H], a, F32R)
        ef, a = at("ef", [P, 2, H], a)
        kt, a = at("kt", [P, 2, 2, H], a)
        vt, a = at("vt", [P, 2, 1024], a)
        skb, a = at("skb", [P, 2, H], gla_buffers)
        svt, a = at("svt", [P, 2, 1024], a)
        stb, a = at("stb", [P, 2, HEADS, DV], a)
        stf_at = arena + 169 * 1024
        stf, _ = at("stf", [P, 2, HEADS, DV], stf_at)
        tabf, b = at("tabf", [P, 2, T], arena)
        levr, b = at("levr", [P, 2, 1024], b, F32R)
        mask, b = at("mask", [P, LEVELS, P], b)
        levf_at = b
        levf, _ = at("levf", [P, 2, 1024], levf_at)
        _, b = at("qi_end", [P, 2, 1024], levf_at)
        gla_arena = arena + 33 * 1024
        up, b = at("up", [P, 2, H + 2 * PAD], b)
        assert b <= gla_arena
        oall, a = at("oall", [P, 8, T], gla_arena)
        fk, a = at("fk", [P, 2, HEADS, CH], a)
        fq, a = at("fq", [P, 2, HEADS, CH], a)
        fs, a = at("fs", [P, 2, HEADS, CH], a)
        fla, a = at("fla", [P, 2, 2, 2, H], a, F32R)
        fkt, a = at("fkt", [P, 2, H], a)
        fvt, a = at("fvt", [P, 2, 1024], a)
        fsb, a = at("fsb", [P, 2, HEADS, DV], a)
        ex, a = at("ex", [P, 2, HEADS, H], a)
        lk, a = at("lk", [P, LEVELS, HEADS, CH], a)
        lq, a = at("lq", [P, LEVELS, HEADS, CH], a)
        qi, _ = at("qi", [P, 2, 2, HEADS, CH], levf_at)
        pt, a = at("pt", [P, HEADS, CH], a)
        frot, a = at("frot", [P, HEADS, CH], a)
        sums, a = at("sums", [P, 2, H + 2 * PAD], a)
        inv_sb, a = at("inv_sb", [P, H], a)
        assert a <= stf_at
        d_d = dram("d_d", [8, P, T])
        u_in = [sem("u_in0"), sem("u_in1")]
        u_s = sem("u_s")
        u_d = sem("u_d")
        u_out = [sem("u_out0"), sem("u_out1")]
        tab_in = sem("tab_in")
        tab_ready = sem("tab_ready")
        p_in = [sem("p_in0"), sem("p_in1")]
        p_out = [sem("p_out0"), sem("p_out1")]
        p_dve = sem("p_dve")
        p_kr = sem("p_kr")
        p_gk = sem("p_gk")
        p_act = sem("p_act")
        p_ln = sem("p_ln")
        p_la = sem("p_la")
        p_lah = sem("p_lah")
        p_lal = sem("p_lal")
        p_vtr = sem("p_vtr")
        p_vt = sem("p_vt")
        p_ktr = sem("p_ktr")
        p_arg = sem("p_arg")
        p_exp = sem("p_exp")
        p_kt = sem("p_kt")
        s_in = [sem("s_in0"), sem("s_in1")]
        s_out = [sem("s_out0"), sem("s_out1")]
        s_mm = sem("s_mm")
        s_upd = sem("s_upd")
        f_in = [sem("f_in0"), sem("f_in1")]
        f_rot = sem("f_rot")
        f_qr = sem("f_qr")
        f_arg = sem("f_arg")
        f_exp = sem("f_exp")
        f_mul = sem("f_mul")
        f_lev = sem("f_lev")
        f_diag = sem("f_diag")
        f_pred = sem("f_pred")
        f_omm = sem("f_omm")
        f_oev = sem("f_oev")
        f_smm = sem("f_smm")
        f_upd = sem("f_upd")

        ah, a = at("ah", [P, 8, T], arena, F32R)
        qd, _ = at("qd", [P, 8, T], arena)
        zal, _ = at("zal", [P, 8, T], arena)
        _, a = at("oall_end", [P, 8, T], gla_arena)
        al, _ = at("al", [P, 8, T], gla_arena, F32R)
        bh, a = at("bh", [P, 8, T], a, F32R)
        bl, a = at("bl", [P, 8, T], a, F32R)
        mix, _ = at("mix", [P, 8, T], a)
        dh, a = at("dh", [P, 2, 2, T], a, F32R)
        dl, a = at("dl", [P, 2, 2, T], a, F32R)
        osq_at = a
        zb, _ = at("zb", [P, 2, T], osq_at)
        osq, a = at("osq", [P, 2, T], a)
        yb, _ = at("yb", [P, 2, H], a)
        orstd, a = at("orstd", [P, T], a)
        ga, _ = at("ga", [P, 2, T], osq_at)
        sq1, _ = at("sq1", [P, 2, T], osq_at)
        xp_d = dram("xp_d", [KT, P, T])
        q_in = [sem(f"q_in{i}") for i in range(4)]
        q_z = [sem("q_z0"), sem("q_z1")]
        q_dh = sem("q_dh")
        q_dl = sem("q_dl")
        q_sil = sem("q_sil")
        q_y = sem("q_y")
        q_yh = sem("q_yh")
        q_yl = sem("q_yl")
        b_in = sem("b_in")
        b_sg = sem("b_sg")
        o_in = sem("o_in")
        o_sq = sem("o_sq")
        o_st = sem("o_st")
        o_std = sem("o_std")
        o_rec = sem("o_rec")
        o_t = sem("o_t")
        o_sil = sem("o_sil")
        o_n = sem("o_n")
        o_h = sem("o_h")
        o_l = sem("o_l")
        a_in = [sem("a_in0"), sem("a_in1")]
        a_sg = sem("a_sg")
        a_m = sem("a_m")
        a_mh = sem("a_mh")
        a_ml = sem("a_ml")
        r_in = sem("r_in")
        n1_x = sem("n1_x")
        xp_out = sem("xp_out")
        ctx2_in = sem("ctx2_in")

        KB = 1024
        mh, a = at("mh", [P, 8, T], arena, F32R)
        ml, a = at("ml", [P, 8, T], a, F32R)
        assert a <= after_operand
        zcs, a = at("zcs", [P, 8, T], after_operand)
        vsq, _ = at("vsq", [P, 2, T], a)
        vroot, _ = at("vroot", [P, T], a)
        vtok, _ = at("vtok", [P, NCX, 256], a)
        sgw_sb, b = at("sgw_sb", [P, 4, P], after_operand + 3 * 4 * T)
        sgb_sb, _ = at("sgb_sb", [P, 2, P], b)
        hpad, a = at("hpad", [P, 2, T + TAPS - 1], a)
        zkv, a = at("zkv", [P, 8, TA], a)
        zq, a = at("zq", [P, 4, T], a)
        at_bias, a = at("at_bias", [P, 4, H], arena + 64 * KB)
        sl, a = at("sl", [P, 2, H], a)
        pr, a = at("pr", [P, 2, H + C], a)
        ptr, a = at("ptr", [P, 2, H + C], a)
        ks2, a = at("ks2", [P, TA], a)
        vs2, a = at("vs2", [P, 4 * H + C], a)
        qs2, a = at("qs2", [P, T], a)
        vtk, a = at("vtk", [P, 2, H], a)
        vcx, a = at("vcx", [P, C], a)
        osb, a = at("osb", [P, 2, P], a)
        tiny, a = at("tiny", [P, 2, 8], a)
        assert a <= after_operand + 40 * KB
        x2, a = at("x2", [P, KT, T], arena + 64 * KB)
        sq2, a = at("sq2", [P, 2, T], a)
        root2, a = at("root2", [P, T], a)
        xw, a = at("xw", [P, KT, T], a)
        hh, a = at("hh", [P, 2, 2, T], a, F32R)
        hl, a = at("hl", [P, 2, 2, T], a, F32R)
        gp, a = at("gp", [P, 2, T + 2], arena + 96 * KB)
        cb, a = at("cb", [P, 2, T], a)
        sgm, a = at("sgm", [P, 2, T], a)
        z_h = sem("z_h")
        z_cv = sem("z_cv")
        z_pe = sem("z_pe")
        z_act = sem("z_act")
        z_dve = sem("z_dve")
        y_pe = sem("y_pe")
        y_act = sem("y_act")
        y_dve = sem("y_dve")
        sg_in = sem("sg_in")
        bias_in = [sem(f"bias_in{i}") for i in range(4)]
        at_stq = sem("at_stq")
        at_stk = sem("at_stk")
        at_stv = sem("at_stv")
        at_vt = sem("at_vt")
        at_vtk = sem("at_vtk")
        at_s = sem("at_s")
        at_sc = sem("at_sc")
        at_m = sem("at_m")
        at_nm = sem("at_nm")
        at_ex = sem("at_ex")
        at_sum = sem("at_sum")
        at_r = sem("at_r")
        at_tr = sem("at_tr")
        at_ptc = sem("at_ptc")
        at_pv = sem("at_pv")
        at_o = sem("at_o")
        at_ot = sem("at_ot")
        at_hi = sem("at_hi")
        at_lo = sem("at_lo")
        x2_in = sem("x2_in")
        f_pad = sem("f_pad")
        f_cv = sem("f_cv")
        f_sil = sem("f_sil")
        f_hid = sem("f_hid")
        f_hh = sem("f_hh")
        f_hl = sem("f_hl")
        f_fin = sem("f_fin")
        out_done = sem("out_done")

        block = ctx.enter_context(nc.Block())

        def end_phase(eng, n):
            eng.drain().then_inc(phase, 1)
            eng.wait_ge(phase, 3 * n)

        def step(base, i, by):
            return base if i is None else i * by + base


        def pe_unit(pe, b, xhi, xlo, tokens, kts, wcols, bank, ready=None):
            n = tokens.stop - tokens.start
            total, count = 3 * len(kts), 0
            first = None
            for k, wc in zip(kts, wcols):
                if ready is not None:
                    pe.wait_ge(xh_ready, ready + k)
                    pe.wait_ge(xl_ready, ready + k)
                for w, x in ((w_hi, xhi), (w_lo, xhi), (w_hi, xlo)):
                    mm = pe.matmul(pb[bank][:, 0:n], w[:, b, wc:wc + P], x[:, k, tokens],
                                   start=(count == 0), stop=(count == total - 1))
                    first = first or mm
                    count += 1
            return first, mm

        def pe_tile(pe, t0, i=None, tiles=0, units=0, xhi=None, xlo=None, ready=None):
            b, u0 = t0 % 2, UNIT[t0]
            xhi, xlo = xhi or xh, xlo or xl
            pe.wait_ge(w_split, step(t0 + 1, i, tiles))
            for n in range(UNIT[t0 + 1] - u0):
                bank = (u0 + n) % 2
                pe.wait_ge(bank_free[bank], step((u0 + n) // 2 + 1, i, units // 2))
                tokens = slice(n * H, min(n * H + H, TA))
                first, last = pe_unit(pe, b, xhi, xlo, tokens, range(KT), range(0, 1024, P), bank,
                                      ready if n == 0 else None)
                if n == 0:
                    first.then_inc(w_begun, 1)
                last.then_inc(unit_done, 1)

        def act_squares(act, n, tokens, src, sq, wait=None):
            with act.Fori(0, KT // 2) as i:
                for b in range(2):
                    if wait is not None:
                        wait(i, b)
                    act.wait_ge(sq_used, i * 2 + (KT * n + b + 1))
                    act.activation(sq[:, b, 0:tokens], src[:, i * 2 + b, 0:tokens],
                                   ACT.Square).then_inc(sq_ready, 1)

        def pe_squares(pe, n, tokens, sq):
            for k in range(KT):
                pe.wait_ge(sq_ready, KT * n + k + 1)
                for u in range(0, tokens, H):
                    w = min(H, tokens - u)
                    mm = pe.matmul(g[:, u // H, 0:w], mean_d, sq[:, k % 2, u:u + w],
                                   start=(k == 0), stop=(k == KT - 1))
                mm.then_inc(sq_used, 1)

        def act_roots(act, n, tokens, root):
            act.wait_ge(sq_used, 2 + KT * (n + 1))
            for u in range(0, tokens, H):
                w = min(H, tokens - u)
                r = act.activation(root[:, u:u + w], g[:, u // H, 0:w], ACT.Sqrt, bias=epsc[:, 0:1])
            r.then_inc(std_ready, 1)

        UP = [T_FF if n == 0 else T_FF + 4 + 6 * (n - 1) for n in range(GROUPS)]
        DOWN = [T_FF + 8 + 6 * n if n < GROUPS - 1 else NT - 2 for n in range(GROUPS)]
        DOWN_END = [UNIT[t + 2] for t in DOWN]
        DOWN_LAST = UNIT[DOWN[-1]]
        F_UNITS = UNIT[UP[3]] - UNIT[UP[2]]
        gp_root = sq2[:, 0, :]
        out_tiles = out.rearrange("p t n -> t p n")

        def at_tokens(br, bc):
            return lambda x: x.rearrange("p (r c) -> p r c", c=GRID_W)[:, 8 * br:8 * br + 8,
                                                                      16 * bc:16 * bc + 16]

        def step_of(k):
            return k // 4, k // 2 % 2, k % 2

        def rows_of(t0, n):
            return proj_d[t0:t0 + n].rearrange("t p (c n) -> p t c n", n=CH)

        def load_swapped(eng, dst, src, sem):
            for quad in range(4):
                eng.dma_start(dst[32 * quad:32 * quad + 32], src[32 * (quad ^ 1):32 * (quad ^ 1) + 32])\
                   .then_inc(sem, 16)

        @block.sync
        def _(sp):
            sp.dma_start(crow_sb[:, 0:2, :], crow[:, 0:2, :]).then_inc(cond_in, 16)
            for j in range(4):
                sp.dma_start(mod_raw[:, j, :], modw[j]).then_inc(mod_in[j], 16)
            sp.dma_start(xin[:, 0:4, 0:T], xT[:, 0:4, :]).then_inc(x_in, 16)
            for j in range(4):
                sp.wait_ge(mod_free, j + 2)
                sp.dma_start(mod_raw[:, j, :], modw[4 + j]).then_inc(mod_in[j], 16)
            sp.dma_start(xin[:, 4:8, 0:T], xT[:, 4:8, :]).then_inc(x_in, 16)
            sp.dma_start(xin[:, :, T:TA], ctxT).then_inc(x_in, 16)
            sp.dma_start(mat[:, :, :], mats).then_inc(const_in, 16)
            sp.dma_start(col[:, :], cols).then_inc(const_in, 16)
            for b in range(2):
                sp.dma_start(w_raw[:, b, :], wall[b]).then_inc(w_in[b], 16)
            modw4 = modw.rearrange("(i j) p n -> i j p n", j=4)
            wall2 = wall[0:NT - 1].rearrange("(i j) p n -> i j p n", j=2)
            with sp.Fori(2, 4) as i:
                for j in range(4):
                    sp.wait_ge(mod_free, i * 4 + (j - 2))
                    sp.dma_start(mod_raw[:, j, :], modw4[i, j]).then_inc(mod_in[j], 16)
            sp.dma_start(crow_sb[:, 2:4, :], crow[:, 2:4, :]).then_inc(cond2_in, 16)
            with sp.Fori(1, 8) as i:
                for b in range(2):
                    sp.wait_ge(w_split, i * 2 + (b - 1))
                    sp.dma_start(w_raw[:, b, :], wall2[i, b]).then_inc(w_in[b], 16)
                    for j in range(4):
                        sp.wait_ge(mod_free, i * 8 + (4 * b + j + 6))
                        sp.dma_start(mod_raw[:, j, :], modw4[i * 2 + (b + 2), j]).then_inc(mod_in[j], 16)

            def weights(first, last):
                with sp.Fori(first, last) as i:
                    for b in range(2):
                        sp.wait_ge(w_split, i * 2 + (b - 1))
                        sp.dma_start(w_raw[:, b, :], wall2[i, b]).then_inc(w_in[b], 16)

            weights(8, T_POOL // 2 + 1)

            def f_load(c, b):
                sp.dma_start(fk[:, b].rearrange("p h n -> p (h n)"), kr_d[c]).then_inc(f_in[b], 16)
                sp.dma_start(fq[:, b], rows_of(T_Q, 4)[:, :, c, :]).then_inc(f_in[b], 16)
                load_swapped(sp, fs[:, b], rows_of(T_Q, 4)[:, :, c, :], f_in[b])
                sp.dma_start(fla[:, b].bitcast(F32).rearrange("p a d n -> p a (d n)"),
                             la_d[c].rearrange("a p n -> p a n")).then_inc(f_in[b], 16)
                sp.dma_start(fkt[:, b, :], kt_d[c][:, 0:H]).then_inc(f_in[b], 16)
                sp.dma_start(fvt[:, b, :], vt_d[c]).then_inc(f_in[b], 16)
                sp.dma_start(fsb[:, b].rearrange("p h n -> p (h n)"), sb_d[c]).then_inc(f_in[b], 16)

            def f_next(i, b):
                sp.wait_ge(f_smm, i * 2 + (b + 1))
                f_load(i * 2 + (b + 1), 1 - b)

            inv4 = inv.rearrange("p i (h n) -> i h p n", h=2)

            def u_tile(i, b):
                for half in range(2):
                    first = H * half - PAD * half
                    sp.wait_ge(u_out[half], i * 32 + (16 * b + 16))
                    sp.dma_start(up[:, half, PAD * (1 - half):PAD * (1 - half) + H + PAD],
                                 ub_d[i, b][:, first:first + H + PAD]).then_inc(u_in[half], 16)
                    sp.wait_ge(u_d, i * 4 + (2 * b + half + 1))
                    sp.dma_start(inv_sb[:, :], inv4[i, half]).then_inc(u_in[half], 16)
                    sp.wait_ge(u_d, i * 4 + (2 * b + half + 2))
                    sp.dma_start(dd[i, b][:, H * half:H * half + H], up[:, half, PAD:PAD + H])\
                      .then_inc(u_out[half], 16)

            ub_d = proj_d[T_UB:T_UB + 8].rearrange("(i j) p n -> i j p n", j=2)
            dd = d_d.rearrange("(i j) p n -> i j p n", j=2)
            for half in range(2):
                sp.sem_inc(u_out[half], 16)
            sp.wait_ge(phase, 9)
            f_load(0, 0)
            with sp.Fori(0, NCX // 2 - 1) as i:
                for b in range(2):
                    f_next(i, b)
                    u_tile(i, b)
            f_next(NCX // 2 - 1, 0)
            for b in range(2):
                u_tile(NCX // 2 - 1, b)
            weights(T_POOL // 2 + 1, T_W2 // 2 + 1)
            sp.wait_ge(phase, 18)
            bias6 = bias.rearrange("r c (i j) q k -> r c i j q k", j=2)
            with sp.Fori(0, AH // 2) as i:
                for k in range(16):
                    bc, br, j = step_of(k)
                    sp.wait_ge(at_sc, i * 16 + (k + 1))
                    sp.dma_start(at_bias[:, k % 4, :], bias6[br, bc, i, j]).then_inc(bias_in[k % 4], 16)
            weights(T_W2 // 2 + 1, NT // 2)
            sp.wait_ge(w_split, NT - 2)
            sp.dma_start(w_raw[:, 0, :], wall[NT - 1]).then_inc(w_in[0], 16)

        @block.gpsimd
        def _(pool):
            def split(b, high, raw):
                pool.wait_ge(w_in[b], raw)
                nc.gpsimd.tensor_tensor(w_hi[:, b, :], w_raw[:, b, :], one[:, 0:1].to_broadcast([P, 1024]),
                                        ALU.mult).then_inc(w_high, 1)
                pool.wait_ge(w_high, high)
                nc.gpsimd.tensor_tensor(w_lo[:, b, :], w_raw[:, b, :], w_hi[:, b, :],
                                        ALU.subtract).then_inc(w_split, 1)

            nc.gpsimd.memset(one[:, :], 1.0).then_inc(one_ready, 1)
            pool.wait_ge(one_ready, 1)
            for b in range(2):
                split(b, b + 1, 16)
            pool.sem_inc(u_d, 1)

            def split_pairs(first, last):
                with pool.Fori(first, last) as i:
                    for b in range(2):
                        pool.wait_ge(w_begun, i * 2 + b)
                        split(b, i * 2 + (b + 1), i * 16 + 16)

            split_pairs(1, T_POOL // 2 + 1)

            pool.wait_ge(phase, 9)
            nc.gpsimd.memset(up[:, 0, 0:PAD], 0.0).then_inc(u_s, 1)
            nc.gpsimd.memset(up[:, 1, PAD + H:PAD + H + PAD], 0.0).then_inc(u_s, 1)
            pool.wait_ge(u_s, 2)
            steps = 2
            for grp in range(4):
                each = grp + 2
                with pool.Fori(0, 2) as j:
                    for half in range(2):
                        u, lo, hi, cur = up[:, half, :], 1, H + 2 * PAD, 0
                        at = [steps + each * half]

                        def chained(instruction):
                            at[0] += 1
                            instruction.then_inc(u_s, 1)
                            pool.wait_ge(u_s, j * (2 * each) + at[0])

                        pool.wait_ge(u_in[half], j * 32 + (64 * grp + 32))
                        pool.wait_ge(u_d, j * 2 + (4 * grp + half + 1))
                        chained(nc.gpsimd.tensor_tensor(sums[:, 0, lo:hi], u[:, lo - 1:hi - 1], u[:, lo:hi],
                                                        ALU.add))
                        for w in WINDOWS[:grp]:
                            k = w // 2
                            lo, hi = lo + k, hi - k
                            chained(nc.gpsimd.tensor_tensor(sums[:, 1 - cur, lo:hi], sums[:, cur, lo - k:hi - k],
                                                            sums[:, cur, lo + k:hi + k], ALU.add))
                            cur = 1 - cur
                        mid = slice(PAD, PAD + H)
                        chained(nc.gpsimd.tensor_tensor(sums[:, 1 - cur, mid], sums[:, cur, mid], inv_sb[:, :],
                                                        ALU.mult))
                        nc.gpsimd.tensor_tensor(u[:, mid], sums[:, 1 - cur, mid], u[:, mid], ALU.subtract)\
                          .then_inc(u_d, 1)
                steps += 4 * each
            split_pairs(T_POOL // 2 + 1, NT // 2)
            pool.wait_ge(w_begun, NT - 1)
            split(0, NT, 16 * (NT // 2 + 1))

        @block.scalar
        def _(act):
            act.sem_inc(sq_used, 2)
            for b in range(2):
                act.sem_inc(store_done[b], 16)

            def operand_tiles(n, tokens, m0, work, high):
                with act.Fori(0, KT) as k:
                    act.wait_ge(t_ready, k + (KT * n + 1))
                    m = act.activation(work[:, k, 0:T], work[:, k, 0:T], ACT.Identity,
                                       scale=gain[:, 0, bass.ds(k, 1)],
                                       bias=modx[:, bass.ds(k + m0, 1)])
                    if tokens > T:
                        m = act.activation(work[:, k, T:TA], work[:, k, T:TA], ACT.Identity,
                                           scale=gain[:, 1, bass.ds(k, 1)],
                                           bias=modc[:, bass.ds(k + m0, 1)])
                    m.then_inc(h_ready, 1)
                    act.wait_ge(h_ready, k + (KT * n + 1))
                    act.activation(high[:, k, 0:tokens], work[:, k, 0:tokens], ACT.Copy)\
                       .then_inc(xh_ready, 1)

            act.wait_ge(cond_in, 16)
            act.activation(crow_sb[:, 0:2, :], crow_sb[:, 0:2, :], ACT.Silu).then_inc(cond_ready, 1)
            act.wait_ge(x_in, 48)
            act_squares(act, 0, TA, xin, squares)
            act.wait_ge(gain_ready, 1)
            act_roots(act, 0, TA, rstd)
            act.wait_ge(gain_ready, 5)
            operand_tiles(0, TA, 0, xin, xh)
            act.wait_ge(cond2_in, 16)
            act.activation(crow_sb[:, 2:4, :], crow_sb[:, 2:4, :], ACT.Silu).then_inc(cond_ready, 1)

            def store_tile(t0, dst, i=None, tiles=0, units=0):
                b, u0, nu = t0 % 2, UNIT[t0], UNIT[t0 + 1] - UNIT[t0]
                act.wait_ge(store_done[b], step(16 * (t0 // 2 + 1), i, 8 * tiles))
                for n in range(nu):
                    u, w = u0 + n, min(H, TA - n * H)
                    act.wait_ge(unit_done, step(u + 1, i, units))
                    act.activation(stage[:, b, n * H:n * H + w], pb[u % 2][:, 0:w], ACT.Copy)\
                       .then_inc(bank_free[u % 2], 1)
                for u in (u0 + nu - 2, u0 + nu - 1):
                    act.wait_ge(bank_free[u % 2], step(u // 2 + 2, i, units // 2))
                act.dma_start(dst[:, 0:min(nu * H, TA)], stage[:, b, 0:min(nu * H, TA)])\
                   .then_inc(store_done[b], 16)

            kv_d = proj_d[0:T_LR].rearrange("(i j) p n -> i j p n", j=2)
            q_d2 = proj_d[T_Q:T_ZA].rearrange("(i j) p n -> i j p n", j=2)
            act.wait_ge(xl_ready, KT)
            with act.Fori(0, T_LR // 2) as i:
                for b in range(2):
                    store_tile(b, kv_d[i, b], i, 2, 6)
            store_tile(T_LR, proj_d[T_LR])
            with act.Fori(0, (T_ZA - T_Q) // 2) as i:
                for b in range(2):
                    store_tile(T_Q + b, q_d2[i, b], i, 2, 4)

            for b in range(2):
                act.wait_ge(store_done[b], 16 * ((T_ZA - b + 1) // 2 + 1))
            end_phase(act, 1)
            act.dma_start(tab[:, :, :], tabs).then_inc(tab_in, 16)
            act.dma_start(wup_sb[:, :], wup).then_inc(tab_in, 16)
            for q in p_out:
                act.sem_inc(q, 80)
            for q, n in ((o_std, 1), (o_n, 1), (a_m, 2), (p_vt, 1), (p_exp, 1), (p_kt, 1), (s_upd, 1), (s_mm, 1), (s_out[0], 16), (s_out[1], 16),
                         (f_exp, 4), (f_mul, 2), (f_pred, 7), (f_omm, 1), (f_oev, 1), (f_smm, 1),
                         (f_upd, 1)):
                act.sem_inc(q, n)
            act.wait_ge(tab_ready, 2)

            def p_load(c, b):
                act.dma_start(kc[:, b], rows_of(T_K, 4)[:, :, c, :]).then_inc(p_in[b], 16)
                load_swapped(act, ks[:, b], rows_of(T_K, 4)[:, :, c, :], p_in[b])
                act.dma_start(vc[:, b], rows_of(T_V, 8)[:, :, c, :]).then_inc(p_in[b], 16)
                for r in (0, 32):
                    act.dma_start(lrc[r:r + 16, b], rows_of(T_LR, 1)[r:r + 16, 0, c, :])\
                       .then_inc(p_in[b], 16)

            in_p = proj_d[T_ZA:T_ZA + 3 * NC].rearrange("(i j) p n -> i j p n", j=6)
            in_s = proj_d[T_ZA + 3 * NC:T_POOL].rearrange("(i j) p n -> i j p n", j=2)

            def p_tile(i, n):
                store_tile(T_ZA + n, in_p[i, n], i, 6, 12)

            def p_chunk(i, b, more):
                c = i * 2 + b
                if more:
                    act.wait_ge(p_kt, c + 1)
                    p_load(i * 2 + (b + 1), 1 - b)
                p_tile(i, 3 * b)
                act.wait_ge(p_gk, c + 1)
                act.activation(soft[:, :, :], g[:, 0:2, :], ACT.Abs).then_inc(p_act, 1)
                act.wait_ge(p_act, i * 4 + (2 * b + 1))
                act.activation(soft[:, :, :], soft[:, :, :], ACT.Exp, scale=-1.0).then_inc(p_act, 1)
                act.wait_ge(p_act, i * 4 + (2 * b + 2))
                act.activation(soft[:, :, :], soft[:, :, :], ACT.Ln, bias=1.0).then_inc(p_ln, 1)
                act.wait_ge(p_out[b], i * 80 + 80)
                act.wait_ge(p_vtr, c + 1)
                act.activation(vt[:, b, :].rearrange("p (a n) -> p a n", a=2), g[:, 3:5, :], ACT.Copy)\
                   .then_inc(p_vt, 1)
                act.wait_ge(p_la, c + 1)
                act.activation(lah[:, b], la[:, :, :], ACT.Copy).then_inc(p_lah, 1)
                p_tile(i, 3 * b + 1)
                act.wait_ge(p_arg, c + 1)
                act.wait_ge(p_kt, c + 1)
                act.activation(ef[:, :, :], g[:, 0:2, :], ACT.Exp)
                act.activation(dec[:, c, :], g[:, 5, 0:16].rearrange("p (a n) -> p a n", n=2)[:, :, 0],
                               ACT.Exp).then_inc(p_exp, 1)
                act.wait_ge(p_kr, c + 1)
                act.dma_start(kr_d[c], kr[:, b].rearrange("p h n -> p (h n)")).then_inc(p_out[b], 16)
                act.wait_ge(p_lal, c + 1)
                act.wait_ge(p_lah, c + 1)
                act.dma_start(la_d[c, 0], lah[:, b].bitcast(F32).rearrange("p h n -> p (h n)")).then_inc(p_out[b], 16)
                act.dma_start(la_d[c, 1], lal[:, b].bitcast(F32).rearrange("p h n -> p (h n)")).then_inc(p_out[b], 16)
                act.wait_ge(p_vt, c + 2)
                act.dma_start(vt_d[c], vt[:, b, :]).then_inc(p_out[b], 16)
                act.wait_ge(p_kt, c + 2)
                act.dma_start(kt_d[c], kt[:, b].rearrange("p h n -> p (h n)")).then_inc(p_out[b], 16)
                p_tile(i, 3 * b + 2)

            p_load(0, 0)
            with act.Fori(0, NC // 2 - 1) as i:
                for b in range(2):
                    p_chunk(i, b, True)
            p_chunk(NC // 2 - 1, 0, True)
            p_chunk(NC // 2 - 1, 1, False)
            for b in range(2):
                act.wait_ge(p_out[b], 80 * (NC // 2 + 1))
            end_phase(act, 2)

            def s_load(c, b, half):
                act.dma_start(skb[:, b, :], kt_d[c][:, half * H:half * H + H]).then_inc(s_in[b], 16)
                act.dma_start(svt[:, b, :], vt_d[c]).then_inc(s_in[b], 16)

            def s_step(n, b, c, then, i=None):
                act.wait_ge(s_mm, n + 1)
                if then is not None:
                    s_load(then[0], 1 - b, then[1])
                if c is not None:
                    act.wait_ge(s_upd, n + 2)
                    act.dma_start(sb_d[c], stb[:, b].rearrange("p h n -> p (h n)")).then_inc(s_out[b], 16)
                    store_tile(T_ZA + 3 * NC + b, in_s[i, b], i, 2, 4)

            s_load(NC - 1, 0, 1)
            with act.Fori(0, NC // 2 - 1) as i:
                for b in range(2):
                    s_step(i * 2 + b, b, i * -2 + (NC - 1 - b), (i * -2 + (NC - 2 - b), 1), i)
            s_step(NC - 2, 0, 1, (0, 1), NC // 2 - 1)
            s_step(NC - 1, 1, 0, (NCX, 0), NC // 2 - 1)
            s_step(NC, 0, None, (NCX + 1, 0))
            for b in range(2):
                act.wait_ge(s_out[b], 16 * (NC // 2 + 1))
            for b in range(2):
                act.wait_ge(store_done[b], 16 * ((T_POOL - b + 1) // 2 + 1))
            end_phase(act, 3)
            for src, dst in ((tabq[:, :, 0:T], tabf), (lev, levf), (hmask, mask)):
                act.dma_start(dst[:, :, :], src).then_inc(tab_in, 16)

            def f_exps(i, b, groups):
                for n in groups:
                    act.wait_ge(f_mul, i * 8 + (4 * b + n + 1))
                    for h in range(HEADS):
                        act.wait_ge(f_arg, i * 32 + (16 * b + 4 * n + h + 1))
                        act.activation(ex[:, n % 2, h, :], g[:, h, :], ACT.Exp).then_inc(f_exp, 1)

            def f_chunk(i, b, more):
                c = i * 2 + b
                f_exps(i, b, (2, 3))
                act.wait_ge(f_lev, i * 16 + (8 * b + 1))
                act.wait_ge(f_omm, c + 1)
                act.activation(pt[:, :, :].rearrange("p h n -> p (h n)"), g[:, 4, :], ACT.Copy, scale=2.0)\
                   .then_inc(f_diag, 1)
                if more:
                    f_exps(i if b == 0 else i + 1, 1 - b, (0, 1))
                act.wait_ge(f_omm, c + 2)
                for n in range(2):
                    v = act.activation(
                        oall[:, :, :].rearrange("p t (c n) -> p c t n", n=CH)[:, c, 4 * n:4 * n + 4, :],
                        pb[n][:, :].rearrange("p (t n) -> p t n", n=CH), ACT.Copy)
                v.then_inc(f_oev, 1)

            f_exps(0, 0, (0, 1))
            with act.Fori(0, NCX // 2 - 1) as i:
                for b in range(2):
                    f_chunk(i, b, True)
            f_chunk(NCX // 2 - 1, 0, True)
            f_chunk(NCX // 2 - 1, 1, False)
            end_phase(act, 4)


            def z_load(n):
                act.dma_start(zb[:, n % 2, :], proj_d[T_ZB + n][:, 0:T]).then_inc(q_z[n % 2], 16)

            def q_high(grp):
                if grp >= 2:
                    act.wait_ge(unit_done, UNIT[T_POOL] + 4 * grp - 4)
                act.wait_ge(q_in[grp], 16)
                for n in (2 * grp, 2 * grp + 1):
                    act.activation(dh[:, grp % 2, n % 2, :], qd[:, n, :], ACT.Copy).then_inc(q_dh, 1)

            def q_gate(grp):
                for n in (2 * grp, 2 * grp + 1):
                    act.wait_ge(q_z[n % 2], 16 * (n // 2 + 1))
                    act.activation(zb[:, n % 2, :], zb[:, n % 2, :], ACT.Silu).then_inc(q_sil, 1)
                for n in (2 * grp, 2 * grp + 1):
                    for half in range(2):
                        u = 2 * n + half
                        act.wait_ge(q_y, u + 1)
                        act.activation(bh[:, n, H * half:H * half + H], yb[:, u % 2, :], ACT.Copy)\
                           .then_inc(q_yh, 1)
                    if n + 2 < 8:
                        z_load(n + 2)

            for half in range(2):
                act.wait_ge(u_out[half], 16 * (NCX + 1))
            for grp in range(4):
                act.dma_start(qd[:, 2 * grp:2 * grp + 2, :],
                              d_d[2 * grp:2 * grp + 2].rearrange("t p n -> p t n")).then_inc(q_in[grp], 16)
                if grp < 2:
                    z_load(grp)
            q_high(0)
            for grp in range(1, 4):
                q_high(grp)
                q_gate(grp - 1)

            za_d = proj_d[T_ZA:T_ZA + 8, :, 0:T].rearrange("(h v) p n -> h p v n", v=2)
            gb_d = proj_d[T_GB:T_GB + 8, :, 0:T].rearrange("(h v) p n -> h p v n", v=2)

            def pair_of(x, h):
                return x[:, :, :].rearrange("p (h v) n -> p h v n", v=2)[:, h]

            def o_load_za(h):
                act.dma_start(pair_of(zal, h), za_d[h]).then_inc(o_in, 16)

            def o_load_gb(h):
                act.dma_start(pair_of(mix, h), gb_d[h]).then_inc(b_in, 16)

            def o_squares(h):
                act.activation(osq[:, :, :], pair_of(oall, h), ACT.Square).then_inc(o_sq, 1)

            def o_root(h):
                act.wait_ge(o_st, h + 1)
                act.wait_ge(o_n, h * 2 + 1)
                act.activation(orstd[:, :].rearrange("p (u n) -> p u n", u=2), g[:, 0:2, :], ACT.Sqrt,
                               bias=epsc[:, 0:1]).then_inc(o_std, 1)

            def o_head(h, root, squares_too):
                act.wait_ge(b_in, h * 16 + 16)
                act.wait_ge(o_in, h * 16 + 16)
                if root:
                    o_load_gb(h + 1)
                    o_load_za(h + 1)
                act.activation(pair_of(mix, h), pair_of(mix, h), ACT.Sigmoid).then_inc(b_sg, 1)
                act.activation(pair_of(zal, h), pair_of(zal, h), ACT.Silu).then_inc(o_sil, 1)
                for v in range(2):
                    act.wait_ge(o_n, h * 2 + (v + 2))
                    act.activation(ah[:, h * 2 + v, :], oall[:, h * 2 + v, :], ACT.Copy).then_inc(o_h, 1)
                if root:
                    o_root(h + 1)
                if squares_too:
                    o_squares(h + 2)

            act.wait_ge(q_dl, 8)
            o_load_za(0)
            q_gate(3)
            o_squares(0)
            act.wait_ge(unit_done, UNIT[T_B])
            o_load_gb(0)
            act.wait_ge(q_yl, 16)
            o_root(0)
            o_squares(1)
            with act.Fori(0, HEADS - 2) as h:
                o_head(h, True, True)
            o_head(HEADS - 2, True, False)
            o_head(HEADS - 1, False, False)

            ga_d = proj_d[T_GA:T_GA + 8].rearrange("(i j) p n -> i j p n", j=2)
            act.wait_ge(o_l, 8)
            for b in range(2):
                act.dma_start(ga[:, b, :], ga_d[0, b][:, 0:T]).then_inc(a_in[b], 16)

            def a_high(i, b, load):
                act.wait_ge(a_m, i * 2 + (b + 3))
                act.activation(bh[:, i * 2 + b, :], mix[:, i * 2 + b, :], ACT.Copy).then_inc(a_mh, 1)
                if load:
                    act.dma_start(ga[:, b, :], ga_d[i + 1, b][:, 0:T]).then_inc(a_in[b], 16)

            def a_sigmoid(i, b):
                act.wait_ge(a_in[b], i * 16 + 16)
                act.activation(ga[:, b, :], ga[:, b, :], ACT.Sigmoid).then_inc(a_sg, 1)

            with act.Fori(0, 3) as i:
                for b in range(2):
                    a_sigmoid(i, b)
                for b in range(2):
                    a_high(i, b, True)
            for b in range(2):
                a_sigmoid(3, b)
            for b in range(2):
                a_high(3, b, False)

            act.wait_ge(a_ml, 8)
            act.dma_start(mix[:, :, :], xT).then_inc(r_in, 16)

            def tile_out(i, b):
                for n in range(2):
                    u = UNIT[T_OUT] + 2 * b + n
                    act.wait_ge(bank_free[u % 2], i * 2 + (u // 2 + 2))

            act_squares(act, 1, T, mix, sq1, tile_out)
            act_roots(act, 1, T, orstd)
            act.dma_start(xin[:, :, T:TA], ctx2T).then_inc(ctx2_in, 16)
            act.wait_ge(n1_x, 8)
            act.dma_start(xp_d.rearrange("t p n -> p t n"), xin[:, :, 0:T]).then_inc(xp_out, 16)
            act.wait_ge(ctx2_in, 16)
            act_squares(act, 2, TA, xin, squares)
            act_roots(act, 2, TA, rstd)
            act.wait_ge(xp_out, 16)
            operand_tiles(1, TA, 24, xin, xh)

            def read_out(t0, dst, func, i=None, tiles=0, units=0, scale=1.0):
                u0, nu = UNIT[t0], UNIT[t0 + 1] - UNIT[t0]
                for n in range(nu):
                    u, w = u0 + n, min(H, TA - n * H)
                    act.wait_ge(unit_done, step(u + 1, i, units))
                    act.activation(dst[:, n * H:n * H + w], pb[u % 2][:, 0:w], func, scale=scale)\
                       .then_inc(bank_free[u % 2], 1)

            act.wait_ge(xl_ready, 2 * KT)
            for t in range(4):
                read_out(T_CV + t, zcs[:, t, :], ACT.Copy if t < 2 else ACT.Sigmoid)
            with act.Fori(0, 2) as i:
                for b in range(2):
                    read_out(T_SG + b, zcs[:, i * 2 + (b + 4), :], ACT.Gelu_apprx_tanh, i, 2, 4)
            with act.Fori(0, 2) as i:
                for b in range(2):
                    read_out(T_K2 + b, zkv[:, i * 2 + b, :], ACT.Copy, i, 2, 6)
            act.wait_ge(z_dve, 1)
            act.activation(zcs[:, 2:4, :], zcs[:, 0:2, :], ACT.Square).then_inc(z_act, 1)
            act.wait_ge(y_dve, 1)
            act.activation(vsq[:, :, :], zcs[:, 6:8, :], ACT.Square).then_inc(y_act, 1)
            for t in range(2):
                read_out(T_V2 + t, zkv[:, 4 + t, :], ACT.Copy)
            act.wait_ge(z_pe, 2)
            act.activation(zcs[:, 2:4, :].rearrange("p t (u n) -> p (t u) n", u=2), g[:, 0:4, :],
                           ACT.Sqrt, bias=epsc[:, 0:1]).then_inc(z_act, 1)
            act.wait_ge(y_pe, 2)
            act.activation(vroot[:, :].rearrange("p (u n) -> p u n", u=2), g[:, 4:6, :], ACT.Sqrt,
                           bias=epsc[:, 0:1]).then_inc(y_act, 1)
            for t in range(2, 4):
                read_out(T_V2 + t, zkv[:, 4 + t, :], ACT.Copy)
            act.wait_ge(y_dve, 3)
            for t in range(2):
                n, m = COL["sg_g"] + t, COL["sg_b"] + t
                v = act.activation(zcs[:, 6 + t, :], zcs[:, 6 + t, :], ACT.Identity,
                                   scale=col[:, n:n + 1], bias=col[:, m:m + 1])
            v.then_inc(y_act, 1)
            act.wait_ge(z_dve, 3)
            act.dma_start(sgw_sb[:, :, :], sgw).then_inc(sg_in, 16)
            act.dma_start(sgb_sb[:, :, :], sgb).then_inc(sg_in, 16)
            for t in range(2):
                n, m = COL["cv_g"] + t, COL["cv_nb"] + t
                v = act.activation(zcs[:, t, :], zcs[:, t, :], ACT.Silu, scale=col[:, n:n + 1],
                                   bias=col[:, m:m + 1])
            v.then_inc(z_act, 1)
            for t in range(2):
                read_out(T_Q2 + t, zq[:, t, :], ACT.Copy, scale=0.125)
            act.wait_ge(y_pe, 3)
            act.activation(vtok[:, :, :].rearrange("p (a n) c -> p a (n c)", a=4), g[:, 0:4, :],
                           ACT.Copy).then_inc(y_act, 1)
            for t in range(2, 4):
                read_out(T_Q2 + t, zq[:, t, :], ACT.Copy, scale=0.125)
            for q, n in ((at_vtk, 1), (at_sc, 4), (at_ex, 2), (at_tr, 2), (at_ptc, 1), (at_pv, 2),
                         (at_o, 2), (at_ot, 2), (at_lo, 1)):
                act.sem_inc(q, n)
            end_phase(act, 5)
            act.wait_ge(z_act, 3)
            act.activation(mh[:, 6:8, :], zcs[:, 0:2, :], ACT.Copy).then_inc(z_act, 1)
            act.wait_ge(y_dve, 5)
            act.activation(mh[:, 4:6, :], zcs[:, 6:8, :], ACT.Copy).then_inc(y_act, 1)
            end_phase(act, 6)

            def at_exp(i, k):
                b = k % 2
                act.wait_ge(at_nm, i * 16 + (k + 1))
                act.wait_ge(at_tr, i * 16 + (k + 1))
                act.activation(pr[:, b, 0:H], sl[:, b, :], ACT.Exp, bias=tiny[:, b, 2:3],
                               accum_out=tiny[:, b, 3:4])
                act.activation(pr[:, b, H:H + C], pb[b][:, 0:C], ACT.Exp,
                               bias=tiny[:, b, 2:3], accum_out=tiny[:, b, 4:5]).then_inc(at_ex, 1)

            def at_high(i, k):
                bc, br, _ = step_of(k)
                act.wait_ge(at_ot, i * 8 + (k // 2 + 3))
                act.activation(at_tokens(br, bc)(mh[:, i, :]),
                               g[:, 4, P:2 * P].rearrange("p (r c) -> p r c", c=16), ACT.Copy)\
                   .then_inc(at_hi, 1)

            def at_queries(i):
                act.activation(qs2[:, :].rearrange("p (b r c) -> p b r c", r=ROWS, c=16),
                               zq[:, i, :].rearrange("p (r b c) -> p b r c", b=4, c=16), ACT.Copy)\
                   .then_inc(at_stq, 1)

            def at_pair(i, more):
                for k in range(16):
                    act.wait_ge(at_tr, i * 16 + (k + 3))
                    act.wait_ge(at_pv, i * 16 + (k + 1))
                    act.activation(ptr[:, k % 2, :],
                                   g[:, 2:4, :].rearrange("p a n -> p (a n)")[:, 0:H + C], ACT.Copy)\
                       .then_inc(at_ptc, 1)
                    if k and k % 2 == 0:
                        at_high(i, k - 1)
                    if k + 2 < 16:
                        at_exp(i, k + 2)
                    elif more:
                        at_exp(i + 1, k - 14)
                    if k == 13 and more:
                        act.wait_ge(at_s, i * 16 + 16)
                        at_queries(i + 1)
                at_high(i, 15)

            at_queries(0)
            for k in range(2):
                at_exp(0, k)
            with act.Fori(0, AH // 2 - 1) as i:
                at_pair(i, True)
            at_pair(AH // 2 - 1, False)
            end_phase(act, 7)

            act.dma_start(x2[:, :, :], xp_d.rearrange("t p n -> p t n")).then_inc(x2_in, 16)

            def tile_added(u0):
                def wait(i, b):
                    for n in range(2):
                        u = u0 + 2 * b + n
                        act.wait_ge(bank_free[u % 2], i * 2 + (u // 2 + 2))
                return wait

            act_squares(act, 3, T, x2, sq2, tile_added(UNIT[T_W2]))
            act_roots(act, 3, T, root2)
            operand_tiles(2, T, 48, xw, mh)

            act.wait_ge(xl_ready, 3 * KT)
            act.wait_ge(f_pad, 1)

            def f_copy(t0, kt, tile, i=None):
                for n in range(2):
                    u = UNIT[t0] + n
                    act.wait_ge(unit_done, step(u + 1, i, 2 * F_UNITS))
                    if n == 0 and tile >= 2:
                        act.wait_ge(f_cv, step(3 * (tile - 1), i, 12))
                    act.activation(gp[:, kt, 1 + H * n:1 + H * n + H], pb[u % 2][:, :], ACT.Copy)\
                       .then_inc(bank_free[u % 2], 1)

            def f_silu(kt, tile, i=None):
                fb = COL["ff_b"] + tile
                act.wait_ge(f_cv, step(3 * (tile + 1), i, 12))
                if tile >= 2:
                    act.wait_ge(f_hid, step(2 * (tile - 1), i, 8))
                bias_of = col[:, fb:fb + 1] if i is None else col[:, bass.ds(i * 4 + fb, 1)]
                act.activation(sgm[:, kt, :], cb[:, kt, :], ACT.Silu, bias=bias_of).then_inc(f_sil, 1)

            def f_high(par, kt, tile, i=None):
                act.wait_ge(f_hid, step(2 * (tile + 1), i, 8))
                if tile >= 4:
                    act.wait_ge(unit_done, step(DOWN_END[tile // 2 - 2], i, 2 * F_UNITS))
                act.activation(hh[:, par, kt, :], cb[:, kt, :], ACT.Copy).then_inc(f_hh, 1)

            def f_up(group, i=None):
                for kt in range(2):
                    tile = 2 * group + kt
                    f_copy(UP[group] + 2 * kt, kt, tile, i)
                    f_silu(kt, tile, i)
                    f_high(group % 2, kt, tile, i)

            f_up(0)
            f_up(1)
            f_up(2)
            with act.Fori(0, (GROUPS - 3) // 2) as i:
                f_up(3, i)
                f_up(4, i)
            act_squares(act, 4, T, x2, cb, tile_added(DOWN_LAST))
            act_roots(act, 4, T, gp_root)
            with act.Fori(0, KT) as k:
                act.wait_ge(f_fin, k + 1)
                act.dma_start(out_tiles[k], x2[:, k, :]).then_inc(out_done, 16)
            act.wait_ge(out_done, 16 * KT)

        @block.vector
        def _(dve):
            def mod_tile(slot, buf, landed, tile, cond, ctx_done=None):
                dve.wait_ge(mod_in[buf], landed)
                dve.wait_ge(mod_free, tile + 1)
                if ctx_done is not None:
                    nc.vector.tensor_tensor_reduce(
                        out=prod[:, :], in0=mod_raw[:, buf, :], in1=crow_sb[:, cond + 1, :], scale=1.0,
                        scalar=0.0, op0=ALU.mult, op1=ALU.add,
                        accum_out=mod_sum[:, 1, slot:slot + 1]).then_inc(mod_ctx, 1)
                    dve.wait_ge(mod_ctx, ctx_done)
                nc.vector.tensor_tensor_reduce(
                    out=prod[:, :], in0=mod_raw[:, buf, :], in1=crow_sb[:, cond, :], scale=1.0,
                    scalar=0.0, op0=ALU.mult, op1=ALU.add,
                    accum_out=mod_sum[:, 0, slot:slot + 1]).then_inc(mod_free, 1)

            def mod_quads(m0, n, cond, ctx_done):
                vx = modx[:, m0:m0 + 4 * n].rearrange("p (i j) -> p i j", j=4)
                vc = modc[:, m0:m0 + 4 * n].rearrange("p (i j) -> p i j", j=4)
                with dve.Fori(0, n) as i:
                    dve.wait_ge(mod_kept, i + (m0 // 4 + 1))
                    for j in range(4):
                        mod_tile(j, j, i * 16 + (16 + 4 * m0), i * 4 + (m0 + j), cond,
                                 None if ctx_done is None else i * 4 + (ctx_done + j))
                    dve.wait_ge(mod_free, i * 4 + (m0 + 5))
                    if ctx_done is not None:
                        nc.vector.tensor_copy(vc[:, i, :], mod_sum[:, 1, :])
                    nc.vector.tensor_copy(vx[:, i, :], mod_sum[:, 0, :]).then_inc(mod_kept, 1)

            nc.vector.memset(epsc[:, :], EPS).then_inc(gain_ready, 1)
            nc.vector.memset(prod[:, :], 0.0).then_inc(mod_free, 1)
            dve.sem_inc(mod_kept, 1)
            dve.wait_ge(cond_ready, 1)
            mod_quads(0, 4, 0, 1)

            def gains(n, m0, bias, norm, seen):
                for j, m in enumerate((modx, modc)):
                    nc.vector.tensor_tensor(m[:, m0:m0 + 16], m[:, m0:m0 + 16], bias, ALU.add)\
                      .then_inc(gain_ready, 1)
                dve.wait_ge(gain_ready, seen + 2)
                for j, m in enumerate((modx, modc)):
                    nc.vector.scalar_tensor_tensor(gain[:, j, :], m[:, m0 + 8:m0 + 16], 1.0, norm,
                                                   ALU.add, ALU.mult).then_inc(gain_ready, 1)

            dve.wait_ge(const_in, 32)
            dve.wait_ge(mod_kept, 5)
            gains(0, 0, col[:, COL["b_mod"]:COL["b_mod"] + 16], col[:, COL["norm_g"]:COL["norm_g"] + 8], 1)

            def reciprocals(n, tokens, root):
                dve.wait_ge(std_ready, n + 1)
                nc.vector.reciprocal(root[:, 0:tokens], root[:, 0:tokens]).then_inc(rstd_ready, 1)
                dve.wait_ge(rstd_ready, n + 1)

            def normalise(n, tokens, root, src, work, high, low):
                def low_part(k, count):
                    dve.wait_ge(xh_ready, count)
                    nc.vector.tensor_tensor(low[:, k, 0:tokens], work[:, k, 0:tokens],
                                            high[:, k, 0:tokens], ALU.subtract).then_inc(xl_ready, 1)

                def scaled(k):
                    nc.vector.tensor_tensor(work[:, k, 0:tokens], src[:, k, 0:tokens],
                                            root[:, 0:tokens], ALU.mult).then_inc(t_ready, 1)

                scaled(0)
                with dve.Fori(1, KT) as k:
                    scaled(k)
                    low_part(k - 1, k + KT * n)
                low_part(KT - 1, KT * n + KT)

            reciprocals(0, TA, rstd)
            normalise(0, TA, rstd, xin, xin, xh, xl)
            mod_quads(16, 2, 0, None)
            dve.wait_ge(cond_ready, 2)
            mod_quads(24, 4, 2, 17)
            mod_quads(40, 8, 2, None)

            end_phase(dve, 1)
            nc.vector.memset(lrc[:, :, :], 1.0).then_inc(tab_ready, 1)
            dve.wait_ge(tab_in, 32)
            nc.vector.tensor_copy(matr[:, :, :], mat[:, 4:7, :]).then_inc(tab_ready, 1)

            def p_chunk(i, b):
                c = i * 2 + b
                dve.wait_ge(p_in[b], i * 128 + 128)
                dve.wait_ge(p_out[b], i * 80 + 80)
                at_c = (bass.ds(c * CH, CH))
                cos = tab[:, 0, at_c].unsqueeze(1).to_broadcast([P, HEADS, CH])
                sin = tab[:, 1, at_c].unsqueeze(1).to_broadcast([P, HEADS, CH])
                nc.vector.tensor_tensor(kr[:, b], kc[:, b], cos, ALU.mult).then_inc(p_dve, 1)
                nc.vector.tensor_tensor(rot[:, :, :], ks[:, b], sin, ALU.mult).then_inc(p_dve, 1)
                dve.wait_ge(p_dve, i * 4 + (2 * b + 2))
                nc.vector.tensor_tensor(kr[:, b], kr[:, b], rot[:, :, :], ALU.add).then_inc(p_kr, 1)
                dve.wait_ge(p_gk, c + 1)
                dve.wait_ge(p_ln, c + 1)
                nc.vector.scalar_tensor_tensor(la[:, :, :], g[:, 0:2, :], 0.0, soft[:, :, :], ALU.min,
                                               ALU.subtract).then_inc(p_la, 1)
                dve.wait_ge(p_lah, c + 1)
                nc.vector.tensor_tensor(lal[:, b], la[:, :, :], lah[:, b], ALU.subtract).then_inc(p_lal, 1)
                dve.wait_ge(p_exp, c + 2)
                dve.wait_ge(p_ktr, c + 1)
                nc.vector.tensor_tensor(kt[:, b, 0, :], ef[:, 0, :], g[:, 2, :], ALU.mult)
                nc.vector.tensor_tensor(kt[:, b, 1, :], ef[:, 1, :], g[:, 2, :], ALU.mult).then_inc(p_kt, 1)

            with dve.Fori(0, NC // 2) as i:
                for b in range(2):
                    p_chunk(i, b)
            end_phase(dve, 2)
            nc.vector.memset(stf[:, 0], 0.0).then_inc(tab_ready, 1)
            dve.wait_ge(tab_ready, 3)

            def s_update(n, b, c, d, st, saved):
                dve.wait_ge(s_mm, n + 2)
                dve.wait_ge(s_upd, n + 2)
                if saved is not None:
                    dve.wait_ge(s_out[1 - b], saved)
                for h in range(HEADS):
                    u = nc.vector.scalar_tensor_tensor(
                        st[:, 1 - b, h, :], st[:, b, h, :], dec[:, c, 4 * d + h:4 * d + h + 1],
                        g[:, 2 * b + h // 2, DV * (h % 2):DV * (h % 2) + DV], ALU.mult, ALU.add)
                u.then_inc(s_upd, 1)

            nc.vector.memset(stb[:, 0], 0.0).then_inc(s_upd, 1)
            with dve.Fori(0, NC // 2) as i:
                for b in range(2):
                    s_update(i * 2 + b, b, i * -2 + (NC - 1 - b), 1, stb, i * 16 + (16 + 16 * b))
            for b in range(2):
                s_update(NC + b, b, NCX + b, 0, stf, None)
            end_phase(dve, 3)

            dve.wait_ge(tab_in, 80)
            nc.vector.tensor_copy(levr[:, :, :], levf[:, :, :]).then_inc(tab_ready, 1)

            def f_update(i, b):
                c = i * 2 + b
                dve.wait_ge(f_smm, c + 2)
                dve.wait_ge(f_upd, c + 1)
                dve.wait_ge(f_omm, c + 2)
                for h in range(HEADS):
                    u = nc.vector.scalar_tensor_tensor(
                        stf[:, 1 - b, h, :], stf[:, b, h, :], dec[:, c, h:h + 1],
                        g[:, 4 + h // 2, DV * (h % 2):DV * (h % 2) + DV], ALU.mult, ALU.add)
                u.then_inc(f_upd, 1)

            def f_chunk(i, b, before):
                c = i * 2 + b
                dve.wait_ge(f_in[b], i * 160 + 160)
                at_c = (bass.ds(c * CH, CH))
                cos = tabf[:, 0, at_c].unsqueeze(1).to_broadcast([P, HEADS, CH])
                sin = tabf[:, 1, at_c].unsqueeze(1).to_broadcast([P, HEADS, CH])
                nc.vector.tensor_tensor(fq[:, b], fq[:, b], cos, ALU.mult).then_inc(f_rot, 1)
                nc.vector.tensor_tensor(frot[:, :, :], fs[:, b], sin, ALU.mult).then_inc(f_rot, 1)
                dve.wait_ge(f_rot, i * 4 + (2 * b + 2))
                nc.vector.tensor_tensor(fq[:, b], fq[:, b], frot[:, :, :], ALU.add).then_inc(f_qr, 1)
                dve.wait_ge(f_qr, c + 1)
                for n in range(4):
                    half, d = n // 2, n % 2
                    if n == 2 and before is not None:
                        f_update(*before)
                    dve.wait_ge(f_exp, i * 32 + (16 * b + 4 * n + 8))
                    part = half if d == 0 else 1 - half
                    src, dst = (fk, lk) if half == 0 else (fq, lq)
                    for l in range(LEVELS):
                        m = 1 << l
                        def blocks(x):
                            return x.rearrange("p h (k s m) -> p h k s m", s=2, m=m)[:, :, :, part, :]
                        nc.vector.tensor_tensor(
                            blocks(dst[:, l]), blocks(src[:, b]),
                            ex[:, n % 2, :, 64 * l:64 * l + 64].rearrange("p h (k m) -> p h k m", m=m),
                            ALU.mult)
                    nc.vector.tensor_tensor(
                        qi[:, b, d, :, 64 * half:64 * half + 64], fq[:, b, :, 64 * half:64 * half + 64],
                        ex[:, n % 2, :, 448:512], ALU.mult).then_inc(f_mul, 1)
                for l in range(LEVELS):
                    if l == 0:
                        dve.wait_ge(f_diag, c + 1)
                    dve.wait_ge(f_lev, i * 16 + (8 * b + l + 2))
                    dve.wait_ge(f_pred, i * 14 + (7 * b + l + 7))
                    nc.vector.memset(tick[:, :], 0.0)
                    nc.vector.copy_predicated(
                        pt[:, :, :], mask[:, l, :].bitcast(I32).unsqueeze(1).to_broadcast([P, HEADS, CH]),
                        g[:, 4 + (l + 1) % 2, :].rearrange("p (h n) -> p h n", n=CH)).then_inc(f_pred, 1)

            f_chunk(0, 0, None)
            with dve.Fori(0, NCX // 2 - 1) as i:
                f_chunk(i, 1, (i, 0))
                f_chunk(i + 1, 0, (i, 1))
            f_chunk(NCX // 2 - 1, 1, (NCX // 2 - 1, 0))
            f_update(NCX // 2 - 1, 1)
            end_phase(dve, 4)

            def q_low(grp):
                for n in (2 * grp, 2 * grp + 1):
                    dve.wait_ge(q_dh, n + 1)
                    nc.vector.tensor_tensor(dl[:, grp % 2, n % 2, :], qd[:, n, :],
                                            dh[:, grp % 2, n % 2, :], ALU.subtract).then_inc(q_dl, 1)

            def q_gate(grp):
                scale = COL["pool_scale"]

                def low_part(u):
                    dve.wait_ge(q_yh, u + 1)
                    half = slice(H * (u % 2), H * (u % 2) + H)
                    nc.vector.tensor_tensor(bl[:, u // 2, half], yb[:, u % 2, :], bh[:, u // 2, half],
                                            ALU.subtract).then_inc(q_yl, 1)

                for u in range(4 * grp, 4 * grp + 4):
                    n, half = u // 2, slice(H * (u % 2), H * (u % 2) + H)
                    unit = UNIT[T_POOL] + u
                    dve.wait_ge(unit_done, unit + 1)
                    dve.wait_ge(q_sil, n + 1)
                    if u >= 2:
                        dve.wait_ge(q_yl, u - 1)
                    nc.vector.scalar_tensor_tensor(
                        yb[:, u % 2, :], pb[unit % 2][:, :], col[:, scale + n:scale + n + 1],
                        zb[:, n % 2, half], ALU.mult, ALU.mult).then_inc(q_y, 1)
                    dve.wait_ge(q_y, u + 1)
                    nc.vector.tensor_copy(tick[:, :], yb[:, u % 2, 0:1]).then_inc(bank_free[unit % 2], 1)
                    if u % 4:
                        low_part(u - 1)
                low_part(4 * grp + 3)

            q_low(0)
            for grp in range(1, 4):
                q_low(grp)
                q_gate(grp - 1)
            q_gate(3)

            with dve.Fori(0, HEADS) as h:
                def root_half(n):
                    half = slice(H * n, H * n + H)
                    nc.vector.reciprocal(orstd[:, half], orstd[:, half]).then_inc(o_rec, 1)

                def unit_of_b(v, n):
                    u = UNIT[T_B] + 2 * v + n
                    dve.wait_ge(b_sg, h + 1)
                    dve.wait_ge(unit_done, h * 4 + (u + 1))
                    half = slice(H * n, H * n + H)
                    nc.vector.tensor_tensor(mix[:, h * 2 + v, half], mix[:, h * 2 + v, half],
                                            pb[u % 2][:, :], ALU.mult).then_inc(bank_free[u % 2], 1)

                def norm_and_gate(v):
                    t, gg = h * 2 + v, COL["gla_g"] + v
                    nc.vector.tensor_tensor(oall[:, t, :], oall[:, t, :], orstd[:, :], ALU.mult)\
                      .then_inc(o_t, 1)
                    dve.wait_ge(o_t, t + 1)
                    dve.wait_ge(o_sil, h + 1)
                    nc.vector.scalar_tensor_tensor(oall[:, t, :], oall[:, t, :], col[:, gg:gg + 1],
                                                   zal[:, t, :], ALU.mult, ALU.mult).then_inc(o_n, 1)

                def low_part(v):
                    t = h * 2 + v
                    dve.wait_ge(o_h, t + 1)
                    dve.wait_ge(o_n, t + 2)
                    nc.vector.tensor_tensor(al[:, t, :], oall[:, t, :], ah[:, t, :], ALU.subtract)\
                      .then_inc(o_l, 1)

                dve.wait_ge(o_std, h + 2)
                root_half(0)
                unit_of_b(0, 0)
                root_half(1)
                dve.wait_ge(o_rec, h * 2 + 2)
                norm_and_gate(0)
                unit_of_b(0, 1)
                norm_and_gate(1)
                unit_of_b(1, 0)
                low_part(0)
                low_part(1)
                unit_of_b(1, 1)

            with dve.Fori(0, 4) as i:
                for b in range(2):
                    t = i * 2 + b
                    dve.wait_ge(a_sg, t + 1)
                    for n in range(2):
                        u = UNIT[T_A] + 2 * b + n
                        dve.wait_ge(unit_done, i * 4 + (u + 1))
                        half = slice(H * n, H * n + H)
                        nc.vector.tensor_tensor(ga[:, b, half], ga[:, b, half], pb[u % 2][:, :], ALU.mult)\
                          .then_inc(bank_free[u % 2], 1)
                    for u in (UNIT[T_A] + 2 * b, UNIT[T_A] + 2 * b + 1):
                        dve.wait_ge(bank_free[u % 2], i * 2 + (u // 2 + 2))
                    nc.vector.tensor_tensor(mix[:, t, :], mix[:, t, :], ga[:, b, :], ALU.add)\
                      .then_inc(a_m, 1)
                    dve.wait_ge(a_m, t + 3)
                    dve.wait_ge(a_mh, t + 1)
                    nc.vector.tensor_tensor(bl[:, t, :], mix[:, t, :], bh[:, t, :], ALU.subtract)\
                      .then_inc(a_ml, 1)

            gb = COL["b_mod"] + 16
            nc.vector.tensor_tensor(modx[:, 16:24], modx[:, 16:24], col[:, gb:gb + 8], ALU.add)\
              .then_inc(gain_ready, 1)
            dve.wait_ge(gain_ready, 6)
            dve.wait_ge(r_in, 16)
            with dve.Fori(0, 4) as i:
                for b in range(2):
                    t = i * 2 + b
                    for n in range(2):
                        u = UNIT[T_OUT] + 2 * b + n
                        dve.wait_ge(unit_done, i * 4 + (u + 1))
                        half = slice(H * n, H * n + H)
                        nc.vector.scalar_tensor_tensor(
                            mix[:, t, half], pb[u % 2][:, :], modx[:, bass.ds(i * 2 + (16 + b), 1)],
                            mix[:, t, half], ALU.mult, ALU.add).then_inc(bank_free[u % 2], 1)

            dve.wait_ge(mod_kept, 19)
            ab = COL["ada_b"]
            gains(1, 24, col[:, ab:ab + 16], col[:, COL["norm1_g"]:COL["norm1_g"] + 8], 6)
            nc.vector.tensor_tensor(modx[:, 40:72], modx[:, 40:72], col[:, ab + 16:ab + 48], ALU.add)\
              .then_inc(gain_ready, 1)
            reciprocals(1, T, orstd)
            for u in (UNIT[T_OUT] + 14, UNIT[T_OUT] + 15):
                dve.wait_ge(bank_free[u % 2], u // 2 + 2)
            with dve.Fori(0, KT) as k:
                nc.vector.scalar_tensor_tensor(
                    xin[:, k, 0:T], mix[:, k, :], col[:, bass.ds(k + COL["final_g"], 1)], orstd[:, :],
                    ALU.mult, ALU.mult).then_inc(n1_x, 1)
            reciprocals(2, TA, rstd)
            dve.wait_ge(xp_out, 16)
            normalise(1, TA, rstd, xin, xin, xh, xl)

            dve.wait_ge(xl_ready, 2 * KT)
            half = TAPS // 2
            nc.vector.memset(hpad[:, :, 0:half], 0.0)
            nc.vector.memset(hpad[:, :, half + T:half + T + half], 0.0).then_inc(z_h, 1)
            for t in range(2):
                for u in range(UNIT[T_CV + 3], UNIT[T_CV + 4]):
                    dve.wait_ge(bank_free[u % 2], u // 2 + 2)
                nc.vector.tensor_tensor(hpad[:, t, half:half + T], zcs[:, t, :], zcs[:, 2 + t, :],
                                        ALU.mult).then_inc(z_h, 1)
            dve.wait_ge(z_h, 3)
            cw, cbias = COL["cv_w"], COL["cv_b"]
            for t in range(2):
                nc.vector.tensor_scalar(zcs[:, t, :], hpad[:, t, 0:T], col[:, cw + TAPS * t:cw + TAPS * t + 1],
                                        col[:, cbias + t:cbias + t + 1], ALU.mult, ALU.add).then_inc(z_cv, 1)
            with dve.Fori(1, TAPS) as tap:
                for t in range(2):
                    dve.wait_ge(z_cv, tap * 2 + (t - 1))
                    nc.vector.scalar_tensor_tensor(
                        zcs[:, t, :], hpad[:, t, bass.ds(tap, T)], col[:, bass.ds(tap + (cw + TAPS * t), 1)],
                        zcs[:, t, :], ALU.mult, ALU.add).then_inc(z_cv, 1)

            dve.wait_ge(z_pe, 1)
            nc.vector.tensor_tensor(zcs[:, 0:2, :].rearrange("p t (u n) -> p (t u) n", u=2),
                                    zcs[:, 0:2, :].rearrange("p t (u n) -> p (t u) n", u=2), g[:, 0:4, :],
                                    ALU.subtract).then_inc(z_dve, 1)
            dve.wait_ge(y_pe, 1)
            for t in range(2):
                v = nc.vector.tensor_tensor(zcs[:, 6 + t, :].rearrange("p (u n) -> p u n", u=2),
                                            zcs[:, 6 + t, :].rearrange("p (u n) -> p u n", u=2),
                                            g[:, 4:6, :], ALU.subtract)
            v.then_inc(y_dve, 1)
            dve.wait_ge(y_act, 2)
            nc.vector.reciprocal(vroot[:, :], vroot[:, :]).then_inc(y_dve, 1)
            dve.wait_ge(y_dve, 2)
            nc.vector.tensor_tensor(zcs[:, 6:8, :], zcs[:, 6:8, :],
                                    vroot[:, :].unsqueeze(1).to_broadcast([P, 2, T]), ALU.mult)\
              .then_inc(y_dve, 1)
            dve.wait_ge(z_act, 2)
            nc.vector.reciprocal(zcs[:, 2:4, :], zcs[:, 2:4, :]).then_inc(z_dve, 1)
            dve.wait_ge(z_dve, 2)
            nc.vector.tensor_tensor(zcs[:, 0:2, :], zcs[:, 0:2, :], zcs[:, 2:4, :], ALU.mult)\
              .then_inc(z_dve, 1)
            dve.wait_ge(y_pe, 4)
            dve.wait_ge(sg_in, 32)
            for t in range(2):
                v = nc.vector.tensor_tensor(
                    zcs[:, 6 + t, :].rearrange("p (n q) -> p n q", q=CH),
                    g[:, 2 * t:2 * t + 2, :].rearrange("p a (n q) -> p (a n) q", q=CH),
                    sgb_sb[:, t, :].unsqueeze(1).to_broadcast([P, NCX, CH]), ALU.add)
            v.then_inc(y_dve, 1)
            dve.wait_ge(y_dve, 4)
            nc.vector.tensor_tensor(zcs[:, 6:8, :], zcs[:, 6:8, :], zcs[:, 4:6, :], ALU.mult)\
              .then_inc(y_dve, 1)
            end_phase(dve, 5)
            dve.wait_ge(z_act, 4)
            nc.vector.tensor_tensor(ml[:, 6:8, :], zcs[:, 0:2, :], mh[:, 6:8, :], ALU.subtract)\
              .then_inc(z_dve, 1)
            dve.wait_ge(y_act, 5)
            nc.vector.tensor_tensor(ml[:, 4:6, :], zcs[:, 6:8, :], mh[:, 4:6, :], ALU.subtract)\
              .then_inc(y_dve, 1)
            end_phase(dve, 6)

            def at_values(i, n, dst, used):
                w = C if n == 1 else H
                dve.wait_ge(at_vt, i * 5 + (n + 1))
                if used is not None:
                    dve.wait_ge(at_pv, used)
                nc.vector.tensor_copy(dst, g[:, 5, 0:w]).then_inc(at_vtk, 1)

            def at_scores(i, k, used=None):
                b, bc = k % 2, k // 4
                if k % 4 == 0:
                    at_values(i, bc + 1 if bc else 0, vtk[:, bc % 2, :],
                              used if bc == 0 else i * 16 + (max(4 * (bc - 1), 0) + 2))
                dve.wait_ge(bias_in[k % 4], i * 64 + (16 * (k // 4) + 16))
                dve.wait_ge(at_s, i * 16 + (k + 1))
                dve.wait_ge(at_ex, i * 16 + (k + 1))
                nc.vector.memset(tick[:, :], 0.0)
                nc.vector.tensor_tensor_reduce(
                    out=sl[:, b, :], in0=g[:, b, :], in1=at_bias[:, k % 4, :], scale=1.0, scalar=-3e38,
                    op0=ALU.add, op1=ALU.max, accum_out=tiny[:, b, 0:1]).then_inc(at_sc, 1)
                nc.vector.tensor_reduce(tiny[:, b, 1:2], pb[b][:, 0:C], mybir.AxisListType.X,
                                        ALU.max).then_inc(at_m, 1)
                dve.wait_ge(at_sc, i * 16 + (k + 5))
                dve.wait_ge(at_m, i * 16 + (k + 1))
                nc.vector.tensor_scalar(tiny[:, b, 2:3], tiny[:, b, 0:1], tiny[:, b, 1:2], -1.0, ALU.max,
                                        ALU.mult).then_inc(at_nm, 1)

            def at_low(i, k):
                bc, br, _ = step_of(k)
                dve.wait_ge(at_hi, i * 8 + (k // 2 + 1))
                nc.vector.tensor_tensor(at_tokens(br, bc)(ml[:, i, :]),
                                        g[:, 4, P:2 * P].rearrange("p (r c) -> p r c", c=16),
                                        at_tokens(br, bc)(mh[:, i, :]), ALU.subtract).then_inc(at_lo, 1)

            def at_stage_values(n):
                v_rows = zkv[:, n, 0:T].rearrange("p (r c) -> p r c", c=GRID_W)
                for w, first in enumerate(KSPAN):
                    nc.vector.tensor_copy(vs2[:, H * w:H * w + H].rearrange("p (r c) -> p r c", c=32),
                                          v_rows[:, :, first:first + 32])
                nc.vector.tensor_copy(vs2[:, 4 * H:4 * H + C], zkv[:, n, T:TA]).then_inc(at_stv, 1)

            def at_pair(i, more):
                for k in range(16):
                    b = k % 2
                    dve.wait_ge(at_ex, i * 16 + (k + 3))
                    nc.vector.tensor_tensor(tiny[:, b, 5:6], tiny[:, b, 3:4], tiny[:, b, 4:5], ALU.add)\
                      .then_inc(at_sum, 1)
                    dve.wait_ge(at_sum, i * 16 + (k + 1))
                    nc.vector.reciprocal(tiny[:, b, 6:7], tiny[:, b, 5:6]).then_inc(at_r, 1)
                    if k == 0:
                        at_values(i, 1, vcx[:, :], i * 16 + 2)
                    if k and k % 2 == 0:
                        at_low(i, k - 1)
                    if k + 2 < 16:
                        at_scores(i, k + 2)
                    elif more:
                        at_scores(i + 1, k - 14, i * 16 + 14)
                    if k == 11 and more:
                        dve.wait_ge(at_vt, i * 5 + 5)
                        at_stage_values(i + 5)
                    if k == 13 and more:
                        dve.wait_ge(at_s, i * 16 + 16)
                        at_stage_keys(i + 1)
                    dve.wait_ge(at_pv, i * 16 + (k + 3))
                    dve.wait_ge(at_r, i * 16 + (k + 1))
                    dve.wait_ge(at_ot, i * 8 + (k // 2 + 1))
                    nc.vector.tensor_scalar(osb[:, k // 2 % 2, 64 * b:64 * b + 64],
                                            g[:, 4, 64 * b:64 * b + 64], tiny[:, b, 6:7], None,
                                            ALU.mult).then_inc(at_o, 1)
                at_low(i, 15)

            def at_stage_keys(i):
                nc.vector.tensor_copy(ks2[:, :], zkv[:, i, :]).then_inc(at_stk, 1)

            at_stage_keys(0)
            at_stage_values(4)
            for k in range(2):
                at_scores(0, k)
            with dve.Fori(0, AH // 2 - 1) as i:
                at_pair(i, True)
            at_pair(AH // 2 - 1, False)
            end_phase(dve, 7)

            gains_x = COL["norm2_g"]
            nc.vector.scalar_tensor_tensor(gain[:, 0, :], modx[:, 56:64], 1.0,
                                           col[:, gains_x:gains_x + 8], ALU.add, ALU.mult)\
              .then_inc(gain_ready, 1)
            dve.wait_ge(x2_in, 16)
            with dve.Fori(0, 4) as i:
                for b in range(2):
                    for n in range(2):
                        u = UNIT[T_W2] + 2 * b + n
                        dve.wait_ge(unit_done, i * 4 + (u + 1))
                        half = slice(H * n, H * n + H)
                        nc.vector.scalar_tensor_tensor(
                            x2[:, i * 2 + b, half], pb[u % 2][:, :], modx[:, bass.ds(i * 2 + (40 + b), 1)],
                            x2[:, i * 2 + b, half], ALU.mult, ALU.add).then_inc(bank_free[u % 2], 1)
            reciprocals(3, T, root2)
            for u in (UNIT[T_FF] - 2, UNIT[T_FF] - 1):
                dve.wait_ge(bank_free[u % 2], u // 2 + 2)
            normalise(2, T, root2, x2, xw, mh, ml)

            dve.wait_ge(xl_ready, 3 * KT)
            nc.vector.memset(gp[:, :, 0:1], 0.0)
            nc.vector.memset(gp[:, :, T + 1:T + 2], 0.0).then_inc(f_pad, 1)
            dve.wait_ge(f_pad, 1)

            def f_taps(t0, kt, tile, i=None):
                fw = COL["ff_w"] + 3 * tile
                for u in (UNIT[t0], UNIT[t0] + 1):
                    dve.wait_ge(bank_free[u % 2], step(u // 2 + 2, i, F_UNITS))
                if tile >= 2:
                    dve.wait_ge(f_hl, step(tile - 1, i, 4))
                for tap in range(3):
                    w = col[:, fw + tap:fw + tap + 1] if i is None else col[:, bass.ds(i * 12 + (fw + tap), 1)]
                    if tap == 0:
                        v = nc.vector.tensor_scalar(cb[:, kt, :], gp[:, kt, 0:T], w, None, ALU.mult)
                    else:
                        v = nc.vector.scalar_tensor_tensor(cb[:, kt, :], gp[:, kt, tap:tap + T], w,
                                                           cb[:, kt, :], ALU.mult, ALU.add)
                    v.then_inc(f_cv, 1)
                    if tap < 2:
                        dve.wait_ge(f_cv, step(3 * tile + tap + 1, i, 12))

            def f_hidden(t0, kt, tile, i=None):
                dve.wait_ge(f_sil, step(tile + 1, i, 4))
                for n in range(2):
                    u = UNIT[t0] + n
                    dve.wait_ge(unit_done, step(u + 1, i, 2 * F_UNITS))
                    half = slice(H * n, H * n + H)
                    nc.vector.tensor_tensor(cb[:, kt, half], sgm[:, kt, half], pb[u % 2][:, :], ALU.mult)\
                      .then_inc(f_hid, 1)
                    dve.wait_ge(f_hid, step(2 * tile + n + 1, i, 8))
                    nc.vector.tensor_copy(tick[:, :], cb[:, kt, H * n:H * n + 1])\
                      .then_inc(bank_free[u % 2], 1)

            def f_low(par, kt, tile, i=None):
                dve.wait_ge(f_hh, step(tile + 1, i, 4))
                nc.vector.tensor_tensor(hl[:, par, kt, :], cb[:, kt, :], hh[:, par, kt, :], ALU.subtract)\
                  .then_inc(f_hl, 1)

            def f_up(group, i=None):
                for kt in range(2):
                    tile, t = 2 * group + kt, UP[group] + 2 * kt
                    f_taps(t, kt, tile, i)
                    f_hidden(t + 1, kt, tile, i)
                    if kt == 0 or group == 0:
                        f_low(group % 2, kt, tile, i)

            def f_down(group, i=None):
                u0 = UNIT[DOWN[group]]
                if group:
                    for u in (DOWN_END[group - 1] - 2, DOWN_END[group - 1] - 1):
                        dve.wait_ge(bank_free[u % 2], step(u // 2 + 2, i, F_UNITS))
                for m in range(KT):
                    for n in range(2):
                        u = u0 + 2 * m + n
                        dve.wait_ge(unit_done, step(u + 1, i, 2 * F_UNITS))
                        half = slice(H * n, H * n + H)
                        nc.vector.scalar_tensor_tensor(
                            x2[:, m, half], pb[u % 2][:, :], modx[:, 64 + m:65 + m], x2[:, m, half],
                            ALU.mult, ALU.add).then_inc(bank_free[u % 2], 1)
                    if m == 0 and group < GROUPS - 1:
                        f_low((group + 1) % 2, 1, 2 * group + 3, i)

            f_up(0)
            f_up(1)
            f_down(0)
            f_up(2)
            f_down(1)
            with dve.Fori(0, (GROUPS - 3) // 2) as i:
                f_up(3, i)
                f_down(2, i)
                f_up(4, i)
                f_down(3, i)
            f_down(GROUPS - 1)
            reciprocals(4, T, gp_root)
            for u in (UNIT[NT] - 2, UNIT[NT] - 1):
                dve.wait_ge(bank_free[u % 2], u // 2 + 2)
            with dve.Fori(0, KT) as k:
                nc.vector.scalar_tensor_tensor(
                    x2[:, k, :], x2[:, k, :], col[:, bass.ds(k + COL["final_g2"], 1)], gp_root,
                    ALU.mult, ALU.mult).then_inc(f_fin, 1)

        @block.tensor
        def _(pe):
            for b in range(2):
                pe.sem_inc(bank_free[b], 1)
            pe.wait_ge(const_in, 32)
            pe_squares(pe, 0, TA, squares)
            pe_tile(pe, 0, ready=1)
            pe_tile(pe, 1)
            with pe.Fori(1, T_LR // 2) as i:
                for b in range(2):
                    pe_tile(pe, b, i, 2, 6)
            pe_tile(pe, T_LR)
            with pe.Fori(0, (T_ZA - T_Q) // 2) as i:
                for b in range(2):
                    pe_tile(pe, T_Q + b, i, 2, 4)

            pe.drain().then_inc(phase, 1)

            def p_tile(i, n):
                pe_tile(pe, T_ZA + n, i, 6, 12)

            def p_chunk(i, b):
                c = i * 2 + b
                p_tile(i, 3 * b)
                if b == 0:
                    pe.wait_ge(tab_ready, 2)
                pe.wait_ge(p_in[b], i * 128 + 128)
                pe.wait_ge(p_exp, c + 1)
                for d in range(2):
                    r = slice(32 * d, 32 * d + 17)
                    mm = pe.matmul(g[:, d, :], lrc[r, b, :], wup_sb[r, :], start=True, stop=True)
                mm.then_inc(p_gk, 1)
                pe.wait_ge(p_vt, c + 1)
                for n in range(8):
                    mm = pe.transpose(g[:, 3 + n // 4, CH * (n % 4):CH * (n % 4) + CH], vc[:, b, n, :], ident)
                mm.then_inc(p_vtr, 1)
                pe.wait_ge(p_kr, c + 1)
                pe.wait_ge(p_kt, c + 1)
                for h in range(HEADS):
                    mm = pe.transpose(g[:, 2, CH * h:CH * h + CH], kr[:, b, h, :], ident)
                mm.then_inc(p_ktr, 1)
                p_tile(i, 3 * b + 1)
                pe.wait_ge(p_lal, c + 1)
                for d in range(2):
                    for n, x in enumerate((lah, lal)):
                        pe.matmul(g[:, d, :], matr[:, d, :], x[:, b, d, :], start=(n == 0), stop=(n == 1))
                for d in range(2):
                    for h in range(HEADS):
                        o = 2 * (HEADS * d + h)
                        for n, x in enumerate((lah, lal)):
                            mm = pe.matmul(g[:, 5, o:o + 2], x[:, b, d, DK * h:DK * h + DK],
                                           matr[:, 2, 0:2], start=(n == 0), stop=(n == 1))
                mm.then_inc(p_arg, 1)
                p_tile(i, 3 * b + 2)

            with pe.Fori(0, NC // 2) as i:
                for b in range(2):
                    p_chunk(i, b)
            pe.drain().then_inc(phase, 1)

            def s_products(n, b, loads):
                pe.wait_ge(s_in[b], loads)
                pe.wait_ge(s_upd, n + 1)
                for h in range(HEADS):
                    mm = pe.matmul(g[:, 2 * b + h // 2, DV * (h % 2):DV * (h % 2) + DV],
                                   skb[:, b, DK * h:DK * h + DK], svt[:, b, DV * h:DV * h + DV],
                                   start=True, stop=True)
                mm.then_inc(s_mm, 1)

            with pe.Fori(0, NC // 2) as i:
                for b in range(2):
                    pe_tile(pe, T_ZA + 3 * NC + b, i, 2, 4)
                    s_products(i * 2 + b, b, i * 32 + 32)
            for b in range(2):
                s_products(NC + b, b, 32 * (NC // 2 + 1))
            end_phase(pe, 3)
            pe.wait_ge(tab_ready, 4)

            def f_exponents(i, b, groups):
                for n in groups:
                    half, d = n // 2, n % 2
                    for h in range(HEADS):
                        pe.wait_ge(f_exp, i * 32 + (16 * b + 4 * n + h + 1))
                        for x in range(2):
                            mm = pe.matmul(g[:, h, :], fla[:, b, x, d, DK * h:DK * h + DK],
                                           levr[:, d, H * half:H * half + H], start=(x == 0), stop=(x == 1))
                        mm.then_inc(f_arg, 1)

            def f_chunk(i, b, more):
                c = i * 2 + b

                def scores(m, keys, queries):
                    for h in range(HEADS):
                        mm = pe.matmul(g[:, 4 + m % 2, CH * h:CH * h + CH], keys[:, h, :],
                                       queries[:, h, :], start=True, stop=True)
                    mm.then_inc(f_lev, 1)

                f_exponents(i, b, (2, 3))
                pe.wait_ge(f_qr, c + 1)
                pe.wait_ge(f_upd, c + 1)
                scores(0, fk[:, b], fq[:, b])
                pe.wait_ge(f_mul, i * 8 + (4 * b + 6))
                for l in range(LEVELS):
                    if l == 1:
                        pe.wait_ge(f_diag, c + 1)
                    pe.wait_ge(f_pred, i * 14 + (7 * b + (7 if l == 0 else l + 6)))
                    scores(l + 1, lk[:, l], lq[:, l])
                    if l == 3 and more:
                        pe.wait_ge(f_in[1 - b], (i if b == 0 else i + 1) * 160 + 160)
                        f_exponents(i if b == 0 else i + 1, 1 - b, (0, 1))
                pe.wait_ge(f_pred, i * 14 + (7 * b + 14))
                pe.wait_ge(f_oev, c + 1)
                for h in range(HEADS):
                    for v in range(2):
                        o = pb[h // 2][:, DV * (h % 2) + CH * v:DV * (h % 2) + CH * v + CH]
                        f = slice(DV * h + CH * v, DV * h + CH * v + CH)
                        pe.matmul(o, fvt[:, b, f], pt[:, h, :], start=True, stop=False)
                        pe.matmul(o, stf[:, b, h, CH * v:CH * v + CH], qi[:, b, 0, h, :], start=False,
                                  stop=False)
                        mm = pe.matmul(o, fsb[:, b, h, CH * v:CH * v + CH], qi[:, b, 1, h, :],
                                       start=False, stop=True)
                mm.then_inc(f_omm, 1)
                for h in range(HEADS):
                    mm = pe.matmul(g[:, 4 + h // 2, DV * (h % 2):DV * (h % 2) + DV],
                                   fkt[:, b, DK * h:DK * h + DK], fvt[:, b, DV * h:DV * h + DV],
                                   start=True, stop=True)
                mm.then_inc(f_smm, 1)

            pe.wait_ge(f_in[0], 160)
            f_exponents(0, 0, (0, 1))
            with pe.Fori(0, NCX // 2 - 1) as i:
                for b in range(2):
                    f_chunk(i, b, True)
            f_chunk(NCX // 2 - 1, 0, True)
            f_chunk(NCX // 2 - 1, 1, False)
            end_phase(pe, 4)

            for grp in range(4):
                t = T_POOL + grp // 2
                if grp % 2 == 0:
                    pe.wait_ge(w_split, t + 1)
                pe.wait_ge(q_dl, 2 * grp + 2)
                for m in range(2):
                    for half in range(2):
                        u = UNIT[T_POOL] + 4 * grp + 2 * m + half
                        pe.wait_ge(bank_free[u % 2], u // 2 + 1)
                        first, last = pe_unit(pe, t % 2, dh[:, grp % 2], dl[:, grp % 2],
                                              slice(H * half, H * half + H), range(2),
                                              [512 * (grp % 2) + 256 * k + P * m for k in range(2)], u % 2)
                        if grp % 2 == 0 and m == 0 and half == 0:
                            first.then_inc(w_begun, 1)
                        last.then_inc(unit_done, 1)

            def o_means(h):
                pe.wait_ge(o_sq, h + 1)
                pe.wait_ge(o_std, h + 1)
                for u in range(2):
                    for v in range(2):
                        mm = pe.matmul(g[:, u, :], mean_v, osq[:, v, H * u:H * u + H], start=(v == 0),
                                       stop=(v == 1))
                mm.then_inc(o_st, 1)

            o_means(0)
            pe.wait_ge(q_yl, 16)
            with pe.Fori(0, HEADS - 1) as h:
                pe_tile(pe, T_B, h, 2, 4, bh, bl)
                o_means(h + 1)
                pe_tile(pe, T_B + 1, h, 2, 4, bh, bl)
            for b in range(2):
                pe_tile(pe, T_B + 2 * (HEADS - 1) + b, None, 0, 0, bh, bl)

            pe.wait_ge(o_l, 8)
            with pe.Fori(0, 4) as i:
                for b in range(2):
                    pe_tile(pe, T_A + b, i, 2, 4, ah, al)
            pe.wait_ge(a_ml, 8)
            with pe.Fori(0, 4) as i:
                for b in range(2):
                    pe_tile(pe, T_OUT + b, i, 2, 4, bh, bl)
            pe_squares(pe, 1, T, sq1)
            pe_squares(pe, 2, TA, squares)

            pe_tile(pe, T_CV, ready=KT + 1)
            for t in range(T_CV + 1, T_SG):
                pe_tile(pe, t)
            with pe.Fori(0, 2) as i:
                for b in range(2):
                    pe_tile(pe, T_SG + b, i, 2, 4)
            with pe.Fori(0, 2) as i:
                for b in range(2):
                    pe_tile(pe, T_K2 + b, i, 2, 6)

            def conv_means(src):
                for t in range(2):
                    for n in range(2):
                        mm = pe.matmul(g[:, 2 * t + n, :], mean_g, src[:, t, H * n:H * n + H], start=True,
                                       stop=True)
                mm.then_inc(z_pe, 1)

            def gating_means(src):
                for n in range(2):
                    for t in range(2):
                        mm = pe.matmul(g[:, 4 + n, :], mean_v, src[:, t, H * n:H * n + H], start=(t == 0),
                                       stop=(t == 1))
                mm.then_inc(y_pe, 1)

            pe.wait_ge(z_cv, 2 * TAPS)
            conv_means(zcs[:, 0:2, :])
            for u in (UNIT[T_K2] - 2, UNIT[T_K2] - 1):
                pe.wait_ge(bank_free[u % 2], u // 2 + 2)
            gating_means(zcs[:, 6:8, :])
            for t in range(2):
                pe_tile(pe, T_V2 + t)
            pe.wait_ge(z_act, 1)
            pe.wait_ge(z_dve, 1)
            conv_means(zcs[:, 2:4, :])
            pe.wait_ge(y_act, 1)
            gating_means(vsq[:, :, :])
            for t in (T_V2 + 2, T_V2 + 3, T_Q2):
                pe_tile(pe, t)
            pe.wait_ge(z_act, 2)
            pe.wait_ge(y_act, 3)
            for n in range(NCX):
                for t in range(2):
                    o = (2 * n + t) * P
                    mm = pe.transpose(g[:, o // H, o % H:o % H + P], zcs[:, 6 + t, CH * n:CH * n + CH], ident)
            mm.then_inc(y_pe, 1)
            for t in (T_Q2 + 1, T_Q2 + 2):
                pe_tile(pe, t)
            pe.wait_ge(y_act, 4)
            pe.wait_ge(sg_in, 32)
            for n in range(NCX):
                for q in range(4):
                    t, r = q // 2, 64 * (q % 2)
                    mm = pe.matmul(g[r:r + 64, 2 * t + n // 4, CH * (n % 4):CH * (n % 4) + CH],
                                   vtok[:, n, 64 * q:64 * q + 64], sgw_sb[:, q, :], start=True, stop=True)
            mm.then_inc(y_pe, 1)
            pe_tile(pe, T_Q2 + 3)
            end_phase(pe, 5)
            end_phase(pe, 6)

            def at_transposed(i, n, first, chunks):
                pe.wait_ge(at_vtk, i * 5 + (n + 1))
                for c in range(chunks):
                    mm = pe.transpose(g[:, 5, P * c:P * c + P], vs2[:, first + P * c:first + P * c + P],
                                      ident)
                mm.then_inc(at_vt, 1)

            def at_scores(i, k):
                bc, br, j = step_of(k)
                head = slice(64 * j, 64 * j + 64)
                if k == 0:
                    pe.wait_ge(at_stv, i + 1)
                    pe.wait_ge(at_stq, i + 1)
                    pe.wait_ge(at_stk, i + 1)
                if k % 4 == 0:
                    at_transposed(i, bc + 1 if bc else 0, H * bc, 4)
                pe.wait_ge(at_ex, i * 16 + (k + 1))
                block = 2 * bc + br
                q = qs2[head, P * block:P * block + P]
                keys = ks2[head, :]
                pe.matmul(g[:, k % 2, :], q, keys[:, 0:T].rearrange("p (r c) -> p r c", c=GRID_W)
                          [:, :, KSPAN[bc]:KSPAN[bc] + 32], start=True, stop=True)
                pe.matmul(pb[k % 2][:, 0:C], q, keys[:, T:TA], start=True, stop=True).then_inc(at_s, 1)

            def at_output(i, k):
                pe.wait_ge(at_o, i * 16 + (k + 3))
                pe.wait_ge(at_lo, i * 8 + (k // 2 + 1))
                pe.transpose(g[:, 4, P:2 * P], osb[:, k // 2 % 2, :], ident).then_inc(at_ot, 1)

            def at_pair(i, more):
                for k in range(16):
                    bc, br, j = step_of(k)
                    pe.wait_ge(at_ex, i * 16 + (k + 3))
                    pe.wait_ge(at_ptc, i * 16 + (k + 1))
                    for c in range(6):
                        mm = pe.transpose(g[:, 2 + c // 4, P * (c % 4):P * (c % 4) + P],
                                          pr[:, k % 2, P * c:P * c + P], ident)
                    mm.then_inc(at_tr, 1)
                    if k == 0:
                        at_transposed(i, 1, 4 * H, 2)
                    if k and k % 2 == 0:
                        at_output(i, k - 1)
                    if k + 2 < 16:
                        at_scores(i, k + 2)
                    elif more:
                        at_scores(i + 1, k - 14)
                    pe.wait_ge(at_ptc, i * 16 + (k + 2))
                    pe.wait_ge(at_vtk, i * 5 + (bc + 3))
                    pe.wait_ge(at_o, i * 16 + (k + 2))
                    pe.wait_ge(at_lo, i * 8 + (k // 2 + 1))
                    for c in range(6):
                        v = vtk[:, bc % 2, P * c + 64 * j:P * c + 64 * j + 64] if c < 4 else \
                            vcx[:, P * (c - 4) + 64 * j:P * (c - 4) + 64 * j + 64]
                        mm = pe.matmul(g[:, 4, 64 * j:64 * j + 64], ptr[:, k % 2, P * c:P * c + P], v,
                                       start=(c == 0), stop=(c == 5))
                    mm.then_inc(at_pv, 1)
                at_output(i, 15)

            for k in range(2):
                at_scores(0, k)
            with pe.Fori(0, AH // 2 - 1) as i:
                at_pair(i, True)
            at_pair(AH // 2 - 1, False)
            end_phase(pe, 7)

            with pe.Fori(0, 4) as i:
                for b in range(2):
                    pe_tile(pe, T_W2 + b, i, 2, 4, mh, ml)
            pe_squares(pe, 3, T, sq2)

            def f_up(group, i=None, ready=None):
                for n in range(4):
                    pe_tile(pe, UP[group] + n, i, 12, 2 * F_UNITS, mh, ml, ready if n == 0 else None)

            def f_down(group, i=None):
                pe.wait_ge(f_hl, step(2 * group + 2, i, 4))
                for h in range(2):
                    t0 = DOWN[group] + h
                    pe.wait_ge(w_split, step(t0 + 1, i, 12))
                    for m in range(4):
                        for n in range(2):
                            u = UNIT[t0] + 2 * m + n
                            pe.wait_ge(bank_free[u % 2], step(u // 2 + 1, i, F_UNITS))
                            first, last = pe_unit(pe, t0 % 2, hh[:, group % 2], hl[:, group % 2],
                                                  slice(H * n, H * n + H), range(2),
                                                  [256 * m + P * kt for kt in range(2)], u % 2)
                            if m == 0 and n == 0:
                                first.then_inc(w_begun, 1)
                            last.then_inc(unit_done, 1)

            f_up(0, ready=2 * KT + 1)
            f_up(1)
            f_down(0)
            f_up(2)
            f_down(1)
            with pe.Fori(0, (GROUPS - 3) // 2) as i:
                f_up(3, i)
                f_down(2, i)
                f_up(4, i)
                f_down(3, i)
            f_down(GROUPS - 1)
            pe_squares(pe, 4, T, cb)


def arrays_of(inputs):
    import numpy as np
    f = {k: np.asarray(v) for k, v in inputs.items()}

    def tiles(w):
        k, n = w.shape
        return w.reshape(k // P, P, n // P, P).transpose(2, 1, 0, 3).reshape(n // P, P, k)

    def columns(v):
        return v.reshape(-1, P).T

    def feature_major(x):
        return np.ascontiguousarray(x[0].T.reshape(KT, P, -1).transpose(1, 0, 2))

    w = f["w_in"][0]
    cut = np.cumsum([512, 512, 1024, 1024, 16, 16, 1024, 1024, 1024, 1024])
    q, k, v, za, lrf, lrb, ub, zb, ga, gb = np.split(w, cut[:-1], axis=1)
    lr = np.zeros((D, P), np.float32)
    lr[:, 0:16], lr[:, 32:48] = lrf, lrb
    wp = f["w_pool"][0].reshape(2, 2, 2, P, 256).transpose(0, 3, 1, 2, 4).reshape(2, P, 1024)
    w2 = f["w_in_2"][0]
    q2, k2, v2, sg, cv = np.split(w2, [512, 1024, 1536, 2048], axis=1)
    up, down = tiles(f["ffn_w_up_2"][0]), f["ffn_w_down_2"][0]
    dn = down.reshape(GROUPS, 2, P, 2, 4, P).transpose(0, 3, 2, 4, 1, 5).reshape(GROUPS, 2, P, 1024)
    ff = [up[0:1], up[FT:FT + 1], up[1:2], up[FT + 1:FT + 2]]
    for n in range(GROUPS):
        if n + 1 < GROUPS:
            a = 2 * (n + 1)
            ff += [up[a:a + 1], up[FT + a:FT + a + 1], up[a + 1:a + 2], up[FT + a + 1:FT + a + 2]]
        ff.append(dn[n])
    wall = np.concatenate([tiles(x) for x in (k, v, lr, q, za, ub, zb, ga, gb)] + [wp]
                          + [tiles(f[n][0]) for n in ("w_branch_b", "w_branch_a", "w_out")]
                          + [tiles(x) for x in (cv, sg, k2, v2, q2)] + [tiles(f["w_out_2"][0])] + ff)
    assert wall.shape == (NT, P, 1024), wall.shape

    def rows(m):
        return np.ascontiguousarray(m.T).reshape(-1, P, D)

    cw = f["cv_w_2"][0].reshape(TAPS, 2, P).transpose(2, 1, 0).reshape(P, 2 * TAPS)
    fw = f["ffn_conv_w_2"][0].reshape(3, FT, P).transpose(2, 1, 0).reshape(P, 3 * FT)
    vecs = {"norm_g": f["norm_g"], "b_mod": f["b_mod"], "gla_g": f["gla_norm_g"],
            "pool_scale": f["pool_scale"], "final_g": f["final_norm_g"], "ada_b": f["ada_b_2"],
            "norm1_g": f["norm1_g_2"], "norm2_g": f["norm2_g_2"], "sg_g": f["sg_norm_g_2"],
            "sg_b": f["sg_norm_b_2"], "cv_b": f["cv_b_2"], "cv_g": f["cv_norm_g_2"],
            "cv_nb": f["cv_norm_b_2"], "ff_b": f["ffn_conv_b_2"], "final_g2": f["final_norm_g_2"]}
    cols = np.concatenate([{"cv_w": cw, "ff_w": fw}[n] if n in ("cv_w", "ff_w") else columns(vecs[n])
                           for n, _ in _COLS], axis=1)
    crow = np.stack([f["c"][0], f["c_ctx"], f["c_2"][0], f["c_ctx_2"]])

    mats = np.zeros((P, 7, P), np.float32)
    i = np.arange(P)
    mats[:, 0] = np.eye(P)
    mats[:, 1] = 1 / D
    mats[:, 2] = 1 / DV
    mats[:, 3] = (i[:, None] // 64 == i[None] // 64) / 64.0
    mats[:, 4] = (i[:, None] > i[None]) / GATE_NORM
    mats[:, 5] = (i[:, None] < i[None]) / GATE_NORM
    mats[:, 6] = 1 / GATE_NORM
    nf = DK // 4
    freqs = (np.float32(10000.0) ** (-np.arange(nf, dtype=np.float32) / np.float32(nf))).astype(np.float32)
    t = np.arange(T)
    pos = np.stack([t // GRID_W, t % GRID_W]).astype(np.float32)
    ang = pos[:, None, :] * freqs[None, :, None]
    tabs = np.zeros((P, 2, TA), np.float32)
    tabs[:, 0, T:] = 1
    for half in range(2):
        for part in range(2):
            r = slice(half * 64 + part * 32, half * 64 + part * 32 + 32)
            tabs[r, 0, :T] = np.cos(ang[half])
            tabs[r, 1, :T] = np.sin(ang[half]) * (1 if part else -1)
    tabq = (tabs * np.float32(DK ** -0.5)).astype(np.float32)
    lev = np.zeros((2, 2, 8, P, 64), np.float32)
    hmask = np.zeros((P, LEVELS, P), np.float32)
    for l in range(LEVELS):
        m = 1 << l
        first = i[(i // m) % 2 == 0]
        second = first + m
        r = (first // (2 * m)) * 2 * m + m
        j = i[:, None]
        lev[0, 0, l] = (j > first) & (j < r)
        lev[0, 1, l] = (j >= r) & (j <= second)
        lev[1, 0, l] = (j >= r) & (j < second)
        lev[1, 1, l] = (j >= first) & (j < r)
        same = (i[:, None] // (2 * m)) == (i[None] // (2 * m))
        hmask[:, l] = same & ((i[:, None] // m) != (i[None] // m))
    for half in range(2):
        tok = np.arange(64) + 64 * half
        lev[0, half, 7] = i[:, None] <= tok
        lev[1, half, 7] = i[:, None] >= tok
    lev = (lev / GATE_NORM).transpose(3, 0, 1, 2, 4).reshape(P, 2, 1024).astype(np.float32)
    inv = np.zeros((P, 4, T), np.float32)
    for n, wdw in enumerate(WINDOWS):
        lo, hi = np.clip(t - wdw // 2, 0, T - 1), np.clip(t + (wdw - 1 - wdw // 2), 0, T - 1)
        inv[:, n] = 1.0 / (hi - lo + 1)
    wup = np.zeros((64, 512), np.float32)
    wup[0:16], wup[16] = f["w_gate_up_f"][0], f["b_gate_f"][0]
    wup[32:48], wup[48] = f["w_gate_up_b"][0], f["b_gate_b"][0]
    sgw = f["sg_w_2"][0].transpose(2, 0, 1)
    sgb = np.repeat(f["sg_b_2"][0].reshape(2, 2, 1, P), 64, axis=2).reshape(2, P, P).transpose(1, 0, 2)

    rpb = f["na_rpb_2"][0]
    bias = np.full((2, 4, AH, P, 4 * P), -1e30, np.float32)
    qr, qc = np.arange(8), np.arange(16)
    kr = np.arange(ROWS)
    for br in range(2):
        for bc in range(4):
            qrow, qcol, kcol = br * 8 + qr, bc * 16 + qc, KSPAN[bc] + np.arange(32)
            sr, sc = np.clip(qrow - 4, 0, ROWS - 8), np.clip(qcol - 8, 0, GRID_W - 16)
            inr = (kr[None] >= sr[:, None]) & (kr[None] < sr[:, None] + 8)
            inc = (kcol[None] >= sc[:, None]) & (kcol[None] < sc[:, None] + 16)
            ri = np.clip(kr[None] - qrow[:, None] + 7, 0, 14)
            ci = np.clip(kcol[None] - qcol[:, None] + 15, 0, 30)
            m = inr[:, None, :, None] & inc[None, :, None, :]
            b = rpb[:, ri[:, None, :, None], ci[None, :, None, :]]
            bias[br, bc] = np.where(m, b, np.float32(-1e30)).reshape(AH, P, 4 * P)
    arrays = {
        "modw": np.concatenate([rows(f["w_mod"][0]), rows(f["ada_w_2"][0])]),
        "crow": np.broadcast_to(crow, (P, 4, D)), "cols": cols, "mats": mats, "tabs": tabs, "tabq": tabq,
        "lev": lev, "hmask": hmask, "inv": inv, "sgb": sgb, "xT": feature_major(f["x"]),
        "ctxT": feature_major(f["ctx"]), "ctx2T": feature_major(f["ctx_2"]), "wall": wall, "wup": wup,
        "sgw": sgw, "bias": bias,
    }
    return {k: np.ascontiguousarray(v, dtype=np.float32) for k, v in arrays.items()}


def kernel(**inputs):
    import numpy as np
    import concourse.bacc as bacc
    from concourse.bass_utils import run_bass_kernel_spmd

    nc = bacc.Bacc("TRN2", target_bir_lowering=False, num_devices=1)
    arrays = arrays_of(inputs)
    args = [nc.dram_tensor(f"in_{n}", a.shape, F32, kind="ExternalInput").ap() for n, a in arrays.items()]
    args.append(nc.dram_tensor("out_T", (P, KT, T), F32, kind="ExternalOutput").ap())
    build(nc, *args)
    r = run_bass_kernel_spmd(nc, [{f"in_{n}": a for n, a in arrays.items()}], core_ids=[0])
    y = r.results[0]["out_T"]
    return np.ascontiguousarray(y.transpose(2, 1, 0)).reshape(1, T, D)
```
